# Optimizing a Trainium2 kernel written in Bass

```python
import jax
import jax.numpy as jnp
from jax import lax
import numpy as np

D_MODEL = 2048
BATCH = 1
SEQ = 256
DEPTH = 2
DEC_BATCH = 8
DEC_SEQ = 4
PAST_LEN = 2048
PAGE_SIZE = 128

PLE_DIM = 256
CONV_W = 4
CHUNK = 64
EPS = 1e-6

GDN_HEAD = 128
GDN_QK_HEADS = D_MODEL // GDN_HEAD
GDN_V_HEADS = 2 * GDN_QK_HEADS
GDN_REP = GDN_V_HEADS // GDN_QK_HEADS
GDN_QK_W = GDN_QK_HEADS * GDN_HEAD
GDN_V_W = GDN_V_HEADS * GDN_HEAD
GDN_CONV_DIM = 2 * GDN_QK_W + GDN_V_W
GDN_IN = GDN_CONV_DIM + GDN_V_W + 2 * GDN_V_HEADS

SSD_D_INNER = 2 * D_MODEL
SSD_HEAD = 64
SSD_HEADS = SSD_D_INNER // SSD_HEAD
SSD_STATE = 128
SSD_GROUPS = 8
SSD_HPG = SSD_HEADS // SSD_GROUPS
SSD_GN = SSD_GROUPS * SSD_STATE
SSD_CONV_DIM = SSD_D_INNER + 2 * SSD_GN
SSD_IN = SSD_D_INNER + SSD_CONV_DIM + SSD_HEADS
SSD_NORM_GROUP = SSD_D_INNER // SSD_GROUPS

N_GDN_LAYERS = (DEPTH + 1) // 2
N_SSD_LAYERS = DEPTH // 2

kernel_name = "gdn_mamba2_hybrid_decode_step"

def rmsnorm(x, w):
    xf = x.astype(jnp.float32)
    y = xf * lax.rsqrt(jnp.mean(xf * xf, axis=-1, keepdims=True) + EPS)
    return y * w.astype(jnp.float32)

def l2norm(x):
    return x * lax.rsqrt(jnp.sum(x * x, axis=-1, keepdims=True) + EPS)

def causal_conv(u, buf, w):
    L = u.shape[1]
    full = jnp.concatenate([buf.astype(u.dtype), u], axis=1)
    y = full[:, 0:L] * w[0]
    for j in range(1, CONV_W):
        y = y + full[:, j:j + L] * w[j]
    return y, full[:, L:]

def chunk_decay(acs):
    idx = jnp.arange(acs.shape[-1])
    incl = idx[:, None] >= idx[None, :]
    diff = acs[..., :, None] - acs[..., None, :]
    return jnp.exp(jnp.where(incl, diff, -jnp.inf))

def gdn_chunked(q, k, v, beta, g, S0):
    Bsz, L, H, _ = q.shape
    NC = L // CHUNK

    def chunks(t):
        return t.reshape((Bsz, NC, CHUNK, H) + t.shape[3:]).swapaxes(2, 3)

    q, k, v, beta, g = (chunks(t) for t in (q, k, v, beta, g))
    g = jnp.cumsum(g, axis=-1)
    decay = chunk_decay(g)
    eye = jnp.eye(CHUNK, dtype=jnp.float32)
    strict = jnp.tril(jnp.ones((CHUNK, CHUNK), jnp.float32), -1)
    k_beta = k * beta[..., None]
    a_mat = jnp.einsum("bnhid,bnhjd->bnhij", k_beta, k) * decay * strict
    t_mat = lax.linalg.triangular_solve(eye + a_mat, jnp.broadcast_to(eye, a_mat.shape),
                                        left_side=True, lower=True, unit_diagonal=True)
    u = jnp.einsum("bnhij,bnhje->bnhie", t_mat, v * beta[..., None])
    w = jnp.einsum("bnhij,bnhjd->bnhid", t_mat, k_beta * jnp.exp(g)[..., None])
    qk = jnp.einsum("bnhid,bnhjd->bnhij", q, k) * decay
    g_last = g[..., -1]
    k_dec = k * jnp.exp(g_last[..., None] - g)[..., None]
    q_dec = q * jnp.exp(g)[..., None]

    def step(S, inp):
        u_c, w_c, qk_c, qd_c, kd_c, gl_c = inp
        v_new = u_c - jnp.einsum("bhcd,bhde->bhce", w_c, S)
        o = jnp.einsum("bhcd,bhde->bhce", qd_c, S) + jnp.einsum("bhij,bhje->bhie", qk_c, v_new)
        S = S * jnp.exp(gl_c)[..., None, None] + jnp.einsum("bhcd,bhce->bhde", kd_c, v_new)
        return S, o

    scan_in = tuple(t.swapaxes(0, 1) for t in (u, w, qk, q_dec, k_dec, g_last))
    S, o = lax.scan(step, S0, scan_in)
    o = o.transpose(1, 0, 3, 2, 4).reshape(Bsz, L, H, -1)
    return o, S

def gdn_recurrent(q, k, v, beta, g, S0):
    def step(S, inp):
        q_t, k_t, v_t, b_t, g_t = inp
        S = S * jnp.exp(g_t)[..., None, None]
        kv = jnp.einsum("bhd,bhde->bhe", k_t, S)
        S = S + jnp.einsum("bhd,bhe->bhde", k_t, (v_t - kv) * b_t[..., None])
        return S, jnp.einsum("bhd,bhde->bhe", q_t, S)

    scan_in = tuple(t.swapaxes(0, 1) for t in (q, k, v, beta, g))
    S, o = lax.scan(step, S0, scan_in)
    return o.swapaxes(0, 1), S

def gdn_mixer(hn, conv_buf, S0, w_in, conv_w, A_log, dt_bias, norm_w, w_out, chunked):
    f32 = jnp.float32
    Bsz, L, _ = hn.shape
    proj = hn @ w_in
    o1 = GDN_CONV_DIM
    o2 = o1 + GDN_V_W
    o3 = o2 + GDN_V_HEADS
    qkv, z, a, b = proj[..., :o1], proj[..., o1:o2], proj[..., o2:o3], proj[..., o3:]
    qkv, new_buf = causal_conv(qkv, conv_buf, conv_w)
    qkv = jax.nn.silu(qkv).astype(f32)
    q = qkv[..., :GDN_QK_W].reshape(Bsz, L, GDN_QK_HEADS, GDN_HEAD)
    k = qkv[..., GDN_QK_W:2 * GDN_QK_W].reshape(Bsz, L, GDN_QK_HEADS, GDN_HEAD)
    v = qkv[..., 2 * GDN_QK_W:].reshape(Bsz, L, GDN_V_HEADS, GDN_HEAD)
    q = jnp.repeat(l2norm(q) * (GDN_HEAD ** -0.5), GDN_REP, axis=2)
    k = jnp.repeat(l2norm(k), GDN_REP, axis=2)
    beta = jax.nn.sigmoid(b.astype(f32))
    g = -jnp.exp(A_log.astype(f32)) * jax.nn.softplus(a.astype(f32) + dt_bias.astype(f32))
    mix = gdn_chunked if chunked else gdn_recurrent
    o, S = mix(q, k, v, beta, g, S0.astype(f32))
    zf = z.astype(f32).reshape(Bsz, L, GDN_V_HEADS, GDN_HEAD)
    o = rmsnorm(o, norm_w) * jax.nn.silu(zf)
    out = o.reshape(Bsz, L, GDN_V_W).astype(hn.dtype) @ w_out
    return out, new_buf, S

def ssd_chunked(xs, dt, A, Bm, Cm, S0):
    Bsz, L = xs.shape[:2]
    NC = L // CHUNK
    Xc = (xs * dt[..., None]).reshape(Bsz, NC, CHUNK, SSD_GROUPS, SSD_HPG, SSD_HEAD)
    Bc = Bm.reshape(Bsz, NC, CHUNK, SSD_GROUPS, SSD_STATE)
    Cc = Cm.reshape(Bsz, NC, CHUNK, SSD_GROUPS, SSD_STATE)
    acs = jnp.cumsum((dt * A).reshape(Bsz, NC, CHUNK, SSD_GROUPS, SSD_HPG).transpose(0, 3, 4, 1, 2), axis=-1)
    decay = chunk_decay(acs)
    cb = jnp.einsum("bclgn,bcsgn->bgcls", Cc, Bc)
    y_diag = jnp.einsum("bgcls,bgrcls,bcsgrp->bclgrp", cb, decay, Xc)

    def step(S, inp):
        c_c, b_c, x_c, a_c = inp
        y_off = jnp.einsum("blgn,bgrpn,bgrl->blgrp", c_c, S, jnp.exp(a_c))
        a_last = a_c[..., -1]
        S = S * jnp.exp(a_last)[..., None, None] + jnp.einsum(
            "blgn,bgrl,blgrp->bgrpn", b_c, jnp.exp(a_last[..., None] - a_c), x_c)
        return S, y_off

    scan_in = (Cc.swapaxes(0, 1), Bc.swapaxes(0, 1), Xc.swapaxes(0, 1), acs.transpose(3, 0, 1, 2, 4))
    S, y_off = lax.scan(step, S0, scan_in)
    y = (y_diag + y_off.swapaxes(0, 1)).reshape(Bsz, L, SSD_GROUPS, SSD_HPG, SSD_HEAD)
    return y, S

def ssd_recurrent(xs, dt, A, Bm, Cm, S0):
    def step(S, inp):
        x_t, dt_t, b_t, c_t = inp
        S = S * jnp.exp(dt_t * A)[..., None, None] + jnp.einsum("bgrp,bgn->bgrpn", x_t * dt_t[..., None], b_t)
        return S, jnp.einsum("bgrpn,bgn->bgrp", S, c_t)

    scan_in = tuple(t.swapaxes(0, 1) for t in (xs, dt, Bm, Cm))
    S, y = lax.scan(step, S0, scan_in)
    return y.swapaxes(0, 1), S

def ssd_mixer(hn, conv_buf, S0, w_in, conv_w, conv_b, A_log, dt_bias, D_skip, norm_w, w_out, chunked):
    f32 = jnp.float32
    Bsz, L, _ = hn.shape
    proj = hn @ w_in
    o1 = SSD_D_INNER
    o2 = o1 + SSD_CONV_DIM
    z, xbc, dt_raw = proj[..., :o1], proj[..., o1:o2], proj[..., o2:]
    xbc, new_buf = causal_conv(xbc, conv_buf, conv_w)
    xbc = jax.nn.silu(xbc + conv_b).astype(f32)
    xs = xbc[..., :SSD_D_INNER].reshape(Bsz, L, SSD_GROUPS, SSD_HPG, SSD_HEAD)
    Bm = xbc[..., SSD_D_INNER:SSD_D_INNER + SSD_GN].reshape(Bsz, L, SSD_GROUPS, SSD_STATE)
    Cm = xbc[..., SSD_D_INNER + SSD_GN:].reshape(Bsz, L, SSD_GROUPS, SSD_STATE)
    dt = jax.nn.softplus(dt_raw.astype(f32) + dt_bias.astype(f32)).reshape(Bsz, L, SSD_GROUPS, SSD_HPG)
    A = -jnp.exp(A_log.astype(f32)).reshape(SSD_GROUPS, SSD_HPG)
    S0 = S0.astype(f32).reshape(Bsz, SSD_GROUPS, SSD_HPG, SSD_HEAD, SSD_STATE)
    mix = ssd_chunked if chunked else ssd_recurrent
    y, S = mix(xs, dt, A, Bm, Cm, S0)
    y = y + D_skip.astype(f32).reshape(SSD_GROUPS, SSD_HPG)[..., None] * xs
    y = y.reshape(Bsz, L, SSD_D_INNER) * jax.nn.silu(z.astype(f32))
    yg = y.reshape(Bsz, L, SSD_GROUPS, SSD_NORM_GROUP)
    yg = yg * lax.rsqrt(jnp.mean(yg * yg, axis=-1, keepdims=True) + EPS)
    y = yg.reshape(Bsz, L, SSD_D_INNER) * norm_w.astype(f32)
    out = y.astype(hn.dtype) @ w_out
    return out, new_buf, S.reshape(Bsz, SSD_HEADS, SSD_HEAD, SSD_STATE)

def ple_add(h, p_i, w_proj, w_gate, norm_w):
    e = rmsnorm(p_i @ w_proj, norm_w)
    gate = jax.nn.sigmoid((h @ w_gate).astype(jnp.float32))
    return h + (e * gate).astype(h.dtype)

def trunk(x, p, gdn_conv0, gdn_S0, ssd_conv0, ssd_S0, weights, chunked):
    (norm_w, gdn_w_in, gdn_conv_w, gdn_A_log, gdn_dt_bias, gdn_norm_w, gdn_w_out,
     ssd_w_in, ssd_conv_w, ssd_conv_b, ssd_A_log, ssd_dt_bias, ssd_D, ssd_norm_w, ssd_w_out,
     ple_w_proj, ple_w_gate, ple_norm_w, final_norm_w) = weights
    h = x
    gdn_states, gdn_convs, ssd_states, ssd_convs = [], [], [], []
    for i in range(DEPTH):
        j = i // 2
        hn = rmsnorm(h, norm_w[i]).astype(h.dtype)
        if i % 2 == 0:
            mix, buf, S = gdn_mixer(hn, gdn_conv0[j], gdn_S0[j], gdn_w_in[j], gdn_conv_w[j], gdn_A_log[j],
                                    gdn_dt_bias[j], gdn_norm_w[j], gdn_w_out[j], chunked)
            gdn_states.append(S)
            gdn_convs.append(buf)
        else:
            mix, buf, S = ssd_mixer(hn, ssd_conv0[j], ssd_S0[j], ssd_w_in[j], ssd_conv_w[j], ssd_conv_b[j],
                                    ssd_A_log[j], ssd_dt_bias[j], ssd_D[j], ssd_norm_w[j], ssd_w_out[j], chunked)
            ssd_states.append(S)
            ssd_convs.append(buf)
        h = h + mix
        h = ple_add(h, p[i], ple_w_proj[i], ple_w_gate[i], ple_norm_w[i])
    y = rmsnorm(h, final_norm_w).astype(x.dtype)
    return y, jnp.stack(gdn_states), jnp.stack(gdn_convs), jnp.stack(ssd_states), jnp.stack(ssd_convs)

def setup_inputs(seed: int = 0) -> dict:
    key = jax.random.key(seed)
    ks = jax.random.split(key, 32)
    f32 = jnp.float32
    NG, NS = N_GDN_LAYERS, N_SSD_LAYERS

    def nrm(k, shape, scale):
        return jax.random.normal(k, shape, f32) * scale

    def dt_bias_init(k, shape):
        dt = jnp.exp(jax.random.uniform(k, shape, f32, np.log(1e-3), np.log(1e-1)))
        return dt + jnp.log(-jnp.expm1(-dt))

    return {
        "x_prompt": nrm(ks[0], (BATCH, SEQ, D_MODEL), 1.0),
        "x_sample": nrm(ks[1], (DEC_BATCH, DEC_SEQ, D_MODEL), 1.0),
        "state_gdn": nrm(ks[2], (NG, DEC_BATCH, GDN_V_HEADS, GDN_HEAD, GDN_HEAD), 0.1),
        "cache_gdn_conv": nrm(ks[3], (NG, DEC_BATCH, CONV_W - 1, GDN_CONV_DIM), 1.0),
        "state_ssd": nrm(ks[4], (NS, DEC_BATCH, SSD_HEADS, SSD_HEAD, SSD_STATE), 0.1),
        "cache_ssd_conv": nrm(ks[5], (NS, DEC_BATCH, CONV_W - 1, SSD_CONV_DIM), 1.0),
        "p_prompt": nrm(ks[6], (DEPTH, BATCH, SEQ, PLE_DIM), 1.0),
        "p_sample": nrm(ks[7], (DEPTH, DEC_BATCH, DEC_SEQ, PLE_DIM), 1.0),
        "norm_w": 1.0 + nrm(ks[8], (DEPTH, D_MODEL), 0.02),
        "gdn_w_in": nrm(ks[9], (NG, D_MODEL, GDN_IN), D_MODEL ** -0.5),
        "gdn_conv_w": nrm(ks[10], (NG, CONV_W, GDN_CONV_DIM), CONV_W ** -0.5),
        "gdn_A_log": jnp.log(jax.random.uniform(ks[11], (NG, GDN_V_HEADS), f32, 1.0, 16.0)),
        "gdn_dt_bias": dt_bias_init(ks[12], (NG, GDN_V_HEADS)),
        "gdn_norm_w": 1.0 + nrm(ks[13], (NG, GDN_HEAD), 0.02),
        "gdn_w_out": nrm(ks[14], (NG, GDN_V_W, D_MODEL), GDN_V_W ** -0.5),
        "ssd_w_in": nrm(ks[15], (NS, D_MODEL, SSD_IN), D_MODEL ** -0.5),
        "ssd_conv_w": nrm(ks[16], (NS, CONV_W, SSD_CONV_DIM), CONV_W ** -0.5),
        "ssd_conv_b": nrm(ks[17], (NS, SSD_CONV_DIM), 0.02),
        "ssd_A_log": jnp.log(jax.random.uniform(ks[18], (NS, SSD_HEADS), f32, 1.0, 16.0)),
        "ssd_dt_bias": dt_bias_init(ks[19], (NS, SSD_HEADS)),
        "ssd_D": 1.0 + nrm(ks[20], (NS, SSD_HEADS), 0.02),
        "ssd_norm_w": 1.0 + nrm(ks[21], (NS, SSD_D_INNER), 0.02),
        "ssd_w_out": nrm(ks[22], (NS, SSD_D_INNER, D_MODEL), SSD_D_INNER ** -0.5),
        "ple_w_proj": nrm(ks[23], (DEPTH, PLE_DIM, D_MODEL), PLE_DIM ** -0.5),
        "ple_w_gate": nrm(ks[24], (DEPTH, D_MODEL, D_MODEL), D_MODEL ** -0.5),
        "ple_norm_w": 1.0 + nrm(ks[25], (DEPTH, D_MODEL), 0.02),
        "final_norm_w": 1.0 + nrm(ks[26], (D_MODEL,), 0.02),
    }

def reference(x_prompt, x_sample, state_gdn, cache_gdn_conv, state_ssd, cache_ssd_conv, p_prompt, p_sample,
              norm_w, gdn_w_in, gdn_conv_w, gdn_A_log, gdn_dt_bias, gdn_norm_w, gdn_w_out,
              ssd_w_in, ssd_conv_w, ssd_conv_b, ssd_A_log, ssd_dt_bias, ssd_D, ssd_norm_w, ssd_w_out,
              ple_w_proj, ple_w_gate, ple_norm_w, final_norm_w):
    weights = (norm_w, gdn_w_in, gdn_conv_w, gdn_A_log, gdn_dt_bias, gdn_norm_w, gdn_w_out,
               ssd_w_in, ssd_conv_w, ssd_conv_b, ssd_A_log, ssd_dt_bias, ssd_D, ssd_norm_w, ssd_w_out,
               ple_w_proj, ple_w_gate, ple_norm_w, final_norm_w)
    bp = x_prompt.shape[0]
    gdn_S0 = jnp.zeros((N_GDN_LAYERS, bp, GDN_V_HEADS, GDN_HEAD, GDN_HEAD), jnp.float32)
    gdn_c0 = jnp.zeros((N_GDN_LAYERS, bp, CONV_W - 1, GDN_CONV_DIM), x_prompt.dtype)
    ssd_S0 = jnp.zeros((N_SSD_LAYERS, bp, SSD_HEADS, SSD_HEAD, SSD_STATE), jnp.float32)
    ssd_c0 = jnp.zeros((N_SSD_LAYERS, bp, CONV_W - 1, SSD_CONV_DIM), x_prompt.dtype)
    y_prompt, sg_p, cg_p, ss_p, cs_p = trunk(x_prompt, p_prompt, gdn_c0, gdn_S0, ssd_c0, ssd_S0, weights, True)
    y_sample, sg_s, cg_s, ss_s, cs_s = trunk(x_sample, p_sample, cache_gdn_conv, state_gdn,
                                             cache_ssd_conv, state_ssd, weights, False)
    return (y_prompt, y_sample,
            sg_p.astype(state_gdn.dtype), cg_p.astype(cache_gdn_conv.dtype),
            ss_p.astype(state_ssd.dtype), cs_p.astype(cache_ssd_conv.dtype),
            sg_s.astype(state_gdn.dtype), cg_s.astype(cache_gdn_conv.dtype),
            ss_s.astype(state_ssd.dtype), cs_s.astype(cache_ssd_conv.dtype))


_drawn_inputs = setup_inputs


def setup_inputs(seed=0):
    import zlib

    import numpy as np

    out = dict(_drawn_inputs(seed))
    spreads = {}
    factors = {'gdn_norm_w': 3.212,
     'ssd_D': 7.215,
     'ssd_norm_w': 4.688,
     'ple_norm_w': 3.837,
     'final_norm_w': 2.897}
    for name, (base, spread) in spreads.items():
        noise = np.random.default_rng([zlib.crc32(name.encode()), seed]).standard_normal(out[name].shape)
        drawn = base * np.exp(spread * noise) if base else spread * noise
        out[name] = jnp.asarray(drawn.astype(out[name].dtype))
    for name, factor in factors.items():
        out[name] = (out[name] * factor).astype(out[name].dtype)
    return out
```

```python
from contextlib import ExitStack

import concourse.bass as bass
from concourse import mybir

F32 = mybir.dt.float32
F32R = mybir.dt.float32r
ALU = mybir.AluOpType
ACT = mybir.ActivationFunctionType

P = 128
D_MODEL = 2048
KT = D_MODEL // P
SEQ = 256
DEC_B, DEC_T = 8, 4
NS = DEC_B * DEC_T
T = SEQ + NS
CH = 128
NC = SEQ // CH
CONV_W = 4
PRE = CONV_W - 1
EPS = 1e-6
DEPTH = 2
PLE_K = 256 // P

GH = 16
GV = 2 * GH
SG, SH = 8, 64
HPG = SH // SG
SX = HPG // 2
HD = 64

UP, UC, US = PRE, PRE + SEQ, PRE + SEQ + PRE * DEC_B
UW = US + NS
CW = PRE + PRE * DEC_B
PC_G = 4 * (PRE * DEC_B + CONV_W)
PC_S = 6 * (PRE * DEC_B + CONV_W + 1) + 2 * SX

OFF = [0, 32, 56, 72]
LEN = [32, 24, 16, 8]
NPAIR = 80

T_GPRO = 0
T_GLOOP = T_GPRO + 6
T_GEND = T_GLOOP + 6 * (GH - 1)
T_O1 = T_GEND + 2
T_P1 = T_O1 + 32
T_E1 = T_P1 + 2
T_SPRO = T_E1 + 16
T_SLOOP = T_SPRO + 7
T_SEND = T_SLOOP + 10 * (SG - 1)
T_O2 = T_SEND + 4
T_P2 = T_O2 + 32
T_E2 = T_P2 + 2
N_TILES = T_E2 + 16
N_HALF = 2 * N_TILES
N_ROUND, N_REST = N_HALF // 4, N_HALF % 4

C_NORM, C_PLE, C_FINAL, C_GNORM = 0, 32, 64, 80
C_GDT, C_GA, C_SDT, C_SA = 81, 82, 83, 84
N_PRM = 85
G_DVE_LINKS, S_DVE_LINKS = 28, 27
ARENA = 15900
K_ID, K_ONE, K_INC, K_M1, K_LEV = 0, 1, 2, 3, 4
K_BM = 10
N_CST = 11


def bc(ap, axis, n):
    a = ap.unsqueeze(axis)
    shape = list(a.shape)
    shape[axis] = n
    return a.to_broadcast(shape)


class Order:

    def __init__(self, eng, sem):
        self.eng, self.sem, self.base, self.n, self.m, self.per = eng, sem, 0, 0, 0, 0

    def enter(self, m, per):
        assert self.n == 0 or self.per == 0
        self.base, self.n, self.m, self.per = self.base + self.n, 0, m, per

    def leave(self, times):
        assert self.n == self.per, (self.n, self.per)
        self.base, self.n, self.m, self.per = self.base + self.per * times, 0, 0, 0

    def link(self, ins):
        self.n += 1
        ins.then_inc(self.sem, 1)
        self.eng.wait_ge(self.sem, self.m * self.per + (self.base + self.n))


def build(nc, weights, x_in, p_in, prm_in, cst_in, gpack, spack, gstate, sstate,
          y_out, gconv_out, sconv_out, gst_p, gst_s, sst_p, sst_s,
          g_rows, s_rows, h_spill, G_DVE, G_ACT, S_DVE, S_ACT):
    with ExitStack() as ctx:
        def sb(name, shape, dt=F32):
            return ctx.enter_context(nc.sbuf_tensor(name, shape, dt))

        def sem(name):
            return ctx.enter_context(nc.semaphore(name))

        ring = sb("ring", [P, 4, 8, P])
        wh = sb("wh", [P, 4, 8, P], F32R)
        wl = sb("wl", [P, 4, 8, P], F32R)
        xh = sb("xh", [P, KT, T], F32R)
        xl = sb("xl", [P, KT, T], F32R)
        Y = sb("Y", [P, 2 * KT, T])
        h = sb("h", [P, KT, T])
        cst = sb("cst", [P, N_CST, P])
        prm = sb("prm", [P, N_PRM])
        small = sb("small", [P, 16])
        ccol = sb("ccol", [P, 6 * SH])
        arena = sb("arena", [P, ARENA])

        psj = [ctx.enter_context(nc.psum_tensor(f"psj{i}", [P, 512], F32)) for i in range(2)]
        psA, psB, psC, psD, psE, psF = (
            ctx.enter_context(nc.psum_tensor(f"ps{c}", [P, 512], F32)) for c in "ABCDEF")

        def carve(sizes):
            out, at = {}, 0
            for name, n in sizes:
                out[name] = arena[:, at:at + n]
                at += n
            assert at <= ARENA, at
            return out

        ident, ones = cst[:, K_ID, :], cst[:, K_ONE, :]
        bmask = cst[0:NS, K_BM, 0:DEC_B]
        eps_c = small[:, 0:1]

        ga = carve([("U", 4 * UW), ("CV", 4 * T), ("R", 2 * 3 * T), ("SQ", 2 * T), ("RS", 2 * T),
                    ("pc", PC_G), ("co", 4 * CW), ("cc", 16), ("PR", 2 * NPAIR), ("DEC", 2 * NPAIR),
                    ("CQ", 2 * NPAIR), ("CK", 2 * NPAIR), ("W", 64), ("WD", 64), ("TM", 64), ("BE", 64),
                    ("DT", 512), ("AT", 512), ("E", 512), ("D", 512), ("PP", 512), ("QK", 512), ("VB", 512),
                    ("VN", 512), ("VND", 512), ("KTK", 256), ("S1", 256), ("S2", 256), ("QD", 256),
                    ("O", 2 * T), ("ZS", 2 * T), ("WT", 256)])
        gU = ga["U"].rearrange("p (i u) -> p i u", i=4)
        gCV = ga["CV"].rearrange("p (i t) -> p i t", i=4)
        gR = ga["R"].rearrange("p (j k t) -> p j k t", j=2, k=3)
        gSQ = ga["SQ"].rearrange("p (i t) -> p i t", i=2)
        gRS = ga["RS"].rearrange("p (i t) -> p i t", i=2)
        gpc_cache = ga["pc"][:, 0:4 * 24].rearrange("p (i c) -> p i c", i=4)
        gpc_tap = ga["pc"][:, 96:112].rearrange("p (i c) -> p i c", i=4)
        gco = ga["co"].rearrange("p (i c) -> p i c", i=4)
        gcc = ga["cc"].rearrange("p (k c j) -> p k c j", k=4, c=NC)
        gPR, gDEC, gCQ, gCK = (ga[n].rearrange("p (i c) -> p i c", i=2) for n in ("PR", "DEC", "CQ", "CK"))
        gW, gWD, gTM, gBE = (ga[n].rearrange("p (i c) -> p i c", i=2) for n in ("W", "WD", "TM", "BE"))
        gDT, gAT, gE, gD, gP, gQK, gVB, gVN, gVND = (
            ga[n].rearrange("p (u t) -> p u t", u=4) for n in ("DT", "AT", "E", "D", "PP", "QK", "VB", "VN", "VND"))
        gKT = ga["KTK"].rearrange("p (c t) -> p c t", c=NC)
        gS1 = ga["S1"].rearrange("p (j t) -> p j t", j=2)
        gS2 = ga["S2"].rearrange("p (j t) -> p j t", j=2)
        gQD = ga["QD"].rearrange("p (j t) -> p j t", j=2)
        gO = ga["O"].rearrange("p (j t) -> p j t", j=2)
        gZS = ga["ZS"].rearrange("p (j t) -> p j t", j=2)
        gWT = ga["WT"]
        hf = h[:, :, :].rearrange("p k t -> p (k t)")
        gS = hf[:, 0:2048].rearrange("p (b j e) -> p b j e", b=DEC_B, j=2)
        gKM = hf[0:NS, 2048:3072].rearrange("p (b d) -> p b d", b=DEC_B)
        HRG = arena[:, ARENA - 9 * T:ARENA].rearrange("p (k t) -> p k t", k=9)

        sa = carve([("U", 6 * UW), ("CV", 6 * T), ("R2", HPG * T), ("RP", SX * 224), ("pc", PC_S),
                    ("co", 6 * CW), ("cc", 6 * HPG), ("PR", NPAIR), ("DEC", SX * NPAIR), ("DT", 1024),
                    ("X", 1024), ("XD", 512), ("CB", 256), ("BT", 256), ("XS", 128), ("XE", 128), ("TM", 128),
                    ("XT", 512), ("YT", SX * T), ("ZS", SX * T), ("EG", 80), ("BM", 1024), ("RT", T)])
        sU = sa["U"].rearrange("p (i u) -> p i u", i=6)
        sCV = sa["CV"].rearrange("p (i t) -> p i t", i=6)
        sR2 = sa["R2"].rearrange("p (h t) -> p h t", h=HPG)
        sRP = sa["RP"].rearrange("p (i c) -> p i c", i=SX)
        spc = sa["pc"][:, 0:6 * 29].rearrange("p (i c) -> p i c", i=6)
        spc_norm, spc_D = sa["pc"][:, 174:178], sa["pc"][:, 178:182]
        sco = sa["co"].rearrange("p (i c) -> p i c", i=6)
        scc = sa["cc"].rearrange("p (k c j) -> p k c j", k=3, c=NC)
        sPR = sa["PR"]
        sDEC = sa["DEC"].rearrange("p (i c) -> p i c", i=SX)
        sDT = sa["DT"].rearrange("p (h t) -> p h t", h=HPG)
        sX = sa["X"].rearrange("p (c h d) -> p c h d", c=NC, h=HPG)
        sXD = sa["XD"].rearrange("p (h d) -> p h d", h=HPG)
        sCB = sa["CB"].rearrange("p (c t) -> p c t", c=NC)
        sBT = sa["BT"].rearrange("p (c t) -> p c t", c=NC)
        sXS, sXE, sTM = (sa[n].rearrange("p (i t) -> p i t", i=SX) for n in ("XS", "XE", "TM"))
        sXT = sa["XT"]
        sYT = sa["YT"].rearrange("p (i t) -> p i t", i=SX)
        sZS = sa["ZS"].rearrange("p (i t) -> p i t", i=SX)
        sEGc = sa["EG"][:, 0:8]
        sEGb = sa["EG"][:, 8:72].rearrange("p (h b) -> p h b", h=HPG)
        sS = hf[:, 0:4096].rearrange("p (b h d) -> p b h d", b=DEC_B, h=HPG)
        sS1 = hf[:, 4096:4608]
        sBMv = sa["BM"][0:NS, :].rearrange("p (b n) -> p b n", b=DEC_B)
        sTMr = sa["RT"]

        da = carve([("SQ", 2 * T), ("SGM", 2 * T), ("TM", 2 * T), ("RSTD", T), ("RSE", T), ("pT", 2 * T)])
        dSQ, dSG, dTM = (da[n].rearrange("p (i t) -> p i t", i=2) for n in ("SQ", "SGM", "TM"))
        dRS, dRE = da["RSTD"], da["RSE"]
        dp = da["pT"].rearrange("p (k t) -> p k t", k=PLE_K)
        eb = Y[:, 0:KT, :]

        w_in = [sem(f"w_in{i}") for i in range(4)]
        wh_ready = sem("wh_ready")
        wl_ready = sem("wl_ready")
        half_done = sem("half_done")
        took_act = sem("took_act")
        took_dve = sem("took_dve")
        xh_ready = sem("xh_ready")
        xl_ready = sem("xl_ready")
        dve_order, act_order = sem("dve_order"), sem("act_order")
        c_in = sem("c_in")
        sems = {}

        def S(name):
            if name not in sems:
                sems[name] = sem(name)
            return sems[name]

        X0 = {"g": 0, "oa1": 16, "ob1": 32, "p1": 48, "e1": 50, "s": 66, "oa2": 82, "ob2": 98, "p2": 114, "e2": 116}
        TA_G = 0
        TA_E1 = T_GEND + 2
        TA_S = TA_E1 + 16
        TA_E2 = TA_S + (T_SEND + 4 - T_SPRO)
        TD_O1, TD_P1, TD_O2, TD_P2 = 0, 32, 48, 80

        block = ctx.enter_context(nc.Block())

        @block.sync
        def _(sp):
            sp.dma_start(h[:, :, :], x_in).then_inc(S("x_in"), 16)
            sp.dma_start(cst[:, :, :], cst_in).then_inc(c_in, 16)
            sp.dma_start(prm[:, :], prm_in).then_inc(S("prm_in"), 16)
            for s in range(4):
                sp.dma_start(ring[:, s], weights[s]).then_inc(w_in[s], 16)

            def refill(r, s):
                sp.wait_ge(wl_ready, r * 4 + (s - 3))
                sp.dma_start(ring[:, s], weights[r * 4 + s]).then_inc(w_in[s], 16)

            with sp.Fori(1, N_ROUND) as r:
                for s in range(4):
                    refill(r, s)
            for s in range(N_REST):
                refill(N_ROUND, s)

        @block.gpsimd
        def _(pool):
            def lower(r, s):
                pool.wait_ge(wh_ready, r * 4 + (s + 1))
                pool.tensor_tensor(wl[:, s], ring[:, s], wh[:, s].bitcast(F32), ALU.subtract) \
                    .then_inc(wl_ready, 1)

            with pool.Fori(0, N_ROUND) as r:
                for s in range(4):
                    lower(r, s)
            for s in range(N_REST):
                lower(N_ROUND, s)

        @block.tensor
        def _(pe):
            def project(m, per, t0, e, fresh=None):
                hc = 2 * t0 + e // 4
                if e % 4 == 0:
                    pe.wait_ge(wl_ready, m * (2 * per) + (hc + 1))
                for kt in (2 * e, 2 * e + 1):
                    if fresh is not None:
                        pe.wait_ge(xl_ready, fresh + kt + 1)
                    w_h, w_l = wh[:, hc % 4, kt % 8, :], wl[:, hc % 4, kt % 8, :]
                    out = psj[t0 % 2][:, 0:T]
                    pe.matmul(out, w_h, xh[:, kt, :], start=(kt == 0), stop=False)
                    pe.matmul(out, w_h, xl[:, kt, :], start=False, stop=False)
                    mm = pe.matmul(out, w_l, xh[:, kt, :], start=False, stop=(kt == KT - 1))
                if e % 4 == 3:
                    mm.then_inc(half_done, 1)

            def col_sum(out, rhs, start=True, stop=True):
                return pe.matmul(out, ones, rhs, start=start, stop=stop)

            pe.wait_ge(c_in, 16)
            pe.wait_ge(S("prm_in"), 16)

            def norm_sum(n):
                for kt in range(KT):
                    pe.wait_ge(S("hsq"), n + kt + 1)
                    mm = col_sum(psA[:, 0:T], dSQ[:, kt % 2, :], start=(kt == 0), stop=(kt == KT - 1))
                    mm.then_inc(S("hss"), 1)

            def gdn_mix(m, e):
                if e == 10:
                    pe.wait_ge(S("g_sq"), m * 2 + 1)
                    pe.wait_ge(S("g_y"), m + 1)
                    col_sum(psA[:, 0:T], gSQ[:, 0, :])
                    col_sum(psB[:, 0:T], gSQ[:, 1, :]).then_inc(S("g_ss"), 1)
                if e == 12:
                    pe.wait_ge(S("g_kn"), m + 1)
                    for c in range(NC):
                        pe.transpose(psA[:, c * P:(c + 1) * P], gCV[:, 1, c * CH:(c + 1) * CH], ident)
                        for j in range(2):
                            pe.transpose(psB[:, (2 * c + j) * P:(2 * c + j + 1) * P],
                                         gCV[:, 2 + j, c * CH:(c + 1) * CH], ident)
                        pe.matmul(psC[:, c * CH:(c + 1) * CH], gCV[:, 1, c * CH:(c + 1) * CH],
                                  gCV[:, 1, c * CH:(c + 1) * CH], start=True, stop=True)
                        pe.matmul(psC[:, 256 + c * CH:256 + (c + 1) * CH], gCV[:, 1, c * CH:(c + 1) * CH],
                                  gCV[:, 0, c * CH:(c + 1) * CH], start=True, stop=True)
                    pe.transpose(psE[0:NS, 0:P], gCV[:, 1, SEQ:T], ident).then_inc(S("g_tok"), 1)
                if e == 14:
                    pe.wait_ge(S("g_pr"), m + 1)
                    col_sum(psD[:, 0:2 * NPAIR], ga["PR"])
                    pe.wait_ge(S("g_st_in"), m * 16 + 16)
                    for b in range(DEC_B):
                        for j in range(2):
                            at = 160 + 16 * b + 8 * j
                            mm = pe.matmul(psD[:, at:at + 8], gS[:, b, j, :], gCV[:, 0:2, SEQ + b:T:DEC_B],
                                           start=True, stop=True)
                    mm.then_inc(S("g_smp"), 1)
                if e == 17:
                    pe.wait_ge(S("g_e1"), m + 1)
                    pe.wait_ge(S("g_vb"), m + 1)
                    for u in range(4):
                        mm = pe.transpose(psB[:, u * P:(u + 1) * P], gE[:, u, :], ident)
                    mm.then_inc(S("g_dt"), 1)
                for lv in range(6):
                    if e == 20 + 2 * lv:
                        if lv == 0:
                            pe.wait_ge(S("g_d"), m + 1)
                            pe.wait_ge(S("g_km"), m + 1)
                        else:
                            pe.wait_ge(S("g_ed"), m * 6 + lv)
                        for u in range(4):
                            mm = pe.matmul(psC[:, u * P:(u + 1) * P], gAT[:, u, :], gD[:, u, :],
                                           start=True, stop=True)
                        mm.then_inc(S("g_p"), 1)
                    if e == 21 + 2 * lv:
                        pe.wait_ge(S("g_pm"), m * 6 + lv + 1)
                        for u in range(4):
                            mm = pe.matmul(psA[:, u * P:(u + 1) * P], gP[:, u, :], gE[:, u, :],
                                           start=True, stop=True)
                        if lv < 5:
                            for u in range(4):
                                mm = pe.matmul(psB[:, u * P:(u + 1) * P], gE[:, u, :], gP[:, u, :],
                                               start=True, stop=True)
                        mm.then_inc(S("g_q"), 1)
                if e == 33:
                    pe.wait_ge(S("g_ed"), m * 6 + 6)
                    for j in range(2):
                        mm = pe.matmul(psC[:, j * P:(j + 1) * P], gE[:, j, :], gVB[:, j, :], start=True, stop=True)
                    mm.then_inc(S("g_vn"), 1)
                if e == 35:
                    pe.wait_ge(S("g_vnd"), m * 2 + 1)
                    pe.matmul(psE[:, 0:2 * P], gKT[:, 0, :], ga["VND"][:, 0:2 * P], start=True, stop=True) \
                        .then_inc(S("g_s"), 1)
                if e == 37:
                    pe.wait_ge(S("g_s1"), m + 1)
                    pe.matmul(psD[:, 0:2 * P], gCV[:, 1, CH:2 * CH], ga["S1"], start=True, stop=True) \
                        .then_inc(S("g_ks"), 1)
                    pe.wait_ge(S("g_wd"), m + 1)
                    for j in range(2):
                        mm = pe.transpose(psB[0:NS, j * P:(j + 1) * P], gWD[:, j, :], ident)
                    mm.then_inc(S("g_wt"), 1)
                if e == 40:
                    pe.wait_ge(S("g_rhs"), m + 1)
                    for j in range(2):
                        mm = pe.matmul(psC[:, j * P:(j + 1) * P], gE[:, 2 + j, :], gVB[:, 2 + j, :],
                                       start=True, stop=True)
                    mm.then_inc(S("g_vn"), 1)
                    for j in range(2):
                        o = psF[:, j * SEQ:j * SEQ + CH]
                        pe.matmul(o, gVN[:, j, :], gQK[:, j, :], start=True, stop=True)
                if e == 42:
                    pe.wait_ge(S("g_vnd"), m * 2 + 2)
                    pe.matmul(psE[:, 0:2 * P], gKT[:, 1, :], ga["VND"][:, 2 * P:4 * P], start=True, stop=True) \
                        .then_inc(S("g_s"), 1)
                    for j in range(2):
                        o = psF[:, j * SEQ + CH:(j + 1) * SEQ]
                        pe.matmul(o, gS1[:, j, :], gQD[:, j, :], start=True, stop=False)
                        mm = pe.matmul(o, gVN[:, 2 + j, :], gQK[:, 2 + j, :], start=False, stop=True)
                    mm.then_inc(S("g_o"), 1)
                for i in range(4):
                    if e == 43 + i:
                        if i == 0:
                            pe.wait_ge(S("g_wtc"), m + 1)
                        if i >= 2:
                            pe.wait_ge(S("g_su"), m * 4 + i - 1)
                        bank = (psA, psB)[i % 2]
                        for b in (2 * i, 2 * i + 1):
                            at = (b % 2) * 256
                            mm = pe.matmul(bank[:, at:at + 256], gKM[:, b, :], gWT[0:NS, :], start=True, stop=True)
                        mm.then_inc(S("g_sp"), 1)
                if e == 47:
                    pe.wait_ge(S("g_sq"), m * 2 + 2)
                    col_sum(psC[:, 0:T], gSQ[:, 0, :])
                    col_sum(psD[:, 0:T], gSQ[:, 1, :]).then_inc(S("g_os"), 1)

            def bank_wait_act(m, per, t0, phase_t, took0):
                pe.wait_ge(took_act, m * per + (took0 + t0 - phase_t - 1))

            norm_sum(0)
            for k in range(6):
                if k >= 2:
                    bank_wait_act(0, 0, T_GPRO + k, T_GPRO, TA_G)
                for e in range(8):
                    project(0, 0, T_GPRO + k, e, fresh=X0["g"] if k == 0 else None)
                if k == 2:
                    pe.wait_ge(S("g_hrows"), 1)
                    for n in range(4):
                        for c in range(NC):
                            src = HRG[0:GV, (7, 3, 4, 5)[n], c * CH:(c + 1) * CH]
                            at = (n * NC + c) * GV
                            mm = pe.transpose(psA[:, at:at + GV], src, ident[0:GV, 0:GV])
                    mm.then_inc(S("g_ccol"), 1)

            with pe.Fori(0, GH - 1) as m:
                for e in range(48):
                    if e % 8 == 0:
                        bank_wait_act(m, 6, T_GLOOP + e // 8, T_GPRO, TA_G)
                    project(m, 6, T_GLOOP + e // 8, e % 8)
                    gdn_mix(m, e)
            for e in range(48):
                if 16 <= e < 32:
                    if e % 8 == 0:
                        bank_wait_act(0, 0, T_GEND + (e - 16) // 8, T_GPRO, TA_G)
                    project(0, 0, T_GEND + (e - 16) // 8, e % 8)
                gdn_mix(GH - 1, e)

            def dense(t0, x0, first_free, sem_took, took0, last=None):
                for k in range(2):
                    first_free(k)
                    for e in range(8):
                        project(0, 0, t0 + k, e, fresh=x0 if k == 0 else None)
                with pe.Fori(1, KT // 2) as i:
                    for k in range(2):
                        pe.wait_ge(sem_took, i * 2 + (took0 + k - 1))
                        for e in range(8):
                            project(i, 2, t0 + k, e)
                        if last is not None:
                            last(i, k)

            def out_proj(t0, xa, xb, td, ta):
                dense(t0, xa, lambda k: pe.wait_ge(took_act, ta), took_dve, td)
                dense(t0 + 16, xb, lambda k: pe.wait_ge(took_dve, td + 15 + k), took_dve, td + 16)

            def ple(tp, te, xp, xe, td, ta, hs, es, hq):
                for i in range(KT):
                    a, hc = i // 8, 2 * (tp + i // 8) + (i % 8) // 4
                    if i % 4 == 0:
                        pe.wait_ge(wl_ready, hc + 1)
                    pe.wait_ge(took_dve, td + i - 1)
                    out = psj[(tp + i) % 2][:, 0:T]
                    for kt in range(PLE_K):
                        if i == 0:
                            pe.wait_ge(xl_ready, xp + kt + 1)
                        at = (2 * i + kt) % 8
                        pe.matmul(out, wh[:, hc % 4, at, :], xh[:, kt, :], start=(kt == 0), stop=False)
                        pe.matmul(out, wh[:, hc % 4, at, :], xl[:, kt, :], start=False, stop=False)
                        mm = pe.matmul(out, wl[:, hc % 4, at, :], xh[:, kt, :], start=False, stop=(kt == PLE_K - 1))
                    if i % 4 != 3:
                        mm.then_inc(S("e_done"), 1)
                    else:
                        mm.then_inc(half_done, 1)
                    if i >= 1:
                        pe.wait_ge(S("esq"), es + i)
                        col_sum(psB[:, 0:T], dSQ[:, (i - 1) % 2, :], start=(i == 1), stop=False) \
                            .then_inc(S("ess"), 1)
                pe.wait_ge(S("esq"), es + KT)
                col_sum(psB[:, 0:T], dSQ[:, (KT - 1) % 2, :], start=False, stop=True).then_inc(S("ess"), 1)

                def add_sum(i, k):
                    pe.wait_ge(S("hsq"), i * 2 + (hq + k - 1))
                    col_sum(psA[:, 0:T], dSQ[:, k, :], start=False, stop=False).then_inc(S("hss"), 1)

                for k in range(2):
                    pe.wait_ge(took_dve, td + KT)
                    for e in range(8):
                        project(0, 0, te + k, e, fresh=xe if k == 0 else None)
                for k in range(2, 4):
                    pe.wait_ge(took_act, ta + k - 1)
                    for e in range(8):
                        project(0, 0, te + k, e)
                    pe.wait_ge(S("hsq"), hq + k - 1)
                    col_sum(psA[:, 0:T], dSQ[:, k % 2, :], start=(k == 2), stop=False).then_inc(S("hss"), 1)
                with pe.Fori(2, KT // 2) as i:
                    for k in range(2):
                        pe.wait_ge(took_act, i * 2 + (ta + k - 1))
                        for e in range(8):
                            project(i, 2, te + k, e)
                        add_sum(i, k)
                for k in range(2):
                    pe.wait_ge(S("hsq"), hq + 15 + k)
                    col_sum(psA[:, 0:T], dSQ[:, k, :], start=False, stop=(k == 1)).then_inc(S("hss"), 1)

            out_proj(T_O1, X0["oa1"], X0["ob1"], TD_O1, TA_E1)
            ple(T_P1, T_E1, X0["p1"], X0["e1"], TD_P1, TA_E1, 16, 0, 16)

            def ssd_mix(m, e):
                if e == 17:
                    pe.wait_ge(S("s_cv"), m + 1)
                    pe.wait_ge(S("s_yd"), m + 1)
                    for c in range(NC):
                        pe.transpose(psA[:, c * P:(c + 1) * P], sCV[:, 0, c * CH:(c + 1) * CH], ident)
                        bank = (psB, psC)[c]
                        for i in range(SX):
                            pe.transpose(bank[:, i * P:(i + 1) * P], sCV[:, 2 + i, c * CH:(c + 1) * CH], ident)
                        pe.matmul(psD[:, c * CH:(c + 1) * CH], sCV[:, 0, c * CH:(c + 1) * CH],
                                  sCV[:, 1, c * CH:(c + 1) * CH], start=True, stop=True)
                    pe.transpose(psE[0:NS, 0:P], sCV[:, 0, SEQ:T], ident).then_inc(S("s_tok"), 1)
                if e == 20:
                    pe.wait_ge(S("s_pr"), m + 1)
                    col_sum(psF[:, 0:NPAIR], sPR)
                    pe.wait_ge(S("s_st_in"), m * 16 + 16)
                    for b in range(DEC_B):
                        for i in range(SX):
                            at = P + (i * DEC_B + b) * DEC_T
                            mm = pe.matmul(psF[:, at:at + DEC_T], sS[:, b, 2 * i:2 * i + 2, :],
                                           sCV[:, 1, SEQ + b:T:DEC_B], start=True, stop=True)
                    mm.then_inc(S("s_smp"), 1)
                if e == 24:
                    pe.wait_ge(S("s_xd"), m * 2 + 1)
                    pe.wait_ge(S("s_btc"), m + 1)
                    pe.matmul(psA[:, :], sBT[:, 0, :], sa["XD"], start=True, stop=True).then_inc(S("s_s"), 1)
                for c in range(NC):
                    if e == (28, 36)[c]:
                        pe.wait_ge(S("s_w"), m * 2 + c + 1)
                        for i in range(SX):
                            for j in range(2):
                                mm = pe.matmul((psB, psC)[c][HD * j:HD * j + HD, i * P:(i + 1) * P],
                                               sX[:, c, 2 * i + j, :], sDT[:, 2 * i + j, :], start=True, stop=True)
                        mm.then_inc(S("s_y"), 1)
                if e == 32:
                    pe.wait_ge(S("s_s1"), m + 1)
                    for i in range(SX):
                        mm = pe.matmul(psD[:, i * P:(i + 1) * P], sS1[:, i * P:(i + 1) * P],
                                       sCV[:, 1, CH:2 * CH], start=True, stop=True)
                    mm.then_inc(S("s_off"), 1)
                    pe.wait_ge(S("s_xd"), m * 2 + 2)
                    pe.matmul(psA[:, :], sBT[:, 1, :], sa["XD"], start=True, stop=True).then_inc(S("s_s"), 1)
                if e == 40:
                    pe.wait_ge(S("s_xe"), m + 1)
                    for i in range(SX):
                        mm = pe.transpose(psE[0:NS, i * P:(i + 1) * P], sXE[:, i, :], ident)
                    mm.then_inc(S("s_xt"), 1)
                for b in range(DEC_B):
                    if e == 44 + 2 * b:
                        if b == 0:
                            pe.wait_ge(S("s_xtc"), m + 1)
                            pe.wait_ge(S("s_yt"), m + 1)
                        if b >= 2:
                            pe.wait_ge(S("s_su"), m * 8 + b - 1)
                        pe.matmul((psA, psF)[b % 2][:, :], sBMv[:, b, :], sXT[0:NS, :], start=True, stop=True) \
                            .then_inc(S("s_sp"), 1)
                if e == 72:
                    pe.wait_ge(S("s_sq"), m + 1)
                    for i in range(SX):
                        mm = col_sum(psE[:, 0:T], sZS[:, i, :], start=(i == 0), stop=(i == SX - 1))
                    mm.then_inc(S("s_ss"), 1)

            for k in range(7):
                bank_wait_act(0, 0, max(T_SPRO + k, T_SPRO + 1), T_SPRO, TA_S)
                for e in range(8):
                    project(0, 0, T_SPRO + k, e, fresh=X0["s"] if k == 0 else None)
                if k == 2:
                    pe.wait_ge(S("s_hrows"), 1)
                    for n in range(3):
                        for c in range(NC):
                            src = HRG[0:SH, (4, 3, 5)[n], c * CH:(c + 1) * CH]
                            at = (n * NC + c) * SH
                            mm = pe.transpose(psA[:, at:at + SH], src, ident[0:SH, 0:SH])
                    mm.then_inc(S("s_ccol"), 1)
            with pe.Fori(0, SG - 1) as m:
                for e in range(80):
                    if e % 8 == 0:
                        bank_wait_act(m, 10, T_SLOOP + e // 8, T_SPRO, TA_S)
                    project(m, 10, T_SLOOP + e // 8, e % 8)
                    ssd_mix(m, e)
            for e in range(80):
                if 32 <= e < 64:
                    if e % 8 == 0:
                        bank_wait_act(0, 0, T_SEND + (e - 32) // 8, T_SPRO, TA_S)
                    project(0, 0, T_SEND + (e - 32) // 8, e % 8)
                ssd_mix(SG - 1, e)

            out_proj(T_O2, X0["oa2"], X0["ob2"], TD_O2, TA_E2)
            ple(T_P2, T_E2, X0["p2"], X0["e2"], TD_P2, TA_E2, 32, 16, 32)

        @block.scalar
        def _(act):
            ao = Order(act, act_order)

            def upper(m, per, hc):
                act.wait_ge(w_in[hc % 4], m * (4 * per) + 16 * (hc // 4 + 1))
                if hc >= 4:
                    act.wait_ge(half_done, m * per + (hc - 3))
                act.activation(wh[:, hc % 4], ring[:, hc % 4], ACT.Copy).then_inc(wh_ready, 1)

            def ahead(m, per, t):
                upper(m, 2 * per, 2 * t)
                upper(m, 2 * per, 2 * t + 1)

            def tile_wait(m, per, t):
                act.wait_ge(half_done, m * (2 * per) + 2 * t + 2)

            def split_x(src, n, t0):
                if t0:
                    act.wait_ge(half_done, 2 * t0)
                for kt in range(n):
                    act.activation(xh[:, kt, :], src(kt), ACT.Copy).then_inc(xh_ready, 1)

            def normed_x(base, t0):
                act.wait_ge(S("hss"), base + KT)
                act.activation(dRS, psA[:, 0:T], ACT.Sqrt, bias=eps_c, scale=1.0 / D_MODEL) \
                    .then_inc(S("n_root"), 1)
                if t0:
                    act.wait_ge(half_done, 2 * t0)
                n0 = base
                for kt in range(KT):
                    act.wait_ge(S("xn"), n0 + kt + 1)
                    act.activation(xh[:, kt, :], dTM[:, kt % 2, :], ACT.Copy).then_inc(xh_ready, 1)

            def softplus_rows(n, dtc, ac, tile_t, pre, took):
                tile_wait(0, 0, tile_t)
                act.activation(HRG[0:n, 0, :], psj[tile_t % 2][0:n, 0:T], ACT.Identity,
                               bias=prm[0:n, dtc:dtc + 1]).then_inc(took_act, 1)
                act.wait_ge(took_act, took + 1)
                ao.link(act.activation(HRG[0:n, 1, :], HRG[0:n, 0, :], ACT.Abs))
                act.activation(small[0:n, 2:3], prm[0:n, ac:ac + 1], ACT.Exp)
                act.activation(HRG[0:n, 1, :], HRG[0:n, 1, :], ACT.Exp, scale=-1.0).then_inc(S(pre + "exp"), 1)
                act.wait_ge(S(pre + "w1"), 1)
                act.activation(HRG[0:n, 3, :], HRG[0:n, 2, :], ACT.Ln).then_inc(S(pre + "ln"), 1)
                act.wait_ge(S(pre + "cum"), 1)
                act.activation(HRG[0:n, 8, :], HRG[0:n, 6, :], ACT.Exp)
                act.activation(HRG[0:n, 5, 0:SEQ], HRG[0:n, 1, 0:SEQ], ACT.Exp).then_inc(S(pre + "eg"), 1)

            act.wait_ge(S("x_in"), 16)
            act.wait_ge(S("prm_in"), 16)
            act.wait_ge(S("konst"), 1)
            for kt in range(KT):
                if kt >= 2:
                    act.wait_ge(S("hss"), kt - 1)
                act.activation(dSQ[:, kt % 2, :], h[:, kt, :], ACT.Square).then_inc(S("hsq"), 1)
            ahead(0, 0, 0)
            ahead(0, 0, 1)
            normed_x(0, 0)
            act.dma_start(h_spill, h[:, :, :]).then_inc(S("spill"), 16)

            def take_u(i, U):
                return lambda bank: (act.activation(U[:, i, UP:UC], bank[:, 0:SEQ], ACT.Copy),
                                     act.activation(U[:, i, US:UW], bank[:, SEQ:T], ACT.Copy))[1]

            def g_load(m):
                act.dma_start(ga["R"], g_rows[m].partition_broadcast(P)).then_inc(S("g_r_in"), 16)
                act.dma_start(ga["pc"], gpack[m]).then_inc(S("g_pc_in"), 16)
                act.dma_start(hf[:, 0:2048], gstate[m]).then_inc(S("g_st_in"), 16)

            softplus_rows(GV, C_GDT, C_GA, 0, "g_", TA_G)
            ahead(0, 0, 2)
            tile_wait(0, 0, 1)
            act.activation(HRG[0:GV, 7, :], psj[1][0:GV, 0:T], ACT.Sigmoid).then_inc(took_act, 1)
            ahead(0, 0, 3)
            act.wait_ge(S("g_hrows"), 1)
            act.dma_start(g_rows.rearrange("m (j c) -> (m j) c", j=2), HRG[0:GV, 6:9, :]) \
                .then_inc(S("g_rows_out"), 16)
            act.wait_ge(S("zero_u"), 1)
            tile_wait(0, 0, 2)
            take_u(0, gU)(psj[0]).then_inc(took_act, 1)
            ahead(0, 0, 4)
            act.wait_ge(S("g_ccol"), 1)
            act.activation(ccol[:, 0:256], psA[:, 0:256], ACT.Copy).then_inc(S("g_ccolc"), 1)
            tile_wait(0, 0, 3)
            take_u(1, gU)(psj[1]).then_inc(took_act, 1)
            ahead(0, 0, 5)
            act.wait_ge(S("g_rows_out"), 16)
            act.wait_ge(S("spill"), 16)
            g_load(0)
            tile_wait(0, 0, 4)
            take_u(2, gU)(psj[0]).then_inc(took_act, 1)
            ahead(0, 0, 6)
            tile_wait(0, 0, 5)
            take_u(3, gU)(psj[1]).then_inc(took_act, 1)

            def g_roots(bankq, bankk, scale):
                act.activation(gRS[:, 0, :], bankq[:, 0:T], ACT.Sqrt, bias=eps_c, scale=scale)
                return act.activation(gRS[:, 1, :], bankk[:, 0:T], ACT.Sqrt, bias=eps_c, scale=scale)

            def gdn_body(m, full):
                per = 6 if full else 0
                if full:
                    ahead(m, per, T_GLOOP + 1)
                act.wait_ge(S("g_conv"), m + 1)
                ao.link(act.activation(ga["CV"], ga["CV"], ACT.Silu))
                act.activation(gSQ[:, :, :], gCV[:, 0:2, :], ACT.Square).then_inc(S("g_sq"), 1)
                if full:
                    tile_wait(m, per, T_GLOOP)
                    take_u(0, gU)(psj[T_GLOOP % 2]).then_inc(took_act, 1)
                    ahead(m, per, T_GLOOP + 2)
                else:
                    ahead(0, 0, T_GEND + 1)
                act.wait_ge(S("g_ss"), m + 1)
                g_roots(psA, psB, 1.0).then_inc(S("g_rs"), 1)
                if full:
                    tile_wait(m, per, T_GLOOP + 1)
                    take_u(1, gU)(psj[(T_GLOOP + 1) % 2]).then_inc(took_act, 1)
                    ahead(m, per, T_GLOOP + 3)
                act.wait_ge(S("g_dtx"), m + 1)
                act.activation(ga["DT"], ga["DT"], ACT.Exp)
                act.activation(ga["DEC"], ga["DEC"], ACT.Exp).then_inc(S("g_dte"), 1)
                act.wait_ge(S("g_tok"), m + 1)
                act.activation(ga["KTK"], psA[:, 0:2 * P], ACT.Copy)
                for c in range(NC):
                    for j in range(2):
                        u = 2 * c + j
                        ins = act.activation(gVB[:, u, :], psB[:, u * P:(u + 1) * P], ACT.Copy,
                                             scale=gcc[:, 0, c, j:j + 1])
                ins.then_inc(S("g_vb"), 1)
                act.wait_ge(S("g_dt"), m + 1)
                act.activation(ga["D"], psB[:, :], ACT.Copy).then_inc(S("g_d"), 1)
                zt = T_GLOOP + 2 if full else T_GEND
                tile_wait(m if full else 0, per, zt)
                act.activation(gZS[:, 0, :], psj[zt % 2][:, 0:T], ACT.Silu).then_inc(took_act, 1)
                if full:
                    ahead(m, per, T_GLOOP + 4)
                else:
                    ahead(0, 0, T_O1)
                tile_wait(m if full else 0, per, zt + 1)
                act.activation(gZS[:, 1, :], psj[(zt + 1) % 2][:, 0:T], ACT.Silu).then_inc(took_act, 1)
                if full:
                    ahead(m, per, T_GLOOP + 5)
                act.wait_ge(S("g_vn"), m * 2 + 1)
                act.activation(ga["VN"][:, 0:2 * P], psC[:, 0:2 * P], ACT.Copy)
                for j in range(2):
                    ins = act.activation(gVND[:, j, :], psC[:, j * P:(j + 1) * P], ACT.Copy,
                                         scale=gcc[:, 3, 0, j:j + 1])
                ins.then_inc(S("g_vnd"), 1)
                act.wait_ge(S("g_s"), m * 2 + 1)
                act.wait_ge(S("g_km"), m + 1)
                act.activation(ga["S1"], psE[:, 0:2 * P], ACT.Copy).then_inc(S("g_s1"), 1)
                act.wait_ge(S("g_wt"), m + 1)
                act.activation(gWT[0:NS, :], psB[0:NS, 0:2 * P], ACT.Copy).then_inc(S("g_wtc"), 1)
                if full:
                    tile_wait(m, per, T_GLOOP + 4)
                    take_u(2, gU)(psj[T_GLOOP % 2]).then_inc(took_act, 1)
                    ahead(m, per, T_GLOOP + 6)
                act.wait_ge(S("g_vn"), m * 2 + 2)
                act.activation(ga["VN"][:, 2 * P:4 * P], psC[:, 0:2 * P], ACT.Copy)
                for j in range(2):
                    ins = act.activation(gVND[:, 2 + j, :], psC[:, j * P:(j + 1) * P], ACT.Copy,
                                         scale=gcc[:, 3, 1, j:j + 1])
                ins.then_inc(S("g_vnd"), 1)
                act.wait_ge(S("g_o"), m + 1)
                ao.link(act.activation(gO[:, :, 0:SEQ], psF[:, :].rearrange("p (j t) -> p j t", j=2), ACT.Copy))
                act.wait_ge(S("g_os_dve"), m + 1)
                act.activation(ga["SQ"], ga["O"], ACT.Square).then_inc(S("g_sq"), 1)
                act.wait_ge(S("g_os"), m + 1)
                g_roots(psC, psD, 1.0 / P).then_inc(S("g_rs2"), 1)
                act.wait_ge(S("g_s2"), m + 1)
                act.dma_start(gst_p[m], ga["S2"]).then_inc(S("g_sp_out"), 16)
                act.dma_start(gconv_out[m], ga["co"]).then_inc(S("g_co_out"), 16)
                act.wait_ge(S("g_su"), m * 4 + 4)
                act.dma_start(gst_s[m], hf[:, 0:2048]).then_inc(S("g_st_out"), 16)
                if full:
                    tile_wait(m, per, T_GLOOP + 5)
                    take_u(3, gU)(psj[(T_GLOOP + 5) % 2]).then_inc(took_act, 1)
                act.wait_ge(S("g_y"), m + 2)
                act.wait_ge(S("g_st_out"), m * 16 + 16)
                act.wait_ge(S("g_sp_out"), m * 16 + 16)
                act.wait_ge(S("g_co_out"), m * 16 + 16)
                if full:
                    g_load(m + 1)

            with act.Fori(0, GH - 1) as m:
                ao.enter(m, G_ACT)
                gdn_body(m, True)
            ao.leave(GH - 1)
            gdn_body(GH - 1, False)
            act.dma_start(h[:, :, :], h_spill).then_inc(S("h_back"), 16)

            def dense(t0, src):
                split_x(src, KT, t0)
                ahead(0, 0, t0 + 1)
                with act.Fori(0, KT // 2 - 1) as i:
                    for k in range(2):
                        ahead(i, 2, t0 + 2 + k)
                ahead(0, 0, t0 + KT)

            def ple(tp, te, es, hq, hbase, td, end):
                act.wait_ge(S("p_in"), 16 + es)
                split_x(lambda kt: dp[:, kt, :], PLE_K, tp)
                ahead(0, 0, tp + 1)
                for i in range(KT):
                    if i == 7:
                        ahead(0, 0, te)
                    act.wait_ge(took_dve, td + i + 1)
                    if i >= 2 or es:
                        act.wait_ge(S("ess"), es + i - 1)
                    act.activation(dSQ[:, i % 2, :], eb[:, i, :], ACT.Square).then_inc(S("esq"), 1)
                act.wait_ge(S("ess"), es + KT)
                act.activation(dRE, psB[:, 0:T], ACT.Sqrt, bias=eps_c, scale=1.0 / D_MODEL) \
                    .then_inc(S("e_root"), 1)

                def gate(i, k):
                    act.wait_ge(half_done, i * 4 + 2 * (te + k) + 2)
                    act.wait_ge(S("hnew"), i * 2 + (hq - 16 + k - 1)) if hq - 16 + k - 1 > 0 else None
                    act.activation(dSG[:, k % 2, :], psj[(te + k) % 2][:, 0:T], ACT.Sigmoid).then_inc(took_act, 1)

                def square(i, k):
                    act.wait_ge(S("hnew"), i * 2 + (hq - 16 + k + 1))
                    act.wait_ge(S("hss"), i * 2 + (hq + k - 1))
                    act.activation(dSQ[:, k % 2, :], h[:, (i * 2 + k), :], ACT.Square).then_inc(S("hsq"), 1)

                act.wait_ge(took_dve, td)
                split_x(lambda kt: h[:, kt, :], KT, te)
                ahead(0, 0, te + 1)
                gate(0, 0)
                ahead(0, 0, te + 2)
                gate(0, 1)
                square(0, 0)
                with act.Fori(0, KT // 2 - 2) as i:
                    for k in range(2):
                        ahead(i, 2, te + 3 + k)
                        gate(i, 2 + k)
                        square(i, 1 + k)
                ahead(0, 0, te + KT - 1)
                gate(0, KT - 2)
                square(0, KT - 3)
                if not end:
                    ahead(0, 0, te + KT)
                gate(0, KT - 1)
                square(0, KT - 2)
                square(0, KT - 1)

            def out_proj(t0, td):
                dense(t0, lambda kt: Y[:, kt, :])
                dense(t0 + KT, lambda kt: Y[:, KT + kt, :])

            act.wait_ge(S("g_y"), GH + 1)
            out_proj(T_O1, TD_O1)
            act.dma_start(dp[:, :, :], p_in[0]).then_inc(S("p_in"), 16)
            ple(T_P1, T_E1, 0, 16, 16, TD_P1, False)

            normed_x(16, T_SPRO)
            act.dma_start(h_spill, h[:, :, :]).then_inc(S("spill"), 16)
            ahead(0, 0, T_SPRO + 1)
            softplus_rows(SH, C_SDT, C_SA, T_SPRO, "s_", TA_S)

            def s_load(m):
                act.dma_start(sa["R2"].rearrange("p (h t) -> p h t", h=HPG),
                              s_rows[m].rearrange("h c -> (h c)").partition_broadcast(P)
                              .rearrange("p (h c) -> p h c", h=HPG)[:, :, 0:T]).then_inc(S("s_r_in"), 16)
                for j in range(2):
                    act.dma_start(sRP[HD * j:HD * j + HD, :, :],
                                  s_rows[m].rearrange("h c -> (h c)").partition_broadcast(HD)
                                  .rearrange("p (i j c) -> p i j c", i=SX, j=2)[:, :, j, 256:480]) \
                        .then_inc(S("s_rp_in"), 16)
                act.dma_start(sa["pc"], spack[m]).then_inc(S("s_pc_in"), 16)
                act.dma_start(hf[:, 0:4096], sstate[m]).then_inc(S("s_st_in"), 16)

            ahead(0, 0, T_SPRO + 2)
            act.wait_ge(S("s_hrows"), 1)
            sr = s_rows.rearrange("g h c -> (g h) c")
            act.dma_start(sr[:, 0:T], HRG[0:SH, 6, :]).then_inc(S("s_rows_out"), 16)
            act.dma_start(sr[:, T:T + 160], HRG[0:SH, 8, 128:T]).then_inc(S("s_rows_out"), 16)
            act.dma_start(sr[:, T + 160:T + 192], HRG[0:SH, 4, SEQ:T]).then_inc(S("s_rows_out"), 16)
            for k in range(1, 7):
                tile_wait(0, 0, T_SPRO + k)
                take_u(k - 1, sU)(psj[(T_SPRO + k) % 2]).then_inc(took_act, 1)
                if k == 2:
                    act.wait_ge(S("s_ccol"), 1)
                    act.activation(ccol[:, 0:384], psA[:, 0:384], ACT.Copy).then_inc(S("s_ccolc"), 1)
                if k == 3:
                    act.wait_ge(S("s_rows_out"), 48)
                    act.wait_ge(S("spill"), 32)
                    s_load(0)
                if k < 6:
                    ahead(0, 0, T_SPRO + k + 2)

            def ssd_body(m, full):
                per, t0 = (10, T_SLOOP) if full else (0, T_SEND - 4)
                mt = m if full else 0
                order = [0, 1, 2, 3, None, None, None, None, 4, 5]

                def took(k):
                    if not full and not 4 <= k < 8:
                        return
                    tile_wait(mt, per, t0 + k)
                    bank = psj[(t0 + k) % 2]
                    if order[k] is not None:
                        take_u(order[k], sU)(bank).then_inc(took_act, 1)
                    else:
                        act.activation(sZS[:, k - 4, :], bank[:, 0:T], ACT.Silu).then_inc(took_act, 1)
                    if full and k < 9:
                        ahead(mt, per, t0 + k + 2)
                    if not full and k < 6:
                        ahead(0, 0, t0 + k + 2)
                    if not full and k == 6:
                        ahead(0, 0, T_O2)

                if full:
                    ahead(mt, per, t0 + 1)
                else:
                    ahead(0, 0, T_SEND + 1)
                act.wait_ge(S("s_conv"), m + 1)
                for i in range(6):
                    ins = act.activation(sCV[:, i, :], sCV[:, i, :], ACT.Silu, bias=spc[:, i, 28:29])
                ins.then_inc(S("s_cv"), 1)
                took(0)
                took(1)
                act.wait_ge(S("s_tok"), m + 1)
                act.activation(sa["BT"], psA[:, 0:2 * P], ACT.Copy).then_inc(S("s_btc"), 1)
                act.wait_ge(S("s_r_in"), m * 16 + 16)
                act.activation(sEGc, sR2[:, :, SEQ - 1], ACT.Exp)
                act.activation(sEGb, sR2[:, :, T - DEC_B:T], ACT.Exp)
                act.wait_ge(S("s_decx"), m + 1)
                act.activation(sa["DEC"], sa["DEC"], ACT.Exp).then_inc(S("s_dec"), 1)
                act.wait_ge(S("s_dtx"), m * 2 + 1)
                act.activation(sa["DT"], sa["DT"], ACT.Exp).then_inc(S("s_dt"), 1)
                took(2)
                act.wait_ge(S("s_s"), m * 2 + 1)
                act.activation(sS1, psA[:, :], ACT.Copy).then_inc(S("s_s1"), 1)
                took(3)
                act.wait_ge(S("s_dtx"), m * 2 + 2)
                act.activation(sa["DT"], sa["DT"], ACT.Exp).then_inc(S("s_dt"), 1)
                act.wait_ge(S("s_y"), m * 2 + 1)
                act.activation(sYT[:, :, 0:CH], psB[:, :].rearrange("p (i t) -> p i t", i=SX), ACT.Copy) \
                    .then_inc(S("s_y0"), 1)
                took(4)
                act.wait_ge(S("s_xt"), m + 1)
                act.wait_ge(S("s_bm"), m + 1)
                act.activation(sXT[0:NS, :], psE[0:NS, :], ACT.Copy).then_inc(S("s_xtc"), 1)
                took(5)
                took(6)
                took(7)
                act.wait_ge(S("s_g"), m + 1)
                act.activation(sa["ZS"], sa["YT"], ACT.Square).then_inc(S("s_sq"), 1)
                took(8)
                act.wait_ge(S("s_ss"), m + 1)
                act.activation(sTMr, psE[:, 0:T], ACT.Sqrt, bias=eps_c, scale=1.0 / (SX * P)).then_inc(S("s_root"), 1)
                act.wait_ge(S("s_s2"), m + 1)
                act.dma_start(sst_p[m], sS1).then_inc(S("s_sp_out"), 16)
                act.dma_start(sconv_out[m], sa["co"]).then_inc(S("s_co_out"), 16)
                act.wait_ge(S("s_su"), m * 8 + 8)
                act.dma_start(sst_s[m], hf[:, 0:4096]).then_inc(S("s_st_out"), 16)
                took(9)
                act.wait_ge(S("s_yd"), m + 2)
                act.wait_ge(S("s_st_out"), m * 16 + 16)
                act.wait_ge(S("s_sp_out"), m * 16 + 16)
                act.wait_ge(S("s_co_out"), m * 16 + 16)
                if full:
                    s_load(m + 1)

            with act.Fori(0, SG - 1) as m:
                ao.enter(m, S_ACT)
                ssd_body(m, True)
            ao.leave(SG - 1)
            ssd_body(SG - 1, False)
            act.dma_start(h[:, :, :], h_spill).then_inc(S("h_back"), 16)
            act.wait_ge(S("s_yd"), SG + 1)
            out_proj(T_O2, TD_O2)
            act.dma_start(dp[:, :, :], p_in[1]).then_inc(S("p_in"), 16)
            ple(T_P2, T_E2, 16, 32, 32, TD_P2, True)

            act.wait_ge(S("hss"), 32 + KT)
            act.activation(dRS, psA[:, 0:T], ACT.Sqrt, bias=eps_c, scale=1.0 / D_MODEL).then_inc(S("n_root"), 1)
            for kt in range(0, KT, 4):
                act.wait_ge(S("fin"), kt + 4)
                act.dma_start(y_out[:, kt:kt + 4, :], h[:, kt:kt + 4, :]).then_inc(S("y_done"), 16)
            act.wait_ge(S("y_done"), 16 * (KT // 4))

        @block.vector
        def _(dve):
            do = Order(dve, dve_order)
            dve.memset(small[:, 0:1], EPS).then_inc(S("konst"), 1)

            def lower_x(src, n, x0, m=None):
                for kt in range(n):
                    dve.wait_ge(xh_ready, x0 + kt + 1)
                    dve.tensor_tensor(xl[:, kt, :], src(kt), xh[:, kt, :].bitcast(F32), ALU.subtract) \
                        .then_inc(xl_ready, 1)

            def norm_x(n, wcol, x0):
                dve.wait_ge(S("n_root"), n)
                do.link(dve.reciprocal(dRS, dRS))
                for kt in range(KT):
                    if kt >= 2:
                        dve.wait_ge(xl_ready, x0 + kt - 1)
                    dve.scalar_tensor_tensor(dTM[:, kt % 2, :], h[:, kt, :], prm[:, wcol + kt:wcol + kt + 1],
                                             dRS, ALU.mult, ALU.mult).then_inc(S("xn"), 1)
                    if kt >= 1:
                        k = kt - 1
                        dve.wait_ge(S("xn"), (n - 1) * KT + kt)
                        dve.wait_ge(xh_ready, x0 + k + 1)
                        dve.tensor_tensor(xl[:, k, :], dTM[:, k % 2, :], xh[:, k, :].bitcast(F32), ALU.subtract) \
                            .then_inc(xl_ready, 1)
                k = KT - 1
                dve.wait_ge(S("xn"), n * KT)
                dve.wait_ge(xh_ready, x0 + k + 1)
                dve.tensor_tensor(xl[:, k, :], dTM[:, k % 2, :], xh[:, k, :].bitcast(F32), ALU.subtract) \
                    .then_inc(xl_ready, 1)

            def gate_rows(n, pre):
                H = HRG[0:n]
                dve.wait_ge(S(pre + "exp"), 1)
                do.link(dve.tensor_scalar(H[:, 2, :], H[:, 1, :], 1.0, None, ALU.add))
                dve.tensor_scalar(H[:, 4, :], H[:, 2, :], -1.0, None, ALU.add).then_inc(S(pre + "w1"), 1)
                dve.wait_ge(S(pre + "w1"), 1)
                do.link(dve.tensor_scalar(H[:, 5, :], H[:, 4, :], 0.0, None, ALU.is_equal))
                do.link(dve.tensor_tensor(H[:, 4, :], H[:, 4, :], H[:, 5, :], ALU.add))
                do.link(dve.reciprocal(H[:, 4, :], H[:, 4, :]))
                dve.wait_ge(S(pre + "ln"), 1)
                do.link(dve.tensor_tensor(H[:, 3, :], H[:, 3, :], H[:, 5, :], ALU.add))
                do.link(dve.tensor_tensor(H[:, 3, :], H[:, 3, :], H[:, 1, :], ALU.mult))
                do.link(dve.tensor_tensor(H[:, 3, :], H[:, 3, :], H[:, 4, :], ALU.mult))
                do.link(dve.scalar_tensor_tensor(H[:, 4, :], H[:, 0, :], 0.0, H[:, 3, :], ALU.max, ALU.add))
                do.link(dve.tensor_scalar(H[:, 2, :], H[:, 4, :], small[0:n, 2:3], -1.0, ALU.mult, ALU.mult))
                for c in range(NC):
                    a = slice(c * CH, (c + 1) * CH)
                    dve.tensor_tensor_scan(H[:, 6, a], ones[0:n, :], H[:, 2, a], 0.0, ALU.mult, ALU.add)
                do.link(dve.tensor_copy(H[:, 6, SEQ:SEQ + 8], H[:, 2, SEQ:SEQ + 8]))
                for t in range(1, DEC_T):
                    a = SEQ + 8 * t
                    do.link(dve.tensor_tensor(H[:, 6, a:a + 8], H[:, 6, a - 8:a], H[:, 2, a:a + 8], ALU.add))
                for c in range(NC):
                    a = slice(c * CH, (c + 1) * CH)
                    dve.tensor_scalar(H[:, 1, a], H[:, 6, a], H[:, 6, (c + 1) * CH - 1:(c + 1) * CH], -1.0,
                                      ALU.subtract, ALU.mult)
                dve.tensor_scalar(H[:, 3, :], H[:, 6, :], -1.0, None, ALU.mult).then_inc(S(pre + "cum"), 1)

            dve.wait_ge(S("x_in"), 16)
            dve.wait_ge(S("prm_in"), 16)
            dve.wait_ge(c_in, 16)
            norm_x(1, C_NORM, X0["g"])
            dve.wait_ge(xl_ready, X0["g"] + KT)

            do.link(dve.memset(gU[:, :, 0:PRE], 0.0))
            gate_rows(GV, "g_")
            dve.wait_ge(S("g_eg"), 1)
            dve.wait_ge(took_act, 2)
            dve.scalar_tensor_tensor(HRG[0:GV, 4, :], HRG[0:GV, 7, :], -1.0, HRG[0:GV, 8, :],
                                     ALU.mult, ALU.mult).then_inc(S("g_hrows"), 1)
            dve.memset(small[:, 4:5], 0.0).then_inc(S("zero_u"), 1)
            dve.memset(small[:, 5:6], 0.0).then_inc(S("g_y"), 1)

            def conv(U, CV, n, tap, cache, co, ready, m, took):
                do.link(dve.tensor_copy(U[:, :, UC:US], cache))
                dve.tensor_copy(co[:, :, 0:PRE], U[:, :, UC - PRE:UC])
                dve.tensor_copy(co[:, :, PRE:CW], U[:, :, UW - PRE * DEC_B:UW])
                for j in range(CONV_W):
                    for i in range(n):
                        for dst, a, w in (((0, SEQ), j, SEQ), ((SEQ, T), UC + DEC_B * j, NS)):
                            out, src = CV[:, i, dst[0]:dst[1]], U[:, i, a:a + w]
                            if j == 0:
                                ins = dve.tensor_scalar(out, src, tap(i, j), None, ALU.mult)
                            else:
                                ins = dve.scalar_tensor_tensor(out, src, tap(i, j), out, ALU.mult, ALU.add)
                    if j < CONV_W - 1:
                        do.link(ins)
                ins.then_inc(ready, 1)

            def gdn_sample(piece, m):
                v = gCV[:, 2:4, SEQ:T]
                G, B, EG = (gR[:, :, k, SEQ:T] for k in range(3))
                kq = psD[:, 160:288].rearrange("p (b j q t) -> p q j t b", b=DEC_B, j=2, q=2)
                if piece == 0:
                    dve.wait_ge(S("g_smp"), m + 1)
                    dve.tensor_tensor(gCQ[:, :, :], gDEC[:, :, :], bc(psD[:, 0:NPAIR], 1, 2), ALU.mult)
                    do.link(dve.tensor_tensor(gCK[:, :, :], gDEC[:, :, :], bc(psD[:, NPAIR:2 * NPAIR], 1, 2),
                                              ALU.mult))
                    for s in range(3):
                        a = slice(OFF[s], OFF[s] + LEN[s])
                        dve.tensor_tensor(gCK[:, :, a], gCK[:, :, a], B[:, :, 8 * s:NS], ALU.mult)
                    do.link(dve.tensor_tensor(gBE[:, :, :], B, EG, ALU.mult))
                if piece == 1:
                    e4 = lambda ap: ap.rearrange("p j (t b) -> p j t b", b=DEC_B)
                    dve.tensor_tensor(gW[:, :, :], B, v, ALU.mult)
                    do.link(dve.tensor_tensor(e4(gTM[:, :, :]), e4(gBE[:, :, :]), kq[:, 1], ALU.mult))
                    dve.tensor_tensor(gW[:, :, :], gW[:, :, :], gTM[:, :, :], ALU.subtract)
                    do.link(dve.tensor_tensor(e4(gO[:, :, SEQ:T]), e4(EG), kq[:, 0], ALU.mult))
                if piece in (2, 3, 4):
                    s = piece - 2
                    n = DEC_T - 1 - s
                    src = bc(gW[:, :, 8 * s:8 * s + 8], 2, n)
                    out = gTM[:, :, 0:8 * n].rearrange("p j (t b) -> p j t b", b=8)
                    ck = gCK[:, :, OFF[s] + 8:OFF[s] + LEN[s]].rearrange("p j (t b) -> p j t b", b=8)
                    do.link(dve.tensor_tensor(out, ck, src, ALU.mult))
                    do.link(dve.tensor_tensor(gW[:, :, 8 * s + 8:NS], gW[:, :, 8 * s + 8:NS], gTM[:, :, 0:8 * n],
                                              ALU.subtract))
                if piece == 5:
                    for s in range(DEC_T):
                        a = OFF[s] + LEN[s] - 8
                        ins = dve.tensor_tensor(gWD[:, :, 8 * s:8 * s + 8], gW[:, :, 8 * s:8 * s + 8],
                                                gDEC[:, :, a:a + 8], ALU.mult)
                    ins.then_inc(S("g_wd"), 1)
                if piece == 6:
                    for s in range(DEC_T):
                        n = DEC_T - s
                        out = gTM[:, :, 0:8 * n].rearrange("p j (t b) -> p j t b", b=8)
                        cq = gCQ[:, :, OFF[s]:OFF[s] + LEN[s]].rearrange("p j (t b) -> p j t b", b=8)
                        do.link(dve.tensor_tensor(out, cq, bc(gW[:, :, 8 * s:8 * s + 8], 2, n), ALU.mult))
                        o = gO[:, :, SEQ + 8 * s:T]
                        ins = dve.tensor_tensor(o, o, gTM[:, :, 0:8 * n], ALU.add)
                        if s < DEC_T - 1:
                            do.link(ins)
                    ins.then_inc(S("g_os_dve"), 1)

            def u4(ap):
                return ap.rearrange("p (c j) t -> p c j t", c=NC)

            def gdn_body(m, took0):
                dve.wait_ge(S("g_pc_in"), m * 16 + 16)
                dve.wait_ge(took_act, took0)
                dve.wait_ge(S("g_r_in"), m * 16 + 16)
                dve.tensor_copy(gcc.rearrange("p k c j -> p (k c) j"),
                                ccol[:, 0:8 * GV].rearrange("p (k h) -> p k h", h=GV)[:, :, bass.ds(m * 2, 2)])
                conv(gU, gCV, 4, lambda i, j: gpc_tap[:, i, j:j + 1], gpc_cache, gco, S("g_conv"), m, None)
                for c in range(NC):
                    for j in range(2):
                        dve.tensor_scalar(gDT[:, 2 * c + j, :], gR[:, j, 0, c * CH:(c + 1) * CH],
                                          gcc[:, 1, c, j:j + 1], 0.0, ALU.add, ALU.min)
                G = gR[:, :, 0, SEQ:T].rearrange("p j (t b) -> p j t b", b=8)
                for s in range(DEC_T):
                    n = DEC_T - s
                    ins = dve.tensor_tensor(gDEC[:, :, OFF[s]:OFF[s] + LEN[s]].rearrange("p j (t b) -> p j t b", b=8),
                                            G[:, :, s:, :], bc(gR[:, :, 0, SEQ + 8 * s:SEQ + 8 * s + 8], 2, n),
                                            ALU.subtract)
                ins.then_inc(S("g_dtx"), 1)
                dve.wait_ge(S("g_rs"), m + 1)
                do.link(dve.reciprocal(ga["RS"], ga["RS"]))
                dve.scalar_tensor_tensor(gCV[:, 0, :], gCV[:, 0, :], float(P) ** -0.5, gRS[:, 0, :],
                                         ALU.mult, ALU.mult)
                dve.tensor_tensor(gCV[:, 1, :], gCV[:, 1, :], gRS[:, 1, :], ALU.mult).then_inc(S("g_kn"), 1)
                dve.wait_ge(S("g_kn"), m + 1)
                for s in range(DEC_T):
                    n = DEC_T - s
                    t4 = lambda ap: ap.rearrange("p i (t b) -> p i t b", b=8)
                    k_s = bc(bc(gCV[:, 1, SEQ + 8 * s:SEQ + 8 * s + 8], 1, n), 1, 2)
                    ins = dve.tensor_tensor(t4(gPR[:, :, OFF[s]:OFF[s] + LEN[s]]), t4(gCV[:, 0:2, SEQ + 8 * s:T]),
                                            k_s, ALU.mult)
                ins.then_inc(S("g_pr"), 1)
                dve.tensor_tensor(gQD[:, :, :], bc(gCV[:, 0, CH:2 * CH], 1, 2), gR[:, :, 2, CH:2 * CH], ALU.mult)
                dve.wait_ge(S("g_dte"), m + 1)
                do.link(dve.tensor_tensor(gDT[:, :, :], gDT[:, :, :], bc(cst[:, K_INC, :], 1, 4), ALU.mult))
                dve.wait_ge(S("g_tok"), m + 1)
                kk = bc(psC[:, 0:256].rearrange("p (c t) -> p c t", c=NC), 2, 2)
                qk = bc(psC[:, 256:512].rearrange("p (c t) -> p c t", c=NC), 2, 2)
                do.link(dve.tensor_tensor(u4(gAT[:, :, :]), u4(gDT[:, :, :]), kk, ALU.mult))
                beta = gR[:, :, 1, 0:SEQ].rearrange("p j (c t) -> p c j t", c=NC)
                do.link(dve.tensor_tensor(u4(gAT[:, :, :]), u4(gAT[:, :, :]), beta, ALU.mult))
                do.link(dve.tensor_tensor(gP[:, :, :], gAT[:, :, :], bc(cst[:, K_M1, :], 1, 4), ALU.mult))
                dve.tensor_tensor(gE[:, :, :], bc(ident, 1, 4), gP[:, :, :], ALU.subtract).then_inc(S("g_e1"), 1)
                dve.tensor_tensor(u4(gQK[:, :, :]), u4(gDT[:, :, :]), qk, ALU.mult)
                dve.tensor_tensor(gKM, bc(psE[0:NS, 0:P], 1, DEC_B), bc(bmask, 2, P), ALU.mult) \
                    .then_inc(S("g_km"), 1)
                gdn_sample(0, m)
                for lv in range(6):
                    dve.wait_ge(S("g_p"), m * 6 + lv + 1)
                    if lv == 0:
                        dve.wait_ge(S("g_e1"), m + 1)
                    dve.tensor_tensor(gP[:, :, :], psC[:, :].rearrange("p (u t) -> p u t", u=4),
                                      bc(cst[:, K_LEV + lv, :], 1, 4), ALU.mult).then_inc(S("g_pm"), 1)
                    gdn_sample(lv + 1, m)
                    dve.wait_ge(S("g_q"), m * 6 + lv + 1)
                    ins = dve.tensor_tensor(ga["E"], ga["E"], psA[:, :], ALU.subtract)
                    if lv < 5:
                        ins = dve.tensor_tensor(ga["D"], ga["D"], psB[:, :], ALU.subtract)
                    ins.then_inc(S("g_ed"), 1)
                dve.wait_ge(S("g_ks"), m + 1)
                for j in range(2):
                    ins = dve.scalar_tensor_tensor(gVB[:, 2 + j, :], psD[:, j * P:(j + 1) * P], gcc[:, 2, 1, j:j + 1],
                                                   gVB[:, 2 + j, :], ALU.mult, ALU.add)
                ins.then_inc(S("g_rhs"), 1)
                dve.wait_ge(S("g_s"), m * 2 + 2)
                for j in range(2):
                    ins = dve.scalar_tensor_tensor(gS2[:, j, :], gS1[:, j, :], gR[:, j, 2, SEQ - 1:SEQ],
                                                   psE[:, j * P:(j + 1) * P], ALU.mult, ALU.add)
                ins.then_inc(S("g_s2"), 1)
                for i in range(4):
                    dve.wait_ge(S("g_sp"), m * 4 + i + 1)
                    for b in (2 * i, 2 * i + 1):
                        for j in range(2):
                            at = (b % 2) * 256 + j * P
                            ins = dve.scalar_tensor_tensor(gS[:, b, j, :], gS[:, b, j, :],
                                                           gR[:, j, 2, T - DEC_B + b:T - DEC_B + b + 1],
                                                           (psA, psB)[i % 2][:, at:at + P], ALU.mult, ALU.add)
                    ins.then_inc(S("g_su"), 1)
                dve.wait_ge(S("g_rs2"), m + 1)
                do.link(dve.reciprocal(ga["RS"], ga["RS"]))
                do.link(dve.scalar_tensor_tensor(ga["O"], ga["O"], prm[:, C_GNORM:C_GNORM + 1], ga["RS"],
                                                 ALU.mult, ALU.mult))
                dve.tensor_tensor(Y[:, bass.ds(m * 2, 2), :], gO[:, :, :], gZS[:, :, :], ALU.mult) \
                    .then_inc(S("g_y"), 1)

            dve.wait_ge(S("g_ccolc"), 1)
            with dve.Fori(0, GH - 1) as m:
                do.enter(m, G_DVE)
                gdn_body(m, m * 6 + 6)
            do.leave(GH - 1)
            gdn_body(GH - 1, (GH - 1) * 6 + 6)

            def out_proj(t0, xa, xb, td, back):
                for n, x0 in ((0, xa), (1, xb)):
                    lower_x(lambda kt: Y[:, n * KT + kt, :], KT, x0)
                    if n == 0:
                        dve.wait_ge(S("h_back"), back)
                    with dve.Fori(0, KT // 2) as i:
                        for k in range(2):
                            t = t0 + n * KT + k
                            dve.wait_ge(half_done, i * 4 + 2 * t + 2)
                            if n == 1:
                                dve.wait_ge(took_dve, i * 2 + (td + k + 1))
                            dve.tensor_tensor(h[:, i * 2 + k, :], h[:, i * 2 + k, :], psj[t % 2][:, 0:T], ALU.add) \
                                .then_inc(took_dve, 1)

            def ple(tp, te, xp, xe, td, layer, hq):
                lower_x(lambda kt: dp[:, kt, :], PLE_K, xp)
                for i in range(KT):
                    if i % 4 == 3:
                        dve.wait_ge(half_done, 2 * tp + i // 4 + 1)
                    else:
                        dve.wait_ge(S("e_done"), layer * 12 + i - i // 4 + 1)
                    dve.tensor_copy(eb[:, i, :], psj[(tp + i) % 2][:, 0:T]).then_inc(took_dve, 1)
                lower_x(lambda kt: h[:, kt, :], KT, xe)
                dve.wait_ge(S("e_root"), layer + 1)
                do.link(dve.reciprocal(dRE, dRE))
                wc = C_PLE + layer * KT
                for i in range(KT):
                    ins = dve.scalar_tensor_tensor(eb[:, i, :], eb[:, i, :], prm[:, wc + i:wc + i + 1], dRE,
                                                   ALU.mult, ALU.mult)
                do.link(ins)
                with dve.Fori(0, KT // 2) as i:
                    do.enter(i, 2)
                    for k in range(2):
                        dve.wait_ge(took_act, i * 2 + ((TA_E1, TA_E2)[layer] + k + 1))
                        do.link(dve.tensor_tensor(dTM[:, k, :], eb[:, i * 2 + k, :], dSG[:, k, :], ALU.mult))
                        dve.tensor_tensor(h[:, i * 2 + k, :], h[:, i * 2 + k, :], dTM[:, k, :], ALU.add) \
                            .then_inc(S("hnew"), 1)
                do.leave(KT // 2)

            out_proj(T_O1, X0["oa1"], X0["ob1"], TD_O1, 16)
            ple(T_P1, T_E1, X0["p1"], X0["e1"], TD_P1, 0, 16)

            norm_x(2, C_NORM + KT, X0["s"])
            dve.wait_ge(xl_ready, X0["s"] + KT)
            do.link(dve.memset(sU[:, :, 0:PRE], 0.0))
            gate_rows(SH, "s_")
            dve.wait_ge(S("s_eg"), 1)
            dve.memset(small[:, 4:5], 0.0).then_inc(S("s_hrows"), 1)
            dve.memset(small[:, 5:6], 0.0).then_inc(S("s_yd"), 1)

            def ssd_decays(m, c):
                for hh in range(HPG):
                    ins = dve.tensor_scalar(sDT[:, hh, :], sR2[:, hh, c * CH:(c + 1) * CH],
                                            scc[:, 1, c, hh:hh + 1], 0.0, ALU.add, ALU.min)
                ins.then_inc(S("s_dtx"), 1)

            def ssd_body(m, took0):
                dve.wait_ge(S("s_pc_in"), m * 16 + 16)
                dve.wait_ge(took_act, took0)
                dve.wait_ge(S("s_r_in"), m * 16 + 16)
                dve.wait_ge(S("s_rp_in"), m * 32 + 32)
                dve.tensor_copy(scc.rearrange("p k c j -> p (k c) j"),
                                ccol[:, 0:6 * SH].rearrange("p (k h) -> p k h", h=SH)[:, :, bass.ds(m * HPG, HPG)])
                conv(sU, sCV, 6, lambda i, j: spc[:, i, 24 + j:25 + j], spc[:, :, 0:24], sco, S("s_conv"), m, None)
                A = sRP[:, :, 0:NS].rearrange("p i (t b) -> p i t b", b=8)
                for s in range(DEC_T):
                    n = DEC_T - s
                    ins = dve.tensor_tensor(
                        sDEC[:, :, OFF[s]:OFF[s] + LEN[s]].rearrange("p i (t b) -> p i t b", b=8),
                        A[:, :, s:, :], bc(sRP[:, :, 8 * s:8 * s + 8], 2, n), ALU.subtract)
                ins.then_inc(S("s_decx"), 1)
                ssd_decays(m, 0)
                dve.wait_ge(S("s_cv"), m + 1)
                Bt = sCV[:, 0, SEQ:T]
                Ct = sCV[:, 1, SEQ:T].rearrange("p (t b) -> p t b", b=8)
                for s in range(DEC_T):
                    n = DEC_T - s
                    ins = dve.tensor_tensor(sPR[:, OFF[s]:OFF[s] + LEN[s]].rearrange("p (t b) -> p t b", b=8),
                                            Ct[:, s:, :], bc(Bt[:, 8 * s:8 * s + 8], 1, n), ALU.mult)
                ins.then_inc(S("s_pr"), 1)
                dve.wait_ge(S("s_tok"), m + 1)

                def decayed(c):
                    dve.tensor_tensor(sXD, sX[:, c], bc(scc[:, 2, c, :], 2, HD), ALU.mult).then_inc(S("s_xd"), 1)

                for c in range(NC):
                    ins = dve.tensor_tensor(sX[:, c], (psB, psC)[c][:, :].rearrange("p (h d) -> p h d", h=HPG),
                                            bc(scc[:, 0, c, :], 2, HD), ALU.mult)
                do.link(ins)
                decayed(0)
                dve.tensor_tensor(sCB[:, :, :], psD[:, 0:2 * P].rearrange("p (c t) -> p c t", c=NC),
                                  bc(cst[:, K_INC, :], 1, NC), ALU.mult)
                dve.tensor_tensor(sBMv, bc(psE[0:NS, 0:P], 1, DEC_B), bc(bmask, 2, P), ALU.mult) \
                    .then_inc(S("s_bm"), 1)
                dve.wait_ge(S("s_bm"), m + 1)
                dve.wait_ge(S("s_dt"), m * 2 + 1)
                dve.tensor_tensor(sDT[:, :, :], sDT[:, :, :], bc(sCB[:, 0, :], 1, HPG), ALU.mult).then_inc(S("s_w"), 1)
                dve.wait_ge(S("s_s"), m * 2 + 1)
                decayed(1)
                dve.tensor_tensor(sXS[:, :, :], sCV[:, 2:6, SEQ:T], sRP[:, :, 192:224], ALU.mult)
                dve.wait_ge(S("s_dec"), m + 1)
                dve.wait_ge(S("s_smp"), m + 1)
                ys = sYT[:, :, SEQ:T]
                y4 = lambda ap: ap.rearrange("p i (t b) -> p i t b", b=8)
                do.link(dve.tensor_tensor(y4(ys), y4(sRP[:, :, 160:192]),
                                          psF[:, P:2 * P].rearrange("p (i b t) -> p i t b", i=SX, b=8), ALU.mult))
                for s in range(DEC_T):
                    a = OFF[s] + LEN[s] - 8
                    ins = dve.tensor_tensor(sXE[:, :, 8 * s:8 * s + 8], sXS[:, :, 8 * s:8 * s + 8],
                                            sDEC[:, :, a:a + 8], ALU.mult)
                ins.then_inc(S("s_xe"), 1)
                dve.wait_ge(S("s_xe"), m + 1)
                do.link(dve.tensor_tensor(sDEC[:, :, :], sDEC[:, :, :], bc(psF[:, 0:NPAIR], 1, SX), ALU.mult))
                for s in range(DEC_T):
                    n = DEC_T - s
                    do.link(dve.tensor_tensor(y4(sTM[:, :, 0:8 * n]), y4(sDEC[:, :, OFF[s]:OFF[s] + LEN[s]]),
                                              bc(sXS[:, :, 8 * s:8 * s + 8], 2, n), ALU.mult))
                    do.link(dve.tensor_tensor(ys[:, :, 8 * s:NS], ys[:, :, 8 * s:NS], sTM[:, :, 0:8 * n], ALU.add))
                dve.wait_ge(S("s_y"), m * 2 + 1)
                ssd_decays(m, 1)
                dve.wait_ge(S("s_off"), m + 1)
                y1 = sYT[:, :, CH:SEQ]
                do.link(dve.tensor_tensor(y1, psD[:, :].rearrange("p (i t) -> p i t", i=SX), sRP[:, :, 32:160],
                                          ALU.mult))
                dve.wait_ge(S("s_dt"), m * 2 + 2)
                dve.tensor_tensor(sDT[:, :, :], sDT[:, :, :], bc(sCB[:, 1, :], 1, HPG), ALU.mult).then_inc(S("s_w"), 1)
                dve.wait_ge(S("s_s"), m * 2 + 2)
                s1 = sS1.rearrange("p (h d) -> p h d", h=HPG)
                do.link(dve.tensor_tensor(s1, s1, bc(sEGc, 2, HD), ALU.mult))
                dve.tensor_tensor(sS1, sS1, psA[:, :], ALU.add).then_inc(S("s_s2"), 1)
                dve.wait_ge(S("s_y"), m * 2 + 2)
                dve.wait_ge(S("s_y0"), m + 1)
                do.link(dve.tensor_tensor(y1, y1, psC[:, :].rearrange("p (i t) -> p i t", i=SX), ALU.add))
                for i in range(SX):
                    ins = dve.scalar_tensor_tensor(sYT[:, i, :], sCV[:, 2 + i, :], spc_D[:, i:i + 1], sYT[:, i, :],
                                                   ALU.mult, ALU.add)
                ins.then_inc(S("s_yt"), 1)
                dve.wait_ge(S("s_yt"), m + 1)
                for b in range(DEC_B):
                    do.link(dve.tensor_tensor(sS[:, b], sS[:, b], bc(sEGb[:, :, b], 2, HD), ALU.mult))
                    dve.wait_ge(S("s_sp"), m * 8 + b + 1)
                    dve.tensor_tensor(sS[:, b], sS[:, b],
                                      (psA, psF)[b % 2][:, :].rearrange("p (h d) -> p h d", h=HPG), ALU.add) \
                        .then_inc(S("s_su"), 1)
                gate_y(m)
                dve.wait_ge(S("s_root"), m + 1)
                do.link(dve.reciprocal(sTMr, sTMr))
                for i in range(SX):
                    ins = dve.scalar_tensor_tensor(Y[:, m * SX + i, :], sYT[:, i, :], spc_norm[:, i:i + 1], sTMr,
                                                   ALU.mult, ALU.mult)
                ins.then_inc(S("s_yd"), 1)

            def gate_y(m):
                dve.wait_ge(took_act, took_z[0])
                dve.tensor_tensor(sa["YT"], sa["YT"], sa["ZS"], ALU.mult).then_inc(S("s_g"), 1)

            took_z = [0]
            dve.wait_ge(S("s_ccolc"), 1)
            with dve.Fori(0, SG - 1) as m:
                do.enter(m, S_DVE)
                took_z[0] = m * 10 + (TA_S + 7 + 8)
                ssd_body(m, m * 10 + (TA_S + 7))
            do.leave(SG - 1)
            took_z[0] = TA_S + 7 + 10 * (SG - 1) + 4
            ssd_body(SG - 1, (SG - 1) * 10 + TA_S + 7)

            out_proj(T_O2, X0["oa2"], X0["ob2"], TD_O2, 32)
            ple(T_P2, T_E2, X0["p2"], X0["e2"], TD_P2, 1, 32)

            dve.wait_ge(S("n_root"), 3)
            do.link(dve.reciprocal(dRS, dRS))
            for kt in range(KT):
                dve.scalar_tensor_tensor(h[:, kt, :], h[:, kt, :], prm[:, C_FINAL + kt:C_FINAL + kt + 1], dRS,
                                         ALU.mult, ALU.mult).then_inc(S("fin"), 1)


def _tiles(w, cols):
    k = w.shape[0] // D_MODEL
    out = []
    for part in range(k):
        blk = w[part * D_MODEL:(part + 1) * D_MODEL]
        for c in cols:
            out.append(blk[:, c:c + P].reshape(2, 8, P, P).transpose(0, 2, 1, 3))
    return out


def _narrow(w, c, n):
    import numpy as np
    a = np.concatenate([w[:, c:c + n], np.zeros((w.shape[0], P - n), w.dtype)], axis=1)
    return a.reshape(2, 8, P, P).transpose(0, 2, 1, 3)


def _tokens(prompt, sample):
    import numpy as np
    return np.concatenate([prompt, sample.transpose(1, 0, 2).reshape(NS, -1)], axis=0).T


def kernel(**inputs):
    import numpy as np
    import concourse.bacc as bacc
    from concourse.bass_utils import run_bass_kernel_spmd

    a = {k: np.asarray(v) for k, v in inputs.items()}
    gw, sw = a["gdn_w_in"][0], a["ssd_w_in"][0]
    QK, VW = GH * P, GV * P
    ZG, AG = 2 * QK + VW, 2 * QK + 2 * VW
    q = [P * n for n in range(GH)]
    k = [QK + P * n for n in range(GH)]
    v = [2 * QK + P * n for n in range(GV)]
    z = [ZG + P * n for n in range(GV)]
    DI = SH * HD
    zs = [P * n for n in range(SX * SG)]
    xs = [DI + P * n for n in range(SX * SG)]
    bs = [2 * DI + P * n for n in range(SG)]
    cs = [2 * DI + SG * P + P * n for n in range(SG)]
    stream = [_narrow(gw, AG, GV), _narrow(gw, AG + GV, GV)]
    stream += _tiles(gw, [q[0], k[0], v[0], v[1]])
    for m in range(GH - 1):
        stream += _tiles(gw, [q[m + 1], k[m + 1], z[2 * m], z[2 * m + 1], v[2 * m + 2], v[2 * m + 3]])
    stream += _tiles(gw, z[-2:])

    def dense(n, w_out):
        out = _tiles(w_out, range(0, D_MODEL, P))
        wp = a["ple_w_proj"][n].reshape(PLE_K, P, 2, 2, 4, P)
        out += list(wp.transpose(2, 3, 1, 4, 0, 5).reshape(2, 2, P, 8, P))
        return out + _tiles(a["ple_w_gate"][n], range(0, D_MODEL, P))

    stream += dense(0, a["gdn_w_out"][0])
    stream += [_narrow(sw, 2 * DI + 2 * SG * P, SH)]

    def bcx(g):
        return [bs[g], cs[g]] + xs[SX * g:SX * g + SX]

    stream += _tiles(sw, bcx(0))
    for m in range(SG - 1):
        n = bcx(m + 1)
        stream += _tiles(sw, n[:4] + zs[SX * m:SX * m + SX] + n[4:])
    stream += _tiles(sw, zs[-SX:])
    stream += dense(1, a["ssd_w_out"][0])
    weights = np.stack(stream).reshape(N_HALF, P, 8, P)

    def kt_cols(w):
        return w.reshape(-1, P).T

    def act_layout(x):
        return x.reshape(-1, P, T).transpose(1, 0, 2)

    x_in = act_layout(_tokens(a["x_prompt"][0], a["x_sample"]))
    p_in = np.stack([act_layout(_tokens(a["p_prompt"][n, 0], a["p_sample"][n])) for n in range(DEPTH)])
    prm = np.zeros((P, N_PRM), np.float32)
    prm[:, C_NORM:C_NORM + 32] = kt_cols(a["norm_w"])
    prm[:, C_PLE:C_PLE + 32] = kt_cols(a["ple_norm_w"])
    prm[:, C_FINAL:C_FINAL + 16] = kt_cols(a["final_norm_w"])
    prm[:, C_GNORM] = a["gdn_norm_w"][0]
    prm[:GV, C_GDT], prm[:GV, C_GA] = a["gdn_dt_bias"][0], a["gdn_A_log"][0]
    prm[:SH, C_SDT], prm[:SH, C_SA] = a["ssd_dt_bias"][0], a["ssd_A_log"][0]

    i, j = np.arange(P)[:, None], np.arange(P)[None, :]
    cst = np.zeros((P, N_CST, P), np.float32)
    cst[:, K_ID], cst[:, K_ONE], cst[:, K_INC] = i == j, 1.0, j >= i
    cst[:, K_M1] = (i % 2 == 0) & (j == i + 1)
    for lv in range(6):
        s = 2 << lv
        cst[:, K_LEV + lv] = (i // (2 * s) == j // (2 * s)) & (i // s % 2 == 1) & (j // s % 2 == 0)
    cst[:NS, K_BM, :DEC_B] = i[:NS] % DEC_B == j[:, :DEC_B]

    def chan(w, cols):
        return np.stack([w[:, c:c + P].T for c in cols], axis=1)

    gcache = a["cache_gdn_conv"][0].transpose(1, 0, 2).reshape(PRE * DEC_B, -1)
    scache = a["cache_ssd_conv"][0].transpose(1, 0, 2).reshape(PRE * DEC_B, -1)
    gpack, spack = [], []
    for m in range(GH):
        cols = [q[m], k[m], v[2 * m], v[2 * m + 1]]
        gpack.append(np.concatenate([chan(gcache, cols).reshape(P, -1),
                                     chan(a["gdn_conv_w"][0], cols).reshape(P, -1)], axis=1))
    D = np.repeat(a["ssd_D"][0], HD)[None]
    for g in range(SG):
        cols = [c - DI for c in bcx(g)]
        pack = np.concatenate([chan(scache, cols), chan(a["ssd_conv_w"][0], cols),
                               chan(a["ssd_conv_b"], cols)], axis=2).reshape(P, -1)
        mine = [P * (SX * g + n) for n in range(SX)]
        spack.append(np.concatenate([pack, chan(a["ssd_norm_w"], mine)[:, :, 0], chan(D, mine)[:, :, 0]], axis=1))
    gpack, spack = np.stack(gpack), np.stack(spack)
    gstate = a["state_gdn"][0].reshape(DEC_B, GH, 2, P, P).transpose(1, 3, 0, 2, 4).reshape(GH, P, -1)
    sstate = a["state_ssd"][0].reshape(DEC_B, SG, HPG, HD, P).transpose(1, 4, 0, 2, 3).reshape(SG, P, -1)

    nc = bacc.Bacc("TRN2", target_bir_lowering=False, num_devices=1)
    arrays, args = {}, {}
    for name, arr in (("weights", weights), ("x_in", x_in), ("p_in", p_in), ("prm_in", prm), ("cst_in", cst),
                      ("gpack", gpack), ("spack", spack), ("gstate", gstate), ("sstate", sstate)):
        arrays[name + "_d"] = np.ascontiguousarray(arr)
        args[name] = nc.dram_tensor(name + "_d", arr.shape, F32, kind="ExternalInput").ap()
    for name, shape in (("y_out", (P, KT, T)), ("gconv_out", (GH, P, 4 * CW)), ("sconv_out", (SG, P, 6 * CW)),
                        ("gst_p", (GH, P, 2 * P)), ("gst_s", (GH, P, DEC_B * 2 * P)),
                        ("sst_p", (SG, P, HPG * HD)), ("sst_s", (SG, P, DEC_B * HPG * HD))):
        args[name] = nc.dram_tensor(name + "_d", shape, F32, kind="ExternalOutput").ap()
    for name, shape in (("g_rows", (GH, 2 * 3 * T)), ("s_rows", (SG, HPG, 480)), ("h_spill", (P, KT, T))):
        args[name] = nc.dram_tensor(name + "_d", shape, F32, kind="Internal").ap()
    build(nc, **args, G_DVE=G_DVE_LINKS, G_ACT=2, S_DVE=S_DVE_LINKS, S_ACT=0)
    r = run_bass_kernel_spmd(nc, [arrays], core_ids=[0]).results[0]

    y = r["y_out_d"].transpose(1, 0, 2).reshape(D_MODEL, T).T
    gconv = r["gconv_out_d"].reshape(GH, P, 4, CW)
    gch = np.concatenate([gconv[:, :, 0].transpose(2, 0, 1).reshape(CW, -1),
                          gconv[:, :, 1].transpose(2, 0, 1).reshape(CW, -1),
                          gconv[:, :, 2:4].transpose(3, 0, 2, 1).reshape(CW, -1)], axis=1)
    sconv = r["sconv_out_d"].reshape(SG, P, 6, CW)
    sch = np.concatenate([sconv[:, :, 2:6].transpose(3, 0, 2, 1).reshape(CW, -1),
                          sconv[:, :, 0].transpose(2, 0, 1).reshape(CW, -1),
                          sconv[:, :, 1].transpose(2, 0, 1).reshape(CW, -1)], axis=1)

    def caches(c):
        return c[None, None, :PRE], c[PRE:].reshape(PRE, DEC_B, -1).transpose(1, 0, 2)[None]

    cg_p, cg_s = caches(gch)
    cs_p, cs_s = caches(sch)
    sg_p = r["gst_p_d"].reshape(GH, P, 2, P).transpose(0, 2, 1, 3).reshape(1, 1, GV, P, P)
    sg_s = r["gst_s_d"].reshape(GH, P, DEC_B, 2, P).transpose(2, 0, 3, 1, 4).reshape(1, DEC_B, GV, P, P)
    ss_p = r["sst_p_d"].reshape(SG, P, HPG, HD).transpose(0, 2, 3, 1).reshape(1, 1, SH, HD, P)
    ss_s = r["sst_s_d"].reshape(SG, P, DEC_B, HPG, HD).transpose(2, 0, 3, 4, 1).reshape(1, DEC_B, SH, HD, P)
    y_s = y[SEQ:].reshape(DEC_T, DEC_B, D_MODEL).transpose(1, 0, 2)
    return tuple(np.ascontiguousarray(o) for o in
                 (y[:SEQ][None], y_s, sg_p, cg_p, ss_p, cs_p, sg_s, cg_s, ss_s, cs_s))
```

```python
from contextlib import ExitStack

import concourse.bass as bass
from concourse import mybir

F32 = mybir.dt.float32
F32R = mybir.dt.float32r
ALU = mybir.AluOpType
ACT = mybir.ActivationFunctionType

P = 128
D_MODEL = 2048
KT = D_MODEL // P
SEQ = 256
DEC_B, DEC_T = 8, 4
NS = DEC_B * DEC_T
T = SEQ + NS
CH = 128
NC = SEQ // CH
CONV_W = 4
PRE = CONV_W - 1
EPS = 1e-6
DEPTH = 2
PLE_K = 256 // P

GH = 16
GV = 2 * GH
SG, SH = 8, 64
HPG = SH // SG
SX = HPG // 2
HD = 64

UP, UC, US = PRE, PRE + SEQ, PRE + SEQ + PRE * DEC_B
UW = US + NS
CW = PRE + PRE * DEC_B
PC_G = 4 * (PRE * DEC_B + CONV_W)
PC_S = 6 * (PRE * DEC_B + CONV_W + 1) + 2 * SX

OFF = [0, 32, 56, 72]
LEN = [32, 24, 16, 8]
NPAIR = 80

T_GPRO = 0
T_GLOOP = T_GPRO + 6
T_GEND = T_GLOOP + 6 * (GH - 1)
T_O1 = T_GEND + 2
T_P1 = T_O1 + 32
T_E1 = T_P1 + 2
T_SPRO = T_E1 + 16
T_SLOOP = T_SPRO + 7
T_SEND = T_SLOOP + 10 * (SG - 1)
T_O2 = T_SEND + 4
T_P2 = T_O2 + 32
T_E2 = T_P2 + 2
N_TILES = T_E2 + 16
N_HALF = 2 * N_TILES
N_ROUND, N_REST = N_HALF // 4, N_HALF % 4

C_NORM, C_PLE, C_FINAL, C_GNORM = 0, 32, 64, 80
C_GDT, C_GA, C_SDT, C_SA = 81, 82, 83, 84
N_PRM = 85
G_DVE_LINKS, S_DVE_LINKS = 34, 27
ARENA = 15900
K_ID, K_ONE, K_INC, K_M1, K_LEV = 0, 1, 2, 3, 4
K_BM = 10
N_CST = 11


def bc(ap, axis, n):
    a = ap.unsqueeze(axis)
    shape = list(a.shape)
    shape[axis] = n
    return a.to_broadcast(shape)


class Order:

    def __init__(self, eng, sem):
        self.eng, self.sem, self.base, self.n, self.m, self.per = eng, sem, 0, 0, 0, 0

    def enter(self, m, per):
        assert self.n == 0 or self.per == 0
        self.base, self.n, self.m, self.per = self.base + self.n, 0, m, per

    def leave(self, times):
        assert self.n == self.per, (self.n, self.per)
        self.base, self.n, self.m, self.per = self.base + self.per * times, 0, 0, 0

    def link(self, ins):
        self.n += 1
        ins.then_inc(self.sem, 1)
        self.eng.wait_ge(self.sem, self.m * self.per + (self.base + self.n))


def build(nc, weights, x_in, p_in, prm_in, cst_in, gpack, spack, gstate, sstate,
          y_out, gconv_out, sconv_out, gst_p, gst_s, sst_p, sst_s,
          g_rows, s_rows, h_spill, G_DVE, G_ACT, S_DVE, S_ACT):
    with ExitStack() as ctx:
        def sb(name, shape, dt=F32):
            return ctx.enter_context(nc.sbuf_tensor(name, shape, dt))

        def sem(name):
            return ctx.enter_context(nc.semaphore(name))

        ring = sb("ring", [P, 4, 8, P])
        wh = sb("wh", [P, 4, 8, P], F32R)
        wl = sb("wl", [P, 4, 8, P], F32R)
        xh = sb("xh", [P, KT, T], F32R)
        xl = sb("xl", [P, KT, T], F32R)
        Y = sb("Y", [P, 2 * KT, T])
        h = sb("h", [P, KT, T])
        cst = sb("cst", [P, N_CST, P])
        prm = sb("prm", [P, N_PRM])
        small = sb("small", [P, 16])
        ccol = sb("ccol", [P, 6 * SH])
        arena = sb("arena", [P, ARENA])

        psj = [ctx.enter_context(nc.psum_tensor(f"psj{i}", [P, 512], F32)) for i in range(2)]
        psA, psB, psC, psD, psE, psF = (
            ctx.enter_context(nc.psum_tensor(f"ps{c}", [P, 512], F32)) for c in "ABCDEF")

        def carve(sizes):
            out, at = {}, 0
            for name, n in sizes:
                out[name] = arena[:, at:at + n]
                at += n
            assert at <= ARENA, at
            return out

        ident, ones = cst[:, K_ID, :], cst[:, K_ONE, :]
        bmask = cst[0:NS, K_BM, 0:DEC_B]
        eps_c = small[:, 0:1]

        ga = carve([("U", 4 * UW), ("CR", 4 * T), ("KN", 2 * T), ("R", 2 * 3 * T), ("SQ", 2 * T), ("RS", 2 * T),
                    ("SQO", 2 * T), ("RSO", 2 * T),
                    ("pc", PC_G), ("co", 4 * CW), ("cc", 16), ("PR", 2 * NPAIR), ("DEC", 2 * NPAIR),
                    ("CQ", 2 * NPAIR), ("CK", 2 * NPAIR), ("W", 64), ("WD", 64), ("TM", 64), ("BE", 64),
                    ("DT", 512), ("AT", 512), ("DE", 1024), ("PP", 512), ("QK", 512), ("VB", 512),
                    ("VN", 512), ("VND", 512), ("KTK", 256), ("S1", 256), ("S2", 256), ("QD", 256),
                    ("O", 2 * T), ("ZS", 2 * T), ("WT", 256)])
        gU = ga["U"].rearrange("p (i u) -> p i u", i=4)
        gCR = ga["CR"].rearrange("p (i t) -> p i t", i=4)
        gKN = ga["KN"].rearrange("p (i t) -> p i t", i=2)
        gR = ga["R"].rearrange("p (j k t) -> p j k t", j=2, k=3)
        gSQ = ga["SQ"].rearrange("p (i t) -> p i t", i=2)
        gSQO = ga["SQO"].rearrange("p (i t) -> p i t", i=2)
        gRS = ga["RS"].rearrange("p (i t) -> p i t", i=2)
        gRSO = ga["RSO"].rearrange("p (i t) -> p i t", i=2)
        gpc = ga["pc"].rearrange("p (h c) -> p h c", h=2)
        gpc_cache = [gpc[:, n, 0:48].rearrange("p (i c) -> p i c", i=2) for n in range(2)]
        gpc_tap = [gpc[:, n, 48:56].rearrange("p (i c) -> p i c", i=2) for n in range(2)]
        gco = ga["co"].rearrange("p (i c) -> p i c", i=4)
        gcc = ga["cc"].rearrange("p (k c j) -> p k c j", k=4, c=NC)
        gPR, gDEC, gCQ, gCK = (ga[n].rearrange("p (i c) -> p i c", i=2) for n in ("PR", "DEC", "CQ", "CK"))
        gW, gWD, gTM, gBE = (ga[n].rearrange("p (i c) -> p i c", i=2) for n in ("W", "WD", "TM", "BE"))
        gDT, gAT, gP, gQK, gVB, gVN, gVND = (
            ga[n].rearrange("p (u t) -> p u t", u=4) for n in ("DT", "AT", "PP", "QK", "VB", "VN", "VND"))
        gDE = ga["DE"].rearrange("p (c k j t) -> p c k j t", c=NC, k=2, j=2)
        gKT = ga["KTK"].rearrange("p (c t) -> p c t", c=NC)
        gS1 = ga["S1"].rearrange("p (j t) -> p j t", j=2)
        gS2 = ga["S2"].rearrange("p (j t) -> p j t", j=2)
        gQD = ga["QD"].rearrange("p (j t) -> p j t", j=2)
        gO = ga["O"].rearrange("p (j t) -> p j t", j=2)
        gZS = ga["ZS"].rearrange("p (j t) -> p j t", j=2)
        gWT = ga["WT"]
        hf = h[:, :, :].rearrange("p k t -> p (k t)")
        gS = hf[:, 0:2048].rearrange("p (b j e) -> p b j e", b=DEC_B, j=2)
        gKM = hf[0:NS, 2048:3072].rearrange("p (b d) -> p b d", b=DEC_B)
        HRG = arena[:, ARENA - 9 * T:ARENA].rearrange("p (k t) -> p k t", k=9)

        sa = carve([("U", 6 * UW), ("CV", 6 * T), ("R2", HPG * T), ("RP", SX * 224), ("pc", PC_S),
                    ("co", 6 * CW), ("cc", 6 * HPG), ("PR", NPAIR), ("DEC", SX * NPAIR), ("DT", 1024),
                    ("X", 1024), ("XD", 512), ("CB", 256), ("BT", 256), ("XS", 128), ("XE", 128), ("TM", 128),
                    ("XT", 512), ("YT", SX * T), ("ZS", SX * T), ("EG", 80), ("BM", 1024), ("RT", T)])
        sU = sa["U"].rearrange("p (i u) -> p i u", i=6)
        sCV = sa["CV"].rearrange("p (i t) -> p i t", i=6)
        sR2 = sa["R2"].rearrange("p (h t) -> p h t", h=HPG)
        sRP = sa["RP"].rearrange("p (i c) -> p i c", i=SX)
        spc = sa["pc"][:, 0:6 * 29].rearrange("p (i c) -> p i c", i=6)
        spc_norm, spc_D = sa["pc"][:, 174:178], sa["pc"][:, 178:182]
        sco = sa["co"].rearrange("p (i c) -> p i c", i=6)
        scc = sa["cc"].rearrange("p (k c j) -> p k c j", k=3, c=NC)
        sPR = sa["PR"]
        sDEC = sa["DEC"].rearrange("p (i c) -> p i c", i=SX)
        sDT = sa["DT"].rearrange("p (h t) -> p h t", h=HPG)
        sX = sa["X"].rearrange("p (c h d) -> p c h d", c=NC, h=HPG)
        sXD = sa["XD"].rearrange("p (h d) -> p h d", h=HPG)
        sCB = sa["CB"].rearrange("p (c t) -> p c t", c=NC)
        sBT = sa["BT"].rearrange("p (c t) -> p c t", c=NC)
        sXS, sXE, sTM = (sa[n].rearrange("p (i t) -> p i t", i=SX) for n in ("XS", "XE", "TM"))
        sXT = sa["XT"]
        sYT = sa["YT"].rearrange("p (i t) -> p i t", i=SX)
        sZS = sa["ZS"].rearrange("p (i t) -> p i t", i=SX)
        sEGc = sa["EG"][:, 0:8]
        sEGb = sa["EG"][:, 8:72].rearrange("p (h b) -> p h b", h=HPG)
        sS = hf[:, 0:4096].rearrange("p (b h d) -> p b h d", b=DEC_B, h=HPG)
        sS1 = hf[:, 4096:4608]
        sBMv = sa["BM"][0:NS, :].rearrange("p (b n) -> p b n", b=DEC_B)
        sTMr = sa["RT"]

        da = carve([("SQ", 2 * T), ("SGM", 2 * T), ("TM", 2 * T), ("RSTD", T), ("RSE", T), ("pT", 2 * T)])
        dSQ, dSG, dTM = (da[n].rearrange("p (i t) -> p i t", i=2) for n in ("SQ", "SGM", "TM"))
        dRS, dRE = da["RSTD"], da["RSE"]
        dp = da["pT"].rearrange("p (k t) -> p k t", k=PLE_K)
        eb = Y[:, 0:KT, :]

        w_in = [sem(f"w_in{i}") for i in range(4)]
        wh_ready = sem("wh_ready")
        wl_ready = sem("wl_ready")
        half_done = sem("half_done")
        took_act = sem("took_act")
        took_dve = sem("took_dve")
        xh_ready = sem("xh_ready")
        xl_ready = sem("xl_ready")
        dve_order, act_order = sem("dve_order"), sem("act_order")
        c_in = sem("c_in")
        sems = {}

        def S(name):
            if name not in sems:
                sems[name] = sem(name)
            return sems[name]

        X0 = {"g": 0, "oa1": 16, "ob1": 32, "p1": 48, "e1": 50, "s": 66, "oa2": 82, "ob2": 98, "p2": 114, "e2": 116}
        TA_G = 0
        TA_E1 = T_GEND + 2
        TA_S = TA_E1 + 16
        TA_E2 = TA_S + (T_SEND + 4 - T_SPRO)
        TD_O1, TD_P1, TD_O2, TD_P2 = 0, 32, 48, 80

        block = ctx.enter_context(nc.Block())

        @block.sync
        def _(sp):
            sp.dma_start(h[:, :, :], x_in).then_inc(S("x_in"), 16)
            sp.dma_start(cst[:, :, :], cst_in).then_inc(c_in, 16)
            sp.dma_start(prm[:, :], prm_in).then_inc(S("prm_in"), 16)
            for s in range(4):
                sp.dma_start(ring[:, s], weights[s]).then_inc(w_in[s], 16)

            def refill(r, s):
                sp.wait_ge(wl_ready, r * 4 + (s - 3))
                sp.dma_start(ring[:, s], weights[r * 4 + s]).then_inc(w_in[s], 16)

            with sp.Fori(1, N_ROUND) as r:
                for s in range(4):
                    refill(r, s)
            for s in range(N_REST):
                refill(N_ROUND, s)

        @block.gpsimd
        def _(pool):
            def lower(r, s):
                pool.wait_ge(wh_ready, r * 4 + (s + 1))
                pool.tensor_tensor(wl[:, s], ring[:, s], wh[:, s].bitcast(F32), ALU.subtract) \
                    .then_inc(wl_ready, 1)

            with pool.Fori(0, N_ROUND) as r:
                for s in range(4):
                    lower(r, s)
            for s in range(N_REST):
                lower(N_ROUND, s)

        @block.tensor
        def _(pe):
            def project(m, per, t0, e, fresh=None):
                hc = 2 * t0 + e // 4
                if e % 4 == 0:
                    pe.wait_ge(wl_ready, m * (2 * per) + (hc + 1))
                for kt in (2 * e, 2 * e + 1):
                    if fresh is not None:
                        pe.wait_ge(xl_ready, fresh + kt + 1)
                    w_h, w_l = wh[:, hc % 4, kt % 8, :], wl[:, hc % 4, kt % 8, :]
                    out = psj[t0 % 2][:, 0:T]
                    pe.matmul(out, w_h, xh[:, kt, :], start=(kt == 0), stop=False)
                    pe.matmul(out, w_h, xl[:, kt, :], start=False, stop=False)
                    mm = pe.matmul(out, w_l, xh[:, kt, :], start=False, stop=(kt == KT - 1))
                if e % 4 == 3:
                    mm.then_inc(half_done, 1)

            def col_sum(out, rhs, start=True, stop=True):
                return pe.matmul(out, ones, rhs, start=start, stop=stop)

            pe.wait_ge(c_in, 16)
            pe.wait_ge(S("prm_in"), 16)

            def norm_sum(n):
                for kt in range(KT):
                    pe.wait_ge(S("hsq"), n + kt + 1)
                    mm = col_sum(psA[:, 0:T], dSQ[:, kt % 2, :], start=(kt == 0), stop=(kt == KT - 1))
                    mm.then_inc(S("hss"), 1)

            def gdn_norm(m):
                pe.wait_ge(S("g_sq"), m + 1)
                col_sum(psE[:, 0:T], gSQ[:, 0, :])
                col_sum(psF[:, 0:T], gSQ[:, 1, :]).then_inc(S("g_ss"), 1)

            def gdn_mix(m, e, more):
                if e == 0:
                    pe.wait_ge(S("g_kn"), m + 1)
                    for c in range(NC):
                        k_c, q_c = (gKN[:, n, c * CH:(c + 1) * CH] for n in (1, 0))
                        pe.transpose(psA[:, c * P:(c + 1) * P], k_c, ident)
                        pe.matmul(psC[:, c * CH:(c + 1) * CH], k_c, k_c, start=True, stop=True)
                        pe.matmul(psC[:, 256 + c * CH:256 + (c + 1) * CH], k_c, q_c, start=True, stop=True)
                    pe.transpose(psE[0:NS, 0:P], gKN[:, 1, SEQ:T], ident).then_inc(S("g_tok"), 1)
                if e == 3:
                    pe.wait_ge(S("g_pr"), m + 1)
                    col_sum(psD[:, 0:2 * NPAIR], ga["PR"])
                    pe.wait_ge(S("g_st_in"), m * 16 + 16)
                    for b in range(DEC_B):
                        for j in range(2):
                            at = 160 + 16 * b + 8 * j
                            mm = pe.matmul(psD[:, at:at + 8], gS[:, b, j, :], gKN[:, 0:2, SEQ + b:T:DEC_B],
                                           start=True, stop=True)
                    mm.then_inc(S("g_smp"), 1)
                if e == 5:
                    pe.wait_ge(S("g_e1"), m + 1)
                    for c in range(NC):
                        for j in range(2):
                            mm = pe.transpose(psB[:, (2 * c + j) * P:(2 * c + j + 1) * P], gDE[:, c, 1, j, :], ident)
                    mm.then_inc(S("g_dt"), 1)

                def inv_p(c, lv):
                    if lv == 0:
                        pe.wait_ge(S("g_d"), m + 1)
                        pe.wait_ge(S("g_km"), m + 1)
                    else:
                        pe.wait_ge(S(f"g_de{c}"), m * 6 + lv)
                    for j in range(2):
                        mm = pe.matmul((psC, psE)[c][:, j * P:(j + 1) * P], gAT[:, 2 * c + j, :], gDE[:, c, 0, j, :],
                                       start=True, stop=True)
                    mm.then_inc(S(f"g_p{c}"), 1)

                def inv_q(c, lv):
                    pe.wait_ge(S(f"g_pm{c}"), m * 6 + lv + 1)
                    bank = (psA, psF)[c]
                    if lv < 5:
                        for j in range(2):
                            pe.matmul(bank[:, j * P:(j + 1) * P], gDE[:, c, 1, j, :], gP[:, 2 * c + j, :],
                                      start=True, stop=True)
                    for j in range(2):
                        mm = pe.matmul(bank[:, (2 + j) * P:(3 + j) * P], gP[:, 2 * c + j, :], gDE[:, c, 1, j, :],
                                       start=True, stop=True)
                    mm.then_inc(S(f"g_q{c}"), 1)

                for lv in range(6):
                    if e == 7 + 2 * lv:
                        if lv > 0:
                            inv_q(1, lv - 1)
                        inv_p(0, lv)
                    if e == 8 + 2 * lv:
                        inv_p(1, lv)
                        inv_q(0, lv)
                if e == 19:
                    inv_q(1, 5)
                    pe.wait_ge(S("g_cv"), m + 1)
                    for c in range(NC):
                        for j in range(2):
                            mm = pe.transpose(psB[:, (2 * c + j) * P:(2 * c + j + 1) * P],
                                              gCR[:, 2 + j, c * CH:(c + 1) * CH], ident)
                    mm.then_inc(S("g_tokv"), 1)

                def new_values(c):
                    for j in range(2):
                        mm = pe.matmul(psC[:, j * P:(j + 1) * P], gDE[:, c, 1, j, :], gVB[:, 2 * c + j, :],
                                       start=True, stop=True)
                    mm.then_inc(S("g_vn"), 1)

                if e == 22:
                    pe.wait_ge(S("g_de0"), m * 6 + 6)
                    pe.wait_ge(S("g_vb"), m + 1)
                    new_values(0)
                if e == 24:
                    pe.wait_ge(S("g_vnd"), m * 2 + 1)
                    pe.wait_ge(S("g_de1"), m * 6 + 6)
                    pe.matmul(psE[:, 0:2 * P], gKT[:, 0, :], ga["VND"][:, 0:2 * P], start=True, stop=True) \
                        .then_inc(S("g_s"), 1)
                    for j in range(2):
                        pe.matmul(psF[:, j * SEQ:j * SEQ + CH], gVN[:, j, :], gQK[:, j, :], start=True, stop=True)
                if e == 26:
                    pe.wait_ge(S("g_s1"), m + 1)
                    pe.wait_ge(S("g_wd"), m + 1)
                    pe.matmul(psD[:, 0:2 * P], gKN[:, 1, CH:2 * CH], ga["S1"], start=True, stop=True) \
                        .then_inc(S("g_ks"), 1)
                    for j in range(2):
                        mm = pe.transpose(psB[0:NS, j * P:(j + 1) * P], gWD[:, j, :], ident)
                    mm.then_inc(S("g_wt"), 1)
                if e == 28:
                    pe.wait_ge(S("g_rhs"), m + 1)
                    new_values(1)
                if e == 30:
                    pe.wait_ge(S("g_vnd"), m * 2 + 2)
                    pe.matmul(psE[:, 0:2 * P], gKT[:, 1, :], ga["VND"][:, 2 * P:4 * P], start=True, stop=True) \
                        .then_inc(S("g_s"), 1)
                    for j in range(2):
                        o = psF[:, j * SEQ + CH:(j + 1) * SEQ]
                        pe.matmul(o, gS1[:, j, :], gQD[:, j, :], start=True, stop=False)
                        mm = pe.matmul(o, gVN[:, 2 + j, :], gQK[:, 2 + j, :], start=False, stop=True)
                    mm.then_inc(S("g_o"), 1)
                for i in range(4):
                    if e == 31 + i:
                        if i == 0:
                            pe.wait_ge(S("g_wtc"), m + 1)
                        if i >= 2:
                            pe.wait_ge(S("g_su"), m * 4 + i - 1)
                        bank = (psA, psB)[i % 2]
                        for b in (2 * i, 2 * i + 1):
                            at = (b % 2) * 256
                            mm = pe.matmul(bank[:, at:at + 256], gKM[:, b, :], gWT[0:NS, :], start=True, stop=True)
                        mm.then_inc(S("g_sp"), 1)
                if e == 35:
                    pe.wait_ge(S("g_osq"), m + 1)
                    col_sum(psC[:, 0:T], gSQO[:, 0, :])
                    col_sum(psD[:, 0:T], gSQO[:, 1, :]).then_inc(S("g_os"), 1)
                if e == 38 and more:
                    pe.wait_ge(S("g_s2"), m + 1)
                    gdn_norm(m + 1)

            def bank_wait_act(m, per, t0, phase_t, took0):
                pe.wait_ge(took_act, m * per + (took0 + t0 - phase_t - 1))

            norm_sum(0)
            for k in range(6):
                if k >= 2:
                    bank_wait_act(0, 0, T_GPRO + k, T_GPRO, TA_G)
                for e in range(8):
                    project(0, 0, T_GPRO + k, e, fresh=X0["g"] if k == 0 else None)
                if k == 2:
                    pe.wait_ge(S("g_hrows"), 1)
                    for n in range(4):
                        for c in range(NC):
                            src = HRG[0:GV, (7, 3, 4, 5)[n], c * CH:(c + 1) * CH]
                            at = (n * NC + c) * GV
                            mm = pe.transpose(psA[:, at:at + GV], src, ident[0:GV, 0:GV])
                    mm.then_inc(S("g_ccol"), 1)

            gdn_norm(0)
            with pe.Fori(0, GH - 1) as m:
                for e in range(48):
                    if e % 8 == 0:
                        bank_wait_act(m, 6, T_GLOOP + e // 8, T_GPRO, TA_G)
                    project(m, 6, T_GLOOP + e // 8, e % 8)
                    gdn_mix(m, e, True)
            for e in range(48):
                if 4 <= e < 20:
                    if e % 8 == 4:
                        bank_wait_act(0, 0, T_GEND + (e - 4) // 8, T_GPRO, TA_G)
                    project(0, 0, T_GEND + (e - 4) // 8, (e - 4) % 8)
                gdn_mix(GH - 1, e, False)

            def dense(t0, x0, first_free, sem_took, took0, last=None):
                for k in range(2):
                    first_free(k)
                    for e in range(8):
                        project(0, 0, t0 + k, e, fresh=x0 if k == 0 else None)
                with pe.Fori(1, KT // 2) as i:
                    for k in range(2):
                        pe.wait_ge(sem_took, i * 2 + (took0 + k - 1))
                        for e in range(8):
                            project(i, 2, t0 + k, e)
                        if last is not None:
                            last(i, k)

            def out_proj(t0, xa, xb, td, ta):
                dense(t0, xa, lambda k: pe.wait_ge(took_act, ta), took_dve, td)
                dense(t0 + 16, xb, lambda k: pe.wait_ge(took_dve, td + 15 + k), took_dve, td + 16)

            def ple(tp, te, xp, xe, td, ta, hs, es, hq):
                for i in range(KT):
                    a, hc = i // 8, 2 * (tp + i // 8) + (i % 8) // 4
                    if i % 4 == 0:
                        pe.wait_ge(wl_ready, hc + 1)
                    pe.wait_ge(took_dve, td + i - 1)
                    out = psj[(tp + i) % 2][:, 0:T]
                    for kt in range(PLE_K):
                        if i == 0:
                            pe.wait_ge(xl_ready, xp + kt + 1)
                        at = (2 * i + kt) % 8
                        pe.matmul(out, wh[:, hc % 4, at, :], xh[:, kt, :], start=(kt == 0), stop=False)
                        pe.matmul(out, wh[:, hc % 4, at, :], xl[:, kt, :], start=False, stop=False)
                        mm = pe.matmul(out, wl[:, hc % 4, at, :], xh[:, kt, :], start=False, stop=(kt == PLE_K - 1))
                    if i % 4 != 3:
                        mm.then_inc(S("e_done"), 1)
                    else:
                        mm.then_inc(half_done, 1)
                    if i >= 1:
                        pe.wait_ge(S("esq"), es + i)
                        col_sum(psB[:, 0:T], dSQ[:, (i - 1) % 2, :], start=(i == 1), stop=False) \
                            .then_inc(S("ess"), 1)
                pe.wait_ge(S("esq"), es + KT)
                col_sum(psB[:, 0:T], dSQ[:, (KT - 1) % 2, :], start=False, stop=True).then_inc(S("ess"), 1)

                def add_sum(i, k):
                    pe.wait_ge(S("hsq"), i * 2 + (hq + k - 1))
                    col_sum(psA[:, 0:T], dSQ[:, k, :], start=False, stop=False).then_inc(S("hss"), 1)

                for k in range(2):
                    pe.wait_ge(took_dve, td + KT)
                    for e in range(8):
                        project(0, 0, te + k, e, fresh=xe if k == 0 else None)
                for k in range(2, 4):
                    pe.wait_ge(took_act, ta + k - 1)
                    for e in range(8):
                        project(0, 0, te + k, e)
                    pe.wait_ge(S("hsq"), hq + k - 1)
                    col_sum(psA[:, 0:T], dSQ[:, k % 2, :], start=(k == 2), stop=False).then_inc(S("hss"), 1)
                with pe.Fori(2, KT // 2) as i:
                    for k in range(2):
                        pe.wait_ge(took_act, i * 2 + (ta + k - 1))
                        for e in range(8):
                            project(i, 2, te + k, e)
                        add_sum(i, k)
                for k in range(2):
                    pe.wait_ge(S("hsq"), hq + 15 + k)
                    col_sum(psA[:, 0:T], dSQ[:, k, :], start=False, stop=(k == 1)).then_inc(S("hss"), 1)

            out_proj(T_O1, X0["oa1"], X0["ob1"], TD_O1, TA_E1)
            ple(T_P1, T_E1, X0["p1"], X0["e1"], TD_P1, TA_E1, 16, 0, 16)

            def ssd_mix(m, e):
                if e == 17:
                    pe.wait_ge(S("s_cv"), m + 1)
                    pe.wait_ge(S("s_yd"), m + 1)
                    for c in range(NC):
                        pe.transpose(psA[:, c * P:(c + 1) * P], sCV[:, 0, c * CH:(c + 1) * CH], ident)
                        bank = (psB, psC)[c]
                        for i in range(SX):
                            pe.transpose(bank[:, i * P:(i + 1) * P], sCV[:, 2 + i, c * CH:(c + 1) * CH], ident)
                        pe.matmul(psD[:, c * CH:(c + 1) * CH], sCV[:, 0, c * CH:(c + 1) * CH],
                                  sCV[:, 1, c * CH:(c + 1) * CH], start=True, stop=True)
                    pe.transpose(psE[0:NS, 0:P], sCV[:, 0, SEQ:T], ident).then_inc(S("s_tok"), 1)
                if e == 20:
                    pe.wait_ge(S("s_pr"), m + 1)
                    col_sum(psF[:, 0:NPAIR], sPR)
                    pe.wait_ge(S("s_st_in"), m * 16 + 16)
                    for b in range(DEC_B):
                        for i in range(SX):
                            at = P + (i * DEC_B + b) * DEC_T
                            mm = pe.matmul(psF[:, at:at + DEC_T], sS[:, b, 2 * i:2 * i + 2, :],
                                           sCV[:, 1, SEQ + b:T:DEC_B], start=True, stop=True)
                    mm.then_inc(S("s_smp"), 1)
                if e == 24:
                    pe.wait_ge(S("s_xd"), m * 2 + 1)
                    pe.wait_ge(S("s_btc"), m + 1)
                    pe.matmul(psA[:, :], sBT[:, 0, :], sa["XD"], start=True, stop=True).then_inc(S("s_s"), 1)
                for c in range(NC):
                    if e == (28, 36)[c]:
                        pe.wait_ge(S("s_w"), m * 2 + c + 1)
                        for i in range(SX):
                            for j in range(2):
                                mm = pe.matmul((psB, psC)[c][HD * j:HD * j + HD, i * P:(i + 1) * P],
                                               sX[:, c, 2 * i + j, :], sDT[:, 2 * i + j, :], start=True, stop=True)
                        mm.then_inc(S("s_y"), 1)
                if e == 32:
                    pe.wait_ge(S("s_s1"), m + 1)
                    for i in range(SX):
                        mm = pe.matmul(psD[:, i * P:(i + 1) * P], sS1[:, i * P:(i + 1) * P],
                                       sCV[:, 1, CH:2 * CH], start=True, stop=True)
                    mm.then_inc(S("s_off"), 1)
                    pe.wait_ge(S("s_xd"), m * 2 + 2)
                    pe.matmul(psA[:, :], sBT[:, 1, :], sa["XD"], start=True, stop=True).then_inc(S("s_s"), 1)
                if e == 40:
                    pe.wait_ge(S("s_xe"), m + 1)
                    for i in range(SX):
                        mm = pe.transpose(psE[0:NS, i * P:(i + 1) * P], sXE[:, i, :], ident)
                    mm.then_inc(S("s_xt"), 1)
                for b in range(DEC_B):
                    if e == 44 + 2 * b:
                        if b == 0:
                            pe.wait_ge(S("s_xtc"), m + 1)
                            pe.wait_ge(S("s_yt"), m + 1)
                        if b >= 2:
                            pe.wait_ge(S("s_su"), m * 8 + b - 1)
                        pe.matmul((psA, psF)[b % 2][:, :], sBMv[:, b, :], sXT[0:NS, :], start=True, stop=True) \
                            .then_inc(S("s_sp"), 1)
                if e == 72:
                    pe.wait_ge(S("s_sq"), m + 1)
                    for i in range(SX):
                        mm = col_sum(psE[:, 0:T], sZS[:, i, :], start=(i == 0), stop=(i == SX - 1))
                    mm.then_inc(S("s_ss"), 1)

            for k in range(7):
                bank_wait_act(0, 0, max(T_SPRO + k, T_SPRO + 1), T_SPRO, TA_S)
                for e in range(8):
                    project(0, 0, T_SPRO + k, e, fresh=X0["s"] if k == 0 else None)
                if k == 2:
                    pe.wait_ge(S("s_hrows"), 1)
                    for n in range(3):
                        for c in range(NC):
                            src = HRG[0:SH, (4, 3, 5)[n], c * CH:(c + 1) * CH]
                            at = (n * NC + c) * SH
                            mm = pe.transpose(psA[:, at:at + SH], src, ident[0:SH, 0:SH])
                    mm.then_inc(S("s_ccol"), 1)
            with pe.Fori(0, SG - 1) as m:
                for e in range(80):
                    if e % 8 == 0:
                        bank_wait_act(m, 10, T_SLOOP + e // 8, T_SPRO, TA_S)
                    project(m, 10, T_SLOOP + e // 8, e % 8)
                    ssd_mix(m, e)
            for e in range(80):
                if 32 <= e < 64:
                    if e % 8 == 0:
                        bank_wait_act(0, 0, T_SEND + (e - 32) // 8, T_SPRO, TA_S)
                    project(0, 0, T_SEND + (e - 32) // 8, e % 8)
                ssd_mix(SG - 1, e)

            out_proj(T_O2, X0["oa2"], X0["ob2"], TD_O2, TA_E2)
            ple(T_P2, T_E2, X0["p2"], X0["e2"], TD_P2, TA_E2, 32, 16, 32)

        @block.scalar
        def _(act):
            ao = Order(act, act_order)

            def upper(m, per, hc):
                act.wait_ge(w_in[hc % 4], m * (4 * per) + 16 * (hc // 4 + 1))
                if hc >= 4:
                    act.wait_ge(half_done, m * per + (hc - 3))
                act.activation(wh[:, hc % 4], ring[:, hc % 4], ACT.Copy).then_inc(wh_ready, 1)

            def ahead(m, per, t):
                upper(m, 2 * per, 2 * t)
                upper(m, 2 * per, 2 * t + 1)

            def tile_wait(m, per, t):
                act.wait_ge(half_done, m * (2 * per) + 2 * t + 2)

            def split_x(src, n, t0):
                if t0:
                    act.wait_ge(half_done, 2 * t0)
                for kt in range(n):
                    act.activation(xh[:, kt, :], src(kt), ACT.Copy).then_inc(xh_ready, 1)

            def normed_x(base, t0):
                act.wait_ge(S("hss"), base + KT)
                act.activation(dRS, psA[:, 0:T], ACT.Sqrt, bias=eps_c, scale=1.0 / D_MODEL) \
                    .then_inc(S("n_root"), 1)
                if t0:
                    act.wait_ge(half_done, 2 * t0)
                n0 = base
                for kt in range(KT):
                    act.wait_ge(S("xn"), n0 + kt + 1)
                    act.activation(xh[:, kt, :], dTM[:, kt % 2, :], ACT.Copy).then_inc(xh_ready, 1)

            def softplus_rows(n, dtc, ac, tile_t, pre, took):
                tile_wait(0, 0, tile_t)
                act.activation(HRG[0:n, 0, :], psj[tile_t % 2][0:n, 0:T], ACT.Identity,
                               bias=prm[0:n, dtc:dtc + 1]).then_inc(took_act, 1)
                act.wait_ge(took_act, took + 1)
                ao.link(act.activation(HRG[0:n, 1, :], HRG[0:n, 0, :], ACT.Abs))
                act.activation(small[0:n, 2:3], prm[0:n, ac:ac + 1], ACT.Exp)
                act.activation(HRG[0:n, 1, :], HRG[0:n, 1, :], ACT.Exp, scale=-1.0).then_inc(S(pre + "exp"), 1)
                act.wait_ge(S(pre + "w1"), 1)
                act.activation(HRG[0:n, 3, :], HRG[0:n, 2, :], ACT.Ln).then_inc(S(pre + "ln"), 1)
                act.wait_ge(S(pre + "cum"), 1)
                act.activation(HRG[0:n, 8, :], HRG[0:n, 6, :], ACT.Exp)
                act.activation(HRG[0:n, 5, 0:SEQ], HRG[0:n, 1, 0:SEQ], ACT.Exp).then_inc(S(pre + "eg"), 1)

            act.wait_ge(S("x_in"), 16)
            act.wait_ge(S("prm_in"), 16)
            act.wait_ge(S("konst"), 1)
            for kt in range(KT):
                if kt >= 2:
                    act.wait_ge(S("hss"), kt - 1)
                act.activation(dSQ[:, kt % 2, :], h[:, kt, :], ACT.Square).then_inc(S("hsq"), 1)
            ahead(0, 0, 0)
            ahead(0, 0, 1)
            normed_x(0, 0)
            act.dma_start(h_spill, h[:, :, :]).then_inc(S("spill"), 16)

            def take_u(i, U):
                return lambda bank: (act.activation(U[:, i, UP:UC], bank[:, 0:SEQ], ACT.Copy),
                                     act.activation(U[:, i, US:UW], bank[:, SEQ:T], ACT.Copy))[1]

            def g_load(m):
                act.dma_start(ga["R"], g_rows[m].partition_broadcast(P)).then_inc(S("g_r_in"), 16)
                act.dma_start(gpc[:, 1, :], gpack[m, 1]).then_inc(S("g_pv_in"), 16)
                act.dma_start(hf[:, 0:2048], gstate[m]).then_inc(S("g_st_in"), 16)

            def g_load_qk(m):
                act.dma_start(gpc[:, 0, :], gpack[m, 0]).then_inc(S("g_pq_in"), 16)

            def g_qk_silu(m):
                act.wait_ge(S("g_convq"), m + 1)
                act.dma_start(gconv_out[m, 0], gco[:, 0:2, :]).then_inc(S("g_cq_out"), 16)
                act.activation(gCR[:, 0:2, :], gCR[:, 0:2, :], ACT.Silu).then_inc(S("g_qk"), 1)
                act.wait_ge(S("g_qk"), m + 1)
                act.activation(gSQ[:, :, :], gCR[:, 0:2, :], ACT.Square).then_inc(S("g_sq"), 1)

            def g_qk_roots(m):
                act.wait_ge(S("g_ss"), m + 1)
                g_roots(gRS, psE, psF, 1.0).then_inc(S("g_rs"), 1)

            def g_roots(dst, bank0, bank1, scale):
                act.activation(dst[:, 1, :], bank1[:, 0:T], ACT.Sqrt, bias=eps_c, scale=scale)
                return act.activation(dst[:, 0, :], bank0[:, 0:T], ACT.Sqrt, bias=eps_c, scale=scale)

            softplus_rows(GV, C_GDT, C_GA, 0, "g_", TA_G)
            ahead(0, 0, 2)
            tile_wait(0, 0, 1)
            act.activation(HRG[0:GV, 7, :], psj[1][0:GV, 0:T], ACT.Sigmoid).then_inc(took_act, 1)
            ahead(0, 0, 3)
            act.wait_ge(S("g_hrows"), 1)
            act.dma_start(g_rows.rearrange("m (j c) -> (m j) c", j=2), HRG[0:GV, 6:9, :]) \
                .then_inc(S("g_rows_out"), 16)
            g_load_qk(0)
            act.wait_ge(S("zero_u"), 1)
            tile_wait(0, 0, 2)
            take_u(0, gU)(psj[0]).then_inc(took_act, 1)
            ahead(0, 0, 4)
            act.wait_ge(S("g_ccol"), 1)
            act.activation(ccol[:, 0:256], psA[:, 0:256], ACT.Copy).then_inc(S("g_ccolc"), 1)
            tile_wait(0, 0, 3)
            take_u(1, gU)(psj[1]).then_inc(took_act, 1)
            ahead(0, 0, 5)
            act.wait_ge(S("g_rows_out"), 16)
            act.wait_ge(S("spill"), 16)
            g_load(0)
            tile_wait(0, 0, 4)
            take_u(2, gU)(psj[0]).then_inc(took_act, 1)
            ahead(0, 0, 6)
            g_qk_silu(0)
            tile_wait(0, 0, 5)
            take_u(3, gU)(psj[1]).then_inc(took_act, 1)
            ahead(0, 0, 7)
            g_qk_roots(0)

            def gdn_body(m, full):
                per = 6 if full else 0
                zt = T_GLOOP + 2 if full else T_GEND

                def take_z(j):
                    tile_wait(m if full else 0, per, zt + j)
                    act.activation(gZS[:, j, :], psj[(zt + j) % 2][:, 0:T], ACT.Silu).then_inc(took_act, 1)

                if full:
                    act.wait_ge(S("g_cq_out"), m * 16 + 16)
                    g_load_qk(m + 1)
                act.wait_ge(S("g_dtx"), m + 1)
                act.activation(ga["DT"], ga["DT"], ACT.Exp)
                act.activation(ga["DEC"], ga["DEC"], ACT.Exp).then_inc(S("g_dte"), 1)
                act.wait_ge(S("g_tok"), m + 1)
                act.activation(ga["KTK"], psA[:, 0:2 * P], ACT.Copy)
                if full:
                    tile_wait(m, per, T_GLOOP)
                    take_u(0, gU)(psj[T_GLOOP % 2]).then_inc(took_act, 1)
                    ahead(m, per, T_GLOOP + 2)
                act.wait_ge(S("g_dt"), m + 1)
                act.activation(gDE[:, :, 0, :, :], psB[:, :].rearrange("p (c j t) -> p c j t", c=NC, j=2), ACT.Copy) \
                    .then_inc(S("g_d"), 1)
                if full:
                    tile_wait(m, per, T_GLOOP + 1)
                    take_u(1, gU)(psj[(T_GLOOP + 1) % 2]).then_inc(took_act, 1)
                    ahead(m, per, T_GLOOP + 3)
                else:
                    take_z(0)
                    ahead(0, 0, T_O1)
                act.wait_ge(S("g_convv"), m + 1)
                act.dma_start(gconv_out[m, 1], gco[:, 2:4, :]).then_inc(S("g_cv_out"), 16)
                act.activation(gCR[:, 2:4, :], gCR[:, 2:4, :], ACT.Silu).then_inc(S("g_cv"), 1)
                act.wait_ge(S("g_tokv"), m + 1)
                for c in range(NC):
                    for j in range(2):
                        u = 2 * c + j
                        ins = act.activation(gVB[:, u, :], psB[:, u * P:(u + 1) * P], ACT.Copy,
                                             scale=gcc[:, 0, c, j:j + 1])
                ins.then_inc(S("g_vb"), 1)

                def values(c):
                    act.wait_ge(S("g_vn"), m * 2 + c + 1)
                    act.activation(gVN[:, 2 * c:2 * c + 2, :], psC[:, 0:2 * P].rearrange("p (j t) -> p j t", j=2),
                                   ACT.Copy)
                    for j in range(2):
                        ins = act.activation(gVND[:, 2 * c + j, :], psC[:, j * P:(j + 1) * P], ACT.Copy,
                                             scale=gcc[:, 3, c, j:j + 1])
                    ins.then_inc(S("g_vnd"), 1)

                if full:
                    take_z(0)
                    ahead(m, per, T_GLOOP + 4)
                else:
                    take_z(1)
                values(0)
                act.wait_ge(S("g_s"), m * 2 + 1)
                act.activation(ga["S1"], psE[:, 0:2 * P], ACT.Copy).then_inc(S("g_s1"), 1)
                act.wait_ge(S("g_wt"), m + 1)
                act.activation(gWT[0:NS, :], psB[0:NS, 0:2 * P], ACT.Copy).then_inc(S("g_wtc"), 1)
                values(1)
                act.wait_ge(S("g_o"), m + 1)
                ao.link(act.activation(gO[:, :, 0:SEQ], psF[:, :].rearrange("p (j t) -> p j t", j=2), ACT.Copy))
                act.wait_ge(S("g_os_dve"), m + 1)
                act.activation(ga["SQO"], ga["O"], ACT.Square).then_inc(S("g_osq"), 1)
                if full:
                    take_z(1)
                    ahead(m, per, T_GLOOP + 5)
                    g_qk_silu(m + 1)
                act.wait_ge(S("g_os"), m + 1)
                g_roots(gRSO, psC, psD, 1.0 / P).then_inc(S("g_rs2"), 1)
                act.wait_ge(S("g_s2"), m + 1)
                act.dma_start(gst_p[m], ga["S2"]).then_inc(S("g_sp_out"), 16)
                act.wait_ge(S("g_su"), m * 4 + 4)
                act.dma_start(gst_s[m], hf[:, 0:2048]).then_inc(S("g_st_out"), 16)
                if full:
                    g_qk_roots(m + 1)
                    tile_wait(m, per, T_GLOOP + 4)
                    take_u(2, gU)(psj[T_GLOOP % 2]).then_inc(took_act, 1)
                    ahead(m, per, T_GLOOP + 6)
                act.wait_ge(S("g_y"), m + 2)
                act.wait_ge(S("g_st_out"), m * 16 + 16)
                act.wait_ge(S("g_sp_out"), m * 16 + 16)
                act.wait_ge(S("g_cv_out"), m * 16 + 16)
                if full:
                    g_load(m + 1)
                    tile_wait(m, per, T_GLOOP + 5)
                    take_u(3, gU)(psj[(T_GLOOP + 5) % 2]).then_inc(took_act, 1)
                    ahead(m, per, T_GLOOP + 7)

            with act.Fori(0, GH - 1) as m:
                ao.enter(m, G_ACT)
                gdn_body(m, True)
            ao.leave(GH - 1)
            gdn_body(GH - 1, False)
            act.dma_start(h[:, :, :], h_spill).then_inc(S("h_back"), 16)

            def dense(t0, src):
                split_x(src, KT, t0)
                ahead(0, 0, t0 + 1)
                with act.Fori(0, KT // 2 - 1) as i:
                    for k in range(2):
                        ahead(i, 2, t0 + 2 + k)
                ahead(0, 0, t0 + KT)

            def ple(tp, te, es, hq, hbase, td, end):
                act.wait_ge(S("p_in"), 16 + es)
                split_x(lambda kt: dp[:, kt, :], PLE_K, tp)
                ahead(0, 0, tp + 1)
                for i in range(KT):
                    if i == 7:
                        ahead(0, 0, te)
                    act.wait_ge(took_dve, td + i + 1)
                    if i >= 2 or es:
                        act.wait_ge(S("ess"), es + i - 1)
                    act.activation(dSQ[:, i % 2, :], eb[:, i, :], ACT.Square).then_inc(S("esq"), 1)
                act.wait_ge(S("ess"), es + KT)
                act.activation(dRE, psB[:, 0:T], ACT.Sqrt, bias=eps_c, scale=1.0 / D_MODEL) \
                    .then_inc(S("e_root"), 1)

                def gate(i, k):
                    act.wait_ge(half_done, i * 4 + 2 * (te + k) + 2)
                    act.wait_ge(S("hnew"), i * 2 + (hq - 16 + k - 1)) if hq - 16 + k - 1 > 0 else None
                    act.activation(dSG[:, k % 2, :], psj[(te + k) % 2][:, 0:T], ACT.Sigmoid).then_inc(took_act, 1)

                def square(i, k):
                    act.wait_ge(S("hnew"), i * 2 + (hq - 16 + k + 1))
                    act.wait_ge(S("hss"), i * 2 + (hq + k - 1))
                    act.activation(dSQ[:, k % 2, :], h[:, (i * 2 + k), :], ACT.Square).then_inc(S("hsq"), 1)

                act.wait_ge(took_dve, td)
                split_x(lambda kt: h[:, kt, :], KT, te)
                ahead(0, 0, te + 1)
                gate(0, 0)
                ahead(0, 0, te + 2)
                gate(0, 1)
                square(0, 0)
                with act.Fori(0, KT // 2 - 2) as i:
                    for k in range(2):
                        ahead(i, 2, te + 3 + k)
                        gate(i, 2 + k)
                        square(i, 1 + k)
                ahead(0, 0, te + KT - 1)
                gate(0, KT - 2)
                square(0, KT - 3)
                if not end:
                    ahead(0, 0, te + KT)
                gate(0, KT - 1)
                square(0, KT - 2)
                square(0, KT - 1)

            def out_proj(t0, td):
                dense(t0, lambda kt: Y[:, kt, :])
                dense(t0 + KT, lambda kt: Y[:, KT + kt, :])

            act.wait_ge(S("g_y"), GH + 1)
            out_proj(T_O1, TD_O1)
            act.dma_start(dp[:, :, :], p_in[0]).then_inc(S("p_in"), 16)
            ple(T_P1, T_E1, 0, 16, 16, TD_P1, False)

            normed_x(16, T_SPRO)
            act.dma_start(h_spill, h[:, :, :]).then_inc(S("spill"), 16)
            ahead(0, 0, T_SPRO + 1)
            softplus_rows(SH, C_SDT, C_SA, T_SPRO, "s_", TA_S)

            def s_load(m):
                act.dma_start(sa["R2"].rearrange("p (h t) -> p h t", h=HPG),
                              s_rows[m].rearrange("h c -> (h c)").partition_broadcast(P)
                              .rearrange("p (h c) -> p h c", h=HPG)[:, :, 0:T]).then_inc(S("s_r_in"), 16)
                for j in range(2):
                    act.dma_start(sRP[HD * j:HD * j + HD, :, :],
                                  s_rows[m].rearrange("h c -> (h c)").partition_broadcast(HD)
                                  .rearrange("p (i j c) -> p i j c", i=SX, j=2)[:, :, j, 256:480]) \
                        .then_inc(S("s_rp_in"), 16)
                act.dma_start(sa["pc"], spack[m]).then_inc(S("s_pc_in"), 16)
                act.dma_start(hf[:, 0:4096], sstate[m]).then_inc(S("s_st_in"), 16)

            ahead(0, 0, T_SPRO + 2)
            act.wait_ge(S("s_hrows"), 1)
            sr = s_rows.rearrange("g h c -> (g h) c")
            act.dma_start(sr[:, 0:T], HRG[0:SH, 6, :]).then_inc(S("s_rows_out"), 16)
            act.dma_start(sr[:, T:T + 160], HRG[0:SH, 8, 128:T]).then_inc(S("s_rows_out"), 16)
            act.dma_start(sr[:, T + 160:T + 192], HRG[0:SH, 4, SEQ:T]).then_inc(S("s_rows_out"), 16)
            for k in range(1, 7):
                tile_wait(0, 0, T_SPRO + k)
                take_u(k - 1, sU)(psj[(T_SPRO + k) % 2]).then_inc(took_act, 1)
                if k == 2:
                    act.wait_ge(S("s_ccol"), 1)
                    act.activation(ccol[:, 0:384], psA[:, 0:384], ACT.Copy).then_inc(S("s_ccolc"), 1)
                if k == 3:
                    act.wait_ge(S("s_rows_out"), 48)
                    act.wait_ge(S("spill"), 32)
                    s_load(0)
                ahead(0, 0, T_SPRO + k + 2)

            def ssd_body(m, full):
                per, t0 = (10, T_SLOOP) if full else (0, T_SEND - 4)
                mt = m if full else 0
                order = [0, 1, 2, 3, None, None, None, None, 4, 5]

                def took(k):
                    if not full and not 4 <= k < 8:
                        return
                    tile_wait(mt, per, t0 + k)
                    bank = psj[(t0 + k) % 2]
                    if order[k] is not None:
                        take_u(order[k], sU)(bank).then_inc(took_act, 1)
                    else:
                        act.activation(sZS[:, k - 4, :], bank[:, 0:T], ACT.Silu).then_inc(took_act, 1)
                    if full and k > 0:
                        ahead(mt, per, t0 + k + 2)
                    if not full and k < 6:
                        ahead(0, 0, t0 + k + 2)
                    if not full and k == 6:
                        ahead(0, 0, T_O2)

                if full:
                    tile_wait(mt, per, t0)
                    ahead(mt, per, t0 + 2)
                act.wait_ge(S("s_conv"), m + 1)
                took(0)
                for i in range(6):
                    ins = act.activation(sCV[:, i, :], sCV[:, i, :], ACT.Silu, bias=spc[:, i, 28:29])
                ins.then_inc(S("s_cv"), 1)
                took(1)
                act.wait_ge(S("s_tok"), m + 1)
                act.activation(sa["BT"], psA[:, 0:2 * P], ACT.Copy).then_inc(S("s_btc"), 1)
                act.wait_ge(S("s_r_in"), m * 16 + 16)
                act.activation(sEGc, sR2[:, :, SEQ - 1], ACT.Exp)
                act.activation(sEGb, sR2[:, :, T - DEC_B:T], ACT.Exp)
                act.wait_ge(S("s_decx"), m + 1)
                act.activation(sa["DEC"], sa["DEC"], ACT.Exp).then_inc(S("s_dec"), 1)
                act.wait_ge(S("s_dtx"), m * 2 + 1)
                act.activation(sa["DT"], sa["DT"], ACT.Exp).then_inc(S("s_dt"), 1)
                took(2)
                act.wait_ge(S("s_s"), m * 2 + 1)
                act.activation(sS1, psA[:, :], ACT.Copy).then_inc(S("s_s1"), 1)
                took(3)
                act.wait_ge(S("s_dtx"), m * 2 + 2)
                act.activation(sa["DT"], sa["DT"], ACT.Exp).then_inc(S("s_dt"), 1)
                act.wait_ge(S("s_y"), m * 2 + 1)
                act.activation(sYT[:, :, 0:CH], psB[:, :].rearrange("p (i t) -> p i t", i=SX), ACT.Copy) \
                    .then_inc(S("s_y0"), 1)
                took(4)
                act.wait_ge(S("s_xt"), m + 1)
                act.wait_ge(S("s_bm"), m + 1)
                act.activation(sXT[0:NS, :], psE[0:NS, :], ACT.Copy).then_inc(S("s_xtc"), 1)
                took(5)
                took(6)
                took(7)
                act.wait_ge(S("s_g"), m + 1)
                act.activation(sa["ZS"], sa["YT"], ACT.Square).then_inc(S("s_sq"), 1)
                took(8)
                act.wait_ge(S("s_ss"), m + 1)
                act.activation(sTMr, psE[:, 0:T], ACT.Sqrt, bias=eps_c, scale=1.0 / (SX * P)).then_inc(S("s_root"), 1)
                act.wait_ge(S("s_s2"), m + 1)
                act.dma_start(sst_p[m], sS1).then_inc(S("s_sp_out"), 16)
                act.dma_start(sconv_out[m], sa["co"]).then_inc(S("s_co_out"), 16)
                act.wait_ge(S("s_su"), m * 8 + 8)
                act.dma_start(sst_s[m], hf[:, 0:4096]).then_inc(S("s_st_out"), 16)
                took(9)
                act.wait_ge(S("s_yd"), m + 2)
                act.wait_ge(S("s_st_out"), m * 16 + 16)
                act.wait_ge(S("s_sp_out"), m * 16 + 16)
                act.wait_ge(S("s_co_out"), m * 16 + 16)
                if full:
                    s_load(m + 1)

            with act.Fori(0, SG - 1) as m:
                ao.enter(m, S_ACT)
                ssd_body(m, True)
            ao.leave(SG - 1)
            ssd_body(SG - 1, False)
            act.dma_start(h[:, :, :], h_spill).then_inc(S("h_back"), 16)
            act.wait_ge(S("s_yd"), SG + 1)
            out_proj(T_O2, TD_O2)
            act.dma_start(dp[:, :, :], p_in[1]).then_inc(S("p_in"), 16)
            ple(T_P2, T_E2, 16, 32, 32, TD_P2, True)

            act.wait_ge(S("hss"), 32 + KT)
            act.activation(dRS, psA[:, 0:T], ACT.Sqrt, bias=eps_c, scale=1.0 / D_MODEL).then_inc(S("n_root"), 1)
            for kt in range(0, KT, 4):
                act.wait_ge(S("fin"), kt + 4)
                act.dma_start(y_out[:, kt:kt + 4, :], h[:, kt:kt + 4, :]).then_inc(S("y_done"), 16)
            act.wait_ge(S("y_done"), 16 * (KT // 4))

        @block.vector
        def _(dve):
            do = Order(dve, dve_order)
            dve.memset(small[:, 0:1], EPS).then_inc(S("konst"), 1)

            def lower_x(src, n, x0, m=None):
                for kt in range(n):
                    dve.wait_ge(xh_ready, x0 + kt + 1)
                    dve.tensor_tensor(xl[:, kt, :], src(kt), xh[:, kt, :].bitcast(F32), ALU.subtract) \
                        .then_inc(xl_ready, 1)

            def norm_x(n, wcol, x0):
                dve.wait_ge(S("n_root"), n)
                do.link(dve.reciprocal(dRS, dRS))
                for kt in range(KT):
                    if kt >= 2:
                        dve.wait_ge(xl_ready, x0 + kt - 1)
                    dve.scalar_tensor_tensor(dTM[:, kt % 2, :], h[:, kt, :], prm[:, wcol + kt:wcol + kt + 1],
                                             dRS, ALU.mult, ALU.mult).then_inc(S("xn"), 1)
                    if kt >= 1:
                        k = kt - 1
                        dve.wait_ge(S("xn"), (n - 1) * KT + kt)
                        dve.wait_ge(xh_ready, x0 + k + 1)
                        dve.tensor_tensor(xl[:, k, :], dTM[:, k % 2, :], xh[:, k, :].bitcast(F32), ALU.subtract) \
                            .then_inc(xl_ready, 1)
                k = KT - 1
                dve.wait_ge(S("xn"), n * KT)
                dve.wait_ge(xh_ready, x0 + k + 1)
                dve.tensor_tensor(xl[:, k, :], dTM[:, k % 2, :], xh[:, k, :].bitcast(F32), ALU.subtract) \
                    .then_inc(xl_ready, 1)

            def gate_rows(n, pre):
                H = HRG[0:n]
                dve.wait_ge(S(pre + "exp"), 1)
                do.link(dve.tensor_scalar(H[:, 2, :], H[:, 1, :], 1.0, None, ALU.add))
                dve.tensor_scalar(H[:, 4, :], H[:, 2, :], -1.0, None, ALU.add).then_inc(S(pre + "w1"), 1)
                dve.wait_ge(S(pre + "w1"), 1)
                do.link(dve.tensor_scalar(H[:, 5, :], H[:, 4, :], 0.0, None, ALU.is_equal))
                do.link(dve.tensor_tensor(H[:, 4, :], H[:, 4, :], H[:, 5, :], ALU.add))
                do.link(dve.reciprocal(H[:, 4, :], H[:, 4, :]))
                dve.wait_ge(S(pre + "ln"), 1)
                do.link(dve.tensor_tensor(H[:, 3, :], H[:, 3, :], H[:, 5, :], ALU.add))
                do.link(dve.tensor_tensor(H[:, 3, :], H[:, 3, :], H[:, 1, :], ALU.mult))
                do.link(dve.tensor_tensor(H[:, 3, :], H[:, 3, :], H[:, 4, :], ALU.mult))
                do.link(dve.scalar_tensor_tensor(H[:, 4, :], H[:, 0, :], 0.0, H[:, 3, :], ALU.max, ALU.add))
                do.link(dve.tensor_scalar(H[:, 2, :], H[:, 4, :], small[0:n, 2:3], -1.0, ALU.mult, ALU.mult))
                for c in range(NC):
                    a = slice(c * CH, (c + 1) * CH)
                    dve.tensor_tensor_scan(H[:, 6, a], ones[0:n, :], H[:, 2, a], 0.0, ALU.mult, ALU.add)
                do.link(dve.tensor_copy(H[:, 6, SEQ:SEQ + 8], H[:, 2, SEQ:SEQ + 8]))
                for t in range(1, DEC_T):
                    a = SEQ + 8 * t
                    do.link(dve.tensor_tensor(H[:, 6, a:a + 8], H[:, 6, a - 8:a], H[:, 2, a:a + 8], ALU.add))
                for c in range(NC):
                    a = slice(c * CH, (c + 1) * CH)
                    dve.tensor_scalar(H[:, 1, a], H[:, 6, a], H[:, 6, (c + 1) * CH - 1:(c + 1) * CH], -1.0,
                                      ALU.subtract, ALU.mult)
                dve.tensor_scalar(H[:, 3, :], H[:, 6, :], -1.0, None, ALU.mult).then_inc(S(pre + "cum"), 1)

            dve.wait_ge(S("x_in"), 16)
            dve.wait_ge(S("prm_in"), 16)
            dve.wait_ge(c_in, 16)
            norm_x(1, C_NORM, X0["g"])
            dve.wait_ge(xl_ready, X0["g"] + KT)

            do.link(dve.memset(gU[:, :, 0:PRE], 0.0))
            gate_rows(GV, "g_")
            dve.wait_ge(S("g_eg"), 1)
            dve.wait_ge(took_act, 2)
            dve.scalar_tensor_tensor(HRG[0:GV, 4, :], HRG[0:GV, 7, :], -1.0, HRG[0:GV, 8, :],
                                     ALU.mult, ALU.mult).then_inc(S("g_hrows"), 1)
            dve.memset(small[:, 4:5], 0.0).then_inc(S("zero_u"), 1)
            dve.memset(small[:, 5:6], 0.0).then_inc(S("g_y"), 1)

            def conv_tap(U, CV, n, tap, cache, co, j):
                if j == 0:
                    do.link(dve.tensor_copy(U[:, :, UC:US], cache))
                    dve.tensor_copy(co[:, :, 0:PRE], U[:, :, UC - PRE:UC])
                    dve.tensor_copy(co[:, :, PRE:CW], U[:, :, UW - PRE * DEC_B:UW])
                for i in range(n):
                    for dst, a, w in (((0, SEQ), j, SEQ), ((SEQ, T), UC + DEC_B * j, NS)):
                        out, src = CV[:, i, dst[0]:dst[1]], U[:, i, a:a + w]
                        if j == 0:
                            ins = dve.tensor_scalar(out, src, tap(i, j), None, ALU.mult)
                        else:
                            ins = dve.scalar_tensor_tensor(out, src, tap(i, j), out, ALU.mult, ALU.add)
                return ins

            def conv(U, CV, n, tap, cache, co, ready):
                for j in range(CONV_W):
                    ins = conv_tap(U, CV, n, tap, cache, co, j)
                    if j < CONV_W - 1:
                        do.link(ins)
                ins.then_inc(ready, 1)

            def gdn_qk_conv(m, took):
                dve.wait_ge(S("g_pq_in"), m * 16 + 16)
                dve.wait_ge(took_act, took)
                conv(gU[:, 0:2, :], gCR[:, 0:2, :], 2, lambda i, j: gpc_tap[0][:, i, j:j + 1], gpc_cache[0],
                     gco[:, 0:2, :], S("g_convq"))

            def gdn_qk_norm(m):
                dve.wait_ge(S("g_rs"), m + 1)
                do.link(dve.reciprocal(gRS[:, 1, :], gRS[:, 1, :]))
                dve.tensor_tensor(gKN[:, 1, :], gCR[:, 1, :], gRS[:, 1, :], ALU.mult)
                do.link(dve.reciprocal(gRS[:, 0, :], gRS[:, 0, :]))
                dve.scalar_tensor_tensor(gKN[:, 0, :], gCR[:, 0, :], float(P) ** -0.5, gRS[:, 0, :],
                                         ALU.mult, ALU.mult).then_inc(S("g_kn"), 1)

            def gdn_sample(piece, m):
                v = gCR[:, 2:4, SEQ:T]
                _, B, EG = (gR[:, :, k, SEQ:T] for k in range(3))
                kq = psD[:, 160:288].rearrange("p (b j q t) -> p q j t b", b=DEC_B, j=2, q=2)
                if piece == 0:
                    dve.wait_ge(S("g_smp"), m + 1)
                    dve.tensor_tensor(gCQ[:, :, :], gDEC[:, :, :], bc(psD[:, 0:NPAIR], 1, 2), ALU.mult)
                    do.link(dve.tensor_tensor(gCK[:, :, :], gDEC[:, :, :], bc(psD[:, NPAIR:2 * NPAIR], 1, 2),
                                              ALU.mult))
                    for s in range(3):
                        a = slice(OFF[s], OFF[s] + LEN[s])
                        dve.tensor_tensor(gCK[:, :, a], gCK[:, :, a], B[:, :, 8 * s:NS], ALU.mult)
                    do.link(dve.tensor_tensor(gBE[:, :, :], B, EG, ALU.mult))
                if piece == 1:
                    e4 = lambda ap: ap.rearrange("p j (t b) -> p j t b", b=DEC_B)
                    dve.tensor_tensor(gW[:, :, :], B, v, ALU.mult)
                    do.link(dve.tensor_tensor(e4(gTM[:, :, :]), e4(gBE[:, :, :]), kq[:, 1], ALU.mult))
                    dve.tensor_tensor(gW[:, :, :], gW[:, :, :], gTM[:, :, :], ALU.subtract)
                    do.link(dve.tensor_tensor(e4(gO[:, :, SEQ:T]), e4(EG), kq[:, 0], ALU.mult))
                if piece in (2, 3, 4):
                    s = piece - 2
                    n = DEC_T - 1 - s
                    src = bc(gW[:, :, 8 * s:8 * s + 8], 2, n)
                    out = gTM[:, :, 0:8 * n].rearrange("p j (t b) -> p j t b", b=8)
                    ck = gCK[:, :, OFF[s] + 8:OFF[s] + LEN[s]].rearrange("p j (t b) -> p j t b", b=8)
                    do.link(dve.tensor_tensor(out, ck, src, ALU.mult))
                    do.link(dve.tensor_tensor(gW[:, :, 8 * s + 8:NS], gW[:, :, 8 * s + 8:NS], gTM[:, :, 0:8 * n],
                                              ALU.subtract))
                if piece == 5:
                    for s in range(DEC_T):
                        a = OFF[s] + LEN[s] - 8
                        ins = dve.tensor_tensor(gWD[:, :, 8 * s:8 * s + 8], gW[:, :, 8 * s:8 * s + 8],
                                                gDEC[:, :, a:a + 8], ALU.mult)
                    ins.then_inc(S("g_wd"), 1)
                if piece == 6:
                    for s in range(DEC_T):
                        n = DEC_T - s
                        out = gTM[:, :, 0:8 * n].rearrange("p j (t b) -> p j t b", b=8)
                        cq = gCQ[:, :, OFF[s]:OFF[s] + LEN[s]].rearrange("p j (t b) -> p j t b", b=8)
                        do.link(dve.tensor_tensor(out, cq, bc(gW[:, :, 8 * s:8 * s + 8], 2, n), ALU.mult))
                        o = gO[:, :, SEQ + 8 * s:T]
                        ins = dve.tensor_tensor(o, o, gTM[:, :, 0:8 * n], ALU.add)
                        if s < DEC_T - 1:
                            do.link(ins)
                    ins.then_inc(S("g_os_dve"), 1)

            def u4(ap):
                return ap.rearrange("p (c j) t -> p c j t", c=NC)

            def gdn_body(m, full):
                dve.wait_ge(S("g_r_in"), m * 16 + 16)
                do.link(dve.tensor_copy(
                    gcc.rearrange("p k c j -> p (k c) j"),
                    ccol[:, 0:8 * GV].rearrange("p (k h) -> p k h", h=GV)[:, :, bass.ds(m * 2, 2)]))
                for c in range(NC):
                    for j in range(2):
                        dve.tensor_scalar(gDT[:, 2 * c + j, :], gR[:, j, 0, c * CH:(c + 1) * CH],
                                          gcc[:, 1, c, j:j + 1], 0.0, ALU.add, ALU.min)
                G = gR[:, :, 0, SEQ:T].rearrange("p j (t b) -> p j t b", b=8)
                for s in range(DEC_T):
                    n = DEC_T - s
                    ins = dve.tensor_tensor(gDEC[:, :, OFF[s]:OFF[s] + LEN[s]].rearrange("p j (t b) -> p j t b", b=8),
                                            G[:, :, s:, :], bc(gR[:, :, 0, SEQ + 8 * s:SEQ + 8 * s + 8], 2, n),
                                            ALU.subtract)
                ins.then_inc(S("g_dtx"), 1)
                dve.wait_ge(S("g_kn"), m + 1)
                for s in range(DEC_T):
                    n = DEC_T - s
                    t4 = lambda ap: ap.rearrange("p i (t b) -> p i t b", b=8)
                    k_s = bc(bc(gKN[:, 1, SEQ + 8 * s:SEQ + 8 * s + 8], 1, n), 1, 2)
                    ins = dve.tensor_tensor(t4(gPR[:, :, OFF[s]:OFF[s] + LEN[s]]), t4(gKN[:, 0:2, SEQ + 8 * s:T]),
                                            k_s, ALU.mult)
                ins.then_inc(S("g_pr"), 1)
                dve.wait_ge(S("g_dte"), m + 1)
                do.link(dve.tensor_tensor(gDT[:, :, :], gDT[:, :, :], bc(cst[:, K_INC, :], 1, 4), ALU.mult))
                dve.wait_ge(S("g_tok"), m + 1)
                kk = bc(psC[:, 0:256].rearrange("p (c t) -> p c t", c=NC), 2, 2)
                qk = bc(psC[:, 256:512].rearrange("p (c t) -> p c t", c=NC), 2, 2)
                do.link(dve.tensor_tensor(u4(gAT[:, :, :]), u4(gDT[:, :, :]), kk, ALU.mult))
                beta = gR[:, :, 1, 0:SEQ].rearrange("p j (c t) -> p c j t", c=NC)
                do.link(dve.tensor_tensor(u4(gAT[:, :, :]), u4(gAT[:, :, :]), beta, ALU.mult))
                do.link(dve.tensor_tensor(gP[:, :, :], gAT[:, :, :], bc(cst[:, K_M1, :], 1, 4), ALU.mult))
                dve.tensor_tensor(gDE[:, :, 1, :, :], bc(bc(ident, 1, 2), 1, NC), u4(gP[:, :, :]), ALU.subtract) \
                    .then_inc(S("g_e1"), 1)
                dve.tensor_tensor(u4(gQK[:, :, :]), u4(gDT[:, :, :]), qk, ALU.mult)
                dve.tensor_tensor(gKM, bc(psE[0:NS, 0:P], 1, DEC_B), bc(bmask, 2, P), ALU.mult) \
                    .then_inc(S("g_km"), 1)
                dve.tensor_tensor(gQD[:, :, :], bc(gKN[:, 0, CH:2 * CH], 1, 2), gR[:, :, 2, CH:2 * CH], ALU.mult)

                def v_tap(j):
                    ins = conv_tap(gU[:, 2:4, :], gCR[:, 2:4, :], 2, lambda i, j: gpc_tap[1][:, i, j:j + 1],
                                   gpc_cache[1], gco[:, 2:4, :], j)
                    if j < CONV_W - 1:
                        do.link(ins)
                    else:
                        ins.then_inc(S("g_convv"), 1)

                def mask_p(c, lv):
                    dve.wait_ge(S(f"g_p{c}"), m * 6 + lv + 1)
                    dve.tensor_tensor(gP[:, 2 * c:2 * c + 2, :],
                                      (psC, psE)[c][:, 0:2 * P].rearrange("p (j t) -> p j t", j=2),
                                      bc(cst[:, K_LEV + lv, :], 1, 2), ALU.mult).then_inc(S(f"g_pm{c}"), 1)

                def less_q(c, lv):
                    dve.wait_ge(S(f"g_q{c}"), m * 6 + lv + 1)
                    k = 0 if lv < 5 else 1
                    de = gDE[:, c, k:2].rearrange("p k j t -> p (k j t)")
                    dve.tensor_tensor(de, de, (psA, psF)[c][:, 2 * P * k:], ALU.subtract).then_inc(S(f"g_de{c}"), 1)

                dve.wait_ge(S("g_pv_in"), m * 16 + 16)
                dve.wait_ge(S("g_e1"), m + 1)
                for lv in range(6):
                    mask_p(0, lv)
                    if lv > 0:
                        less_q(1, lv - 1)
                    if lv < CONV_W:
                        v_tap(lv)
                    if lv == 4:
                        gdn_sample(0, m)
                    mask_p(1, lv)
                    less_q(0, lv)
                less_q(1, 5)
                dve.wait_ge(S("g_cv"), m + 1)
                for piece in range(1, 6):
                    gdn_sample(piece, m)
                dve.wait_ge(S("g_ks"), m + 1)
                for j in range(2):
                    ins = dve.scalar_tensor_tensor(gVB[:, 2 + j, :], psD[:, j * P:(j + 1) * P], gcc[:, 2, 1, j:j + 1],
                                                   gVB[:, 2 + j, :], ALU.mult, ALU.add)
                ins.then_inc(S("g_rhs"), 1)
                gdn_sample(6, m)
                if full:
                    gdn_qk_conv(m + 1, m * 6 + 8)
                dve.wait_ge(S("g_s"), m * 2 + 2)
                for j in range(2):
                    ins = dve.scalar_tensor_tensor(gS2[:, j, :], gS1[:, j, :], gR[:, j, 2, SEQ - 1:SEQ],
                                                   psE[:, j * P:(j + 1) * P], ALU.mult, ALU.add)
                ins.then_inc(S("g_s2"), 1)
                for i in range(4):
                    dve.wait_ge(S("g_sp"), m * 4 + i + 1)
                    for b in (2 * i, 2 * i + 1):
                        for j in range(2):
                            at = (b % 2) * 256 + j * P
                            ins = dve.scalar_tensor_tensor(gS[:, b, j, :], gS[:, b, j, :],
                                                           gR[:, j, 2, T - DEC_B + b:T - DEC_B + b + 1],
                                                           (psA, psB)[i % 2][:, at:at + P], ALU.mult, ALU.add)
                    ins.then_inc(S("g_su"), 1)
                dve.wait_ge(S("g_rs2"), m + 1)
                do.link(dve.reciprocal(ga["RSO"], ga["RSO"]))
                do.link(dve.scalar_tensor_tensor(ga["O"], ga["O"], prm[:, C_GNORM:C_GNORM + 1], ga["RSO"],
                                                 ALU.mult, ALU.mult))
                dve.tensor_tensor(Y[:, bass.ds(m * 2, 2), :], gO[:, :, :], gZS[:, :, :], ALU.mult) \
                    .then_inc(S("g_y"), 1)
                if full:
                    gdn_qk_norm(m + 1)

            dve.wait_ge(S("g_ccolc"), 1)
            gdn_qk_conv(0, 4)
            gdn_qk_norm(0)
            dve.wait_ge(took_act, 6)
            with dve.Fori(0, GH - 1) as m:
                do.enter(m, G_DVE)
                gdn_body(m, True)
                dve.wait_ge(took_act, m * 6 + 12)
            do.leave(GH - 1)
            gdn_body(GH - 1, False)

            def out_proj(t0, xa, xb, td, back):
                for n, x0 in ((0, xa), (1, xb)):
                    lower_x(lambda kt: Y[:, n * KT + kt, :], KT, x0)
                    if n == 0:
                        dve.wait_ge(S("h_back"), back)
                    with dve.Fori(0, KT // 2) as i:
                        for k in range(2):
                            t = t0 + n * KT + k
                            dve.wait_ge(half_done, i * 4 + 2 * t + 2)
                            if n == 1:
                                dve.wait_ge(took_dve, i * 2 + (td + k + 1))
                            dve.tensor_tensor(h[:, i * 2 + k, :], h[:, i * 2 + k, :], psj[t % 2][:, 0:T], ALU.add) \
                                .then_inc(took_dve, 1)

            def ple(tp, te, xp, xe, td, layer, hq):
                lower_x(lambda kt: dp[:, kt, :], PLE_K, xp)
                for i in range(KT):
                    if i % 4 == 3:
                        dve.wait_ge(half_done, 2 * tp + i // 4 + 1)
                    else:
                        dve.wait_ge(S("e_done"), layer * 12 + i - i // 4 + 1)
                    dve.tensor_copy(eb[:, i, :], psj[(tp + i) % 2][:, 0:T]).then_inc(took_dve, 1)
                lower_x(lambda kt: h[:, kt, :], KT, xe)
                dve.wait_ge(S("e_root"), layer + 1)
                do.link(dve.reciprocal(dRE, dRE))
                wc = C_PLE + layer * KT
                for i in range(KT):
                    ins = dve.scalar_tensor_tensor(eb[:, i, :], eb[:, i, :], prm[:, wc + i:wc + i + 1], dRE,
                                                   ALU.mult, ALU.mult)
                do.link(ins)
                with dve.Fori(0, KT // 2) as i:
                    do.enter(i, 2)
                    for k in range(2):
                        dve.wait_ge(took_act, i * 2 + ((TA_E1, TA_E2)[layer] + k + 1))
                        do.link(dve.tensor_tensor(dTM[:, k, :], eb[:, i * 2 + k, :], dSG[:, k, :], ALU.mult))
                        dve.tensor_tensor(h[:, i * 2 + k, :], h[:, i * 2 + k, :], dTM[:, k, :], ALU.add) \
                            .then_inc(S("hnew"), 1)
                do.leave(KT // 2)

            out_proj(T_O1, X0["oa1"], X0["ob1"], TD_O1, 16)
            ple(T_P1, T_E1, X0["p1"], X0["e1"], TD_P1, 0, 16)

            norm_x(2, C_NORM + KT, X0["s"])
            dve.wait_ge(xl_ready, X0["s"] + KT)
            do.link(dve.memset(sU[:, :, 0:PRE], 0.0))
            gate_rows(SH, "s_")
            dve.wait_ge(S("s_eg"), 1)
            dve.memset(small[:, 4:5], 0.0).then_inc(S("s_hrows"), 1)
            dve.memset(small[:, 5:6], 0.0).then_inc(S("s_yd"), 1)

            def ssd_decays(m, c):
                for hh in range(HPG):
                    ins = dve.tensor_scalar(sDT[:, hh, :], sR2[:, hh, c * CH:(c + 1) * CH],
                                            scc[:, 1, c, hh:hh + 1], 0.0, ALU.add, ALU.min)
                ins.then_inc(S("s_dtx"), 1)

            def ssd_body(m, took0):
                dve.wait_ge(S("s_pc_in"), m * 16 + 16)
                dve.wait_ge(took_act, took0)
                dve.wait_ge(S("s_r_in"), m * 16 + 16)
                dve.wait_ge(S("s_rp_in"), m * 32 + 32)
                dve.tensor_copy(scc.rearrange("p k c j -> p (k c) j"),
                                ccol[:, 0:6 * SH].rearrange("p (k h) -> p k h", h=SH)[:, :, bass.ds(m * HPG, HPG)])
                conv(sU, sCV, 6, lambda i, j: spc[:, i, 24 + j:25 + j], spc[:, :, 0:24], sco, S("s_conv"))
                A = sRP[:, :, 0:NS].rearrange("p i (t b) -> p i t b", b=8)
                for s in range(DEC_T):
                    n = DEC_T - s
                    ins = dve.tensor_tensor(
                        sDEC[:, :, OFF[s]:OFF[s] + LEN[s]].rearrange("p i (t b) -> p i t b", b=8),
                        A[:, :, s:, :], bc(sRP[:, :, 8 * s:8 * s + 8], 2, n), ALU.subtract)
                ins.then_inc(S("s_decx"), 1)
                ssd_decays(m, 0)
                dve.wait_ge(S("s_cv"), m + 1)
                Bt = sCV[:, 0, SEQ:T]
                Ct = sCV[:, 1, SEQ:T].rearrange("p (t b) -> p t b", b=8)
                for s in range(DEC_T):
                    n = DEC_T - s
                    ins = dve.tensor_tensor(sPR[:, OFF[s]:OFF[s] + LEN[s]].rearrange("p (t b) -> p t b", b=8),
                                            Ct[:, s:, :], bc(Bt[:, 8 * s:8 * s + 8], 1, n), ALU.mult)
                ins.then_inc(S("s_pr"), 1)
                dve.wait_ge(S("s_tok"), m + 1)

                def decayed(c):
                    dve.tensor_tensor(sXD, sX[:, c], bc(scc[:, 2, c, :], 2, HD), ALU.mult).then_inc(S("s_xd"), 1)

                for c in range(NC):
                    ins = dve.tensor_tensor(sX[:, c], (psB, psC)[c][:, :].rearrange("p (h d) -> p h d", h=HPG),
                                            bc(scc[:, 0, c, :], 2, HD), ALU.mult)
                do.link(ins)
                decayed(0)
                dve.tensor_tensor(sCB[:, :, :], psD[:, 0:2 * P].rearrange("p (c t) -> p c t", c=NC),
                                  bc(cst[:, K_INC, :], 1, NC), ALU.mult)
                dve.tensor_tensor(sBMv, bc(psE[0:NS, 0:P], 1, DEC_B), bc(bmask, 2, P), ALU.mult) \
                    .then_inc(S("s_bm"), 1)
                dve.wait_ge(S("s_bm"), m + 1)
                dve.wait_ge(S("s_dt"), m * 2 + 1)
                dve.tensor_tensor(sDT[:, :, :], sDT[:, :, :], bc(sCB[:, 0, :], 1, HPG), ALU.mult).then_inc(S("s_w"), 1)
                dve.wait_ge(S("s_s"), m * 2 + 1)
                decayed(1)
                dve.tensor_tensor(sXS[:, :, :], sCV[:, 2:6, SEQ:T], sRP[:, :, 192:224], ALU.mult)
                dve.wait_ge(S("s_dec"), m + 1)
                dve.wait_ge(S("s_smp"), m + 1)
                ys = sYT[:, :, SEQ:T]
                y4 = lambda ap: ap.rearrange("p i (t b) -> p i t b", b=8)
                do.link(dve.tensor_tensor(y4(ys), y4(sRP[:, :, 160:192]),
                                          psF[:, P:2 * P].rearrange("p (i b t) -> p i t b", i=SX, b=8), ALU.mult))
                for s in range(DEC_T):
                    a = OFF[s] + LEN[s] - 8
                    ins = dve.tensor_tensor(sXE[:, :, 8 * s:8 * s + 8], sXS[:, :, 8 * s:8 * s + 8],
                                            sDEC[:, :, a:a + 8], ALU.mult)
                ins.then_inc(S("s_xe"), 1)
                dve.wait_ge(S("s_xe"), m + 1)
                do.link(dve.tensor_tensor(sDEC[:, :, :], sDEC[:, :, :], bc(psF[:, 0:NPAIR], 1, SX), ALU.mult))
                for s in range(DEC_T):
                    n = DEC_T - s
                    do.link(dve.tensor_tensor(y4(sTM[:, :, 0:8 * n]), y4(sDEC[:, :, OFF[s]:OFF[s] + LEN[s]]),
                                              bc(sXS[:, :, 8 * s:8 * s + 8], 2, n), ALU.mult))
                    do.link(dve.tensor_tensor(ys[:, :, 8 * s:NS], ys[:, :, 8 * s:NS], sTM[:, :, 0:8 * n], ALU.add))
                dve.wait_ge(S("s_y"), m * 2 + 1)
                ssd_decays(m, 1)
                dve.wait_ge(S("s_off"), m + 1)
                y1 = sYT[:, :, CH:SEQ]
                do.link(dve.tensor_tensor(y1, psD[:, :].rearrange("p (i t) -> p i t", i=SX), sRP[:, :, 32:160],
                                          ALU.mult))
                dve.wait_ge(S("s_dt"), m * 2 + 2)
                dve.tensor_tensor(sDT[:, :, :], sDT[:, :, :], bc(sCB[:, 1, :], 1, HPG), ALU.mult).then_inc(S("s_w"), 1)
                dve.wait_ge(S("s_s"), m * 2 + 2)
                s1 = sS1.rearrange("p (h d) -> p h d", h=HPG)
                do.link(dve.tensor_tensor(s1, s1, bc(sEGc, 2, HD), ALU.mult))
                dve.tensor_tensor(sS1, sS1, psA[:, :], ALU.add).then_inc(S("s_s2"), 1)
                dve.wait_ge(S("s_y"), m * 2 + 2)
                dve.wait_ge(S("s_y0"), m + 1)
                do.link(dve.tensor_tensor(y1, y1, psC[:, :].rearrange("p (i t) -> p i t", i=SX), ALU.add))
                for i in range(SX):
                    ins = dve.scalar_tensor_tensor(sYT[:, i, :], sCV[:, 2 + i, :], spc_D[:, i:i + 1], sYT[:, i, :],
                                                   ALU.mult, ALU.add)
                ins.then_inc(S("s_yt"), 1)
                dve.wait_ge(S("s_yt"), m + 1)
                for b in range(DEC_B):
                    do.link(dve.tensor_tensor(sS[:, b], sS[:, b], bc(sEGb[:, :, b], 2, HD), ALU.mult))
                    dve.wait_ge(S("s_sp"), m * 8 + b + 1)
                    dve.tensor_tensor(sS[:, b], sS[:, b],
                                      (psA, psF)[b % 2][:, :].rearrange("p (h d) -> p h d", h=HPG), ALU.add) \
                        .then_inc(S("s_su"), 1)
                gate_y(m)
                dve.wait_ge(S("s_root"), m + 1)
                do.link(dve.reciprocal(sTMr, sTMr))
                for i in range(SX):
                    ins = dve.scalar_tensor_tensor(Y[:, m * SX + i, :], sYT[:, i, :], spc_norm[:, i:i + 1], sTMr,
                                                   ALU.mult, ALU.mult)
                ins.then_inc(S("s_yd"), 1)

            def gate_y(m):
                dve.wait_ge(took_act, took_z[0])
                dve.tensor_tensor(sa["YT"], sa["YT"], sa["ZS"], ALU.mult).then_inc(S("s_g"), 1)

            took_z = [0]
            dve.wait_ge(S("s_ccolc"), 1)
            with dve.Fori(0, SG - 1) as m:
                do.enter(m, S_DVE)
                took_z[0] = m * 10 + (TA_S + 7 + 8)
                ssd_body(m, m * 10 + (TA_S + 7))
            do.leave(SG - 1)
            took_z[0] = TA_S + 7 + 10 * (SG - 1) + 4
            ssd_body(SG - 1, (SG - 1) * 10 + TA_S + 7)

            out_proj(T_O2, X0["oa2"], X0["ob2"], TD_O2, 32)
            ple(T_P2, T_E2, X0["p2"], X0["e2"], TD_P2, 1, 32)

            dve.wait_ge(S("n_root"), 3)
            do.link(dve.reciprocal(dRS, dRS))
            for kt in range(KT):
                dve.scalar_tensor_tensor(h[:, kt, :], h[:, kt, :], prm[:, C_FINAL + kt:C_FINAL + kt + 1], dRS,
                                         ALU.mult, ALU.mult).then_inc(S("fin"), 1)


def _tiles(w, cols):
    k = w.shape[0] // D_MODEL
    out = []
    for part in range(k):
        blk = w[part * D_MODEL:(part + 1) * D_MODEL]
        for c in cols:
            out.append(blk[:, c:c + P].reshape(2, 8, P, P).transpose(0, 2, 1, 3))
    return out


def _narrow(w, c, n):
    import numpy as np
    a = np.concatenate([w[:, c:c + n], np.zeros((w.shape[0], P - n), w.dtype)], axis=1)
    return a.reshape(2, 8, P, P).transpose(0, 2, 1, 3)


def _tokens(prompt, sample):
    import numpy as np
    return np.concatenate([prompt, sample.transpose(1, 0, 2).reshape(NS, -1)], axis=0).T


def kernel(**inputs):
    import numpy as np
    import concourse.bacc as bacc
    from concourse.bass_utils import run_bass_kernel_spmd

    a = {k: np.asarray(v) for k, v in inputs.items()}
    gw, sw = a["gdn_w_in"][0], a["ssd_w_in"][0]
    QK, VW = GH * P, GV * P
    ZG, AG = 2 * QK + VW, 2 * QK + 2 * VW
    q = [P * n for n in range(GH)]
    k = [QK + P * n for n in range(GH)]
    v = [2 * QK + P * n for n in range(GV)]
    z = [ZG + P * n for n in range(GV)]
    DI = SH * HD
    zs = [P * n for n in range(SX * SG)]
    xs = [DI + P * n for n in range(SX * SG)]
    bs = [2 * DI + P * n for n in range(SG)]
    cs = [2 * DI + SG * P + P * n for n in range(SG)]
    stream = [_narrow(gw, AG, GV), _narrow(gw, AG + GV, GV)]
    stream += _tiles(gw, [q[0], k[0], v[0], v[1]])
    for m in range(GH - 1):
        stream += _tiles(gw, [q[m + 1], k[m + 1], z[2 * m], z[2 * m + 1], v[2 * m + 2], v[2 * m + 3]])
    stream += _tiles(gw, z[-2:])

    def dense(n, w_out):
        out = _tiles(w_out, range(0, D_MODEL, P))
        wp = a["ple_w_proj"][n].reshape(PLE_K, P, 2, 2, 4, P)
        out += list(wp.transpose(2, 3, 1, 4, 0, 5).reshape(2, 2, P, 8, P))
        return out + _tiles(a["ple_w_gate"][n], range(0, D_MODEL, P))

    stream += dense(0, a["gdn_w_out"][0])
    stream += [_narrow(sw, 2 * DI + 2 * SG * P, SH)]

    def bcx(g):
        return [bs[g], cs[g]] + xs[SX * g:SX * g + SX]

    stream += _tiles(sw, bcx(0))
    for m in range(SG - 1):
        n = bcx(m + 1)
        stream += _tiles(sw, n[:4] + zs[SX * m:SX * m + SX] + n[4:])
    stream += _tiles(sw, zs[-SX:])
    stream += dense(1, a["ssd_w_out"][0])
    weights = np.stack(stream).reshape(N_HALF, P, 8, P)

    def kt_cols(w):
        return w.reshape(-1, P).T

    def act_layout(x):
        return x.reshape(-1, P, T).transpose(1, 0, 2)

    x_in = act_layout(_tokens(a["x_prompt"][0], a["x_sample"]))
    p_in = np.stack([act_layout(_tokens(a["p_prompt"][n, 0], a["p_sample"][n])) for n in range(DEPTH)])
    prm = np.zeros((P, N_PRM), np.float32)
    prm[:, C_NORM:C_NORM + 32] = kt_cols(a["norm_w"])
    prm[:, C_PLE:C_PLE + 32] = kt_cols(a["ple_norm_w"])
    prm[:, C_FINAL:C_FINAL + 16] = kt_cols(a["final_norm_w"])
    prm[:, C_GNORM] = a["gdn_norm_w"][0]
    prm[:GV, C_GDT], prm[:GV, C_GA] = a["gdn_dt_bias"][0], a["gdn_A_log"][0]
    prm[:SH, C_SDT], prm[:SH, C_SA] = a["ssd_dt_bias"][0], a["ssd_A_log"][0]

    i, j = np.arange(P)[:, None], np.arange(P)[None, :]
    cst = np.zeros((P, N_CST, P), np.float32)
    cst[:, K_ID], cst[:, K_ONE], cst[:, K_INC] = i == j, 1.0, j >= i
    cst[:, K_M1] = (i % 2 == 0) & (j == i + 1)
    for lv in range(6):
        s = 2 << lv
        cst[:, K_LEV + lv] = (i // (2 * s) == j // (2 * s)) & (i // s % 2 == 1) & (j // s % 2 == 0)
    cst[:NS, K_BM, :DEC_B] = i[:NS] % DEC_B == j[:, :DEC_B]

    def chan(w, cols):
        return np.stack([w[:, c:c + P].T for c in cols], axis=1)

    gcache = a["cache_gdn_conv"][0].transpose(1, 0, 2).reshape(PRE * DEC_B, -1)
    scache = a["cache_ssd_conv"][0].transpose(1, 0, 2).reshape(PRE * DEC_B, -1)
    gpack, spack = [], []
    for m in range(GH):
        gpack.append(np.stack([np.concatenate([chan(gcache, cols).reshape(P, -1),
                                               chan(a["gdn_conv_w"][0], cols).reshape(P, -1)], axis=1)
                               for cols in ([q[m], k[m]], [v[2 * m], v[2 * m + 1]])]))
    D = np.repeat(a["ssd_D"][0], HD)[None]
    for g in range(SG):
        cols = [c - DI for c in bcx(g)]
        pack = np.concatenate([chan(scache, cols), chan(a["ssd_conv_w"][0], cols),
                               chan(a["ssd_conv_b"], cols)], axis=2).reshape(P, -1)
        mine = [P * (SX * g + n) for n in range(SX)]
        spack.append(np.concatenate([pack, chan(a["ssd_norm_w"], mine)[:, :, 0], chan(D, mine)[:, :, 0]], axis=1))
    gpack, spack = np.stack(gpack), np.stack(spack)
    gstate = a["state_gdn"][0].reshape(DEC_B, GH, 2, P, P).transpose(1, 3, 0, 2, 4).reshape(GH, P, -1)
    sstate = a["state_ssd"][0].reshape(DEC_B, SG, HPG, HD, P).transpose(1, 4, 0, 2, 3).reshape(SG, P, -1)

    nc = bacc.Bacc("TRN2", target_bir_lowering=False, num_devices=1)
    arrays, args = {}, {}
    for name, arr in (("weights", weights), ("x_in", x_in), ("p_in", p_in), ("prm_in", prm), ("cst_in", cst),
                      ("gpack", gpack), ("spack", spack), ("gstate", gstate), ("sstate", sstate)):
        arrays[name + "_d"] = np.ascontiguousarray(arr)
        args[name] = nc.dram_tensor(name + "_d", arr.shape, F32, kind="ExternalInput").ap()
    for name, shape in (("y_out", (P, KT, T)), ("gconv_out", (GH, 2, P, 2 * CW)), ("sconv_out", (SG, P, 6 * CW)),
                        ("gst_p", (GH, P, 2 * P)), ("gst_s", (GH, P, DEC_B * 2 * P)),
                        ("sst_p", (SG, P, HPG * HD)), ("sst_s", (SG, P, DEC_B * HPG * HD))):
        args[name] = nc.dram_tensor(name + "_d", shape, F32, kind="ExternalOutput").ap()
    for name, shape in (("g_rows", (GH, 2 * 3 * T)), ("s_rows", (SG, HPG, 480)), ("h_spill", (P, KT, T))):
        args[name] = nc.dram_tensor(name + "_d", shape, F32, kind="Internal").ap()
    build(nc, **args, G_DVE=G_DVE_LINKS, G_ACT=1, S_DVE=S_DVE_LINKS, S_ACT=0)
    r = run_bass_kernel_spmd(nc, [arrays], core_ids=[0]).results[0]

    y = r["y_out_d"].transpose(1, 0, 2).reshape(D_MODEL, T).T
    gconv = r["gconv_out_d"].reshape(GH, 2, P, 2, CW).transpose(0, 2, 1, 3, 4).reshape(GH, P, 4, CW)
    gch = np.concatenate([gconv[:, :, 0].transpose(2, 0, 1).reshape(CW, -1),
                          gconv[:, :, 1].transpose(2, 0, 1).reshape(CW, -1),
                          gconv[:, :, 2:4].transpose(3, 0, 2, 1).reshape(CW, -1)], axis=1)
    sconv = r["sconv_out_d"].reshape(SG, P, 6, CW)
    sch = np.concatenate([sconv[:, :, 2:6].transpose(3, 0, 2, 1).reshape(CW, -1),
                          sconv[:, :, 0].transpose(2, 0, 1).reshape(CW, -1),
                          sconv[:, :, 1].transpose(2, 0, 1).reshape(CW, -1)], axis=1)

    def caches(c):
        return c[None, None, :PRE], c[PRE:].reshape(PRE, DEC_B, -1).transpose(1, 0, 2)[None]

    cg_p, cg_s = caches(gch)
    cs_p, cs_s = caches(sch)
    sg_p = r["gst_p_d"].reshape(GH, P, 2, P).transpose(0, 2, 1, 3).reshape(1, 1, GV, P, P)
    sg_s = r["gst_s_d"].reshape(GH, P, DEC_B, 2, P).transpose(2, 0, 3, 1, 4).reshape(1, DEC_B, GV, P, P)
    ss_p = r["sst_p_d"].reshape(SG, P, HPG, HD).transpose(0, 2, 3, 1).reshape(1, 1, SH, HD, P)
    ss_s = r["sst_s_d"].reshape(SG, P, DEC_B, HPG, HD).transpose(2, 0, 3, 4, 1).reshape(1, DEC_B, SH, HD, P)
    y_s = y[SEQ:].reshape(DEC_T, DEC_B, D_MODEL).transpose(1, 0, 2)
    return tuple(np.ascontiguousarray(o) for o in
                 (y[:SEQ][None], y_s, sg_p, cg_p, ss_p, cs_p, sg_s, cg_s, ss_s, cs_s))
```

```python
from contextlib import ExitStack

import concourse.bass as bass
from concourse import mybir

F32 = mybir.dt.float32
F32R = mybir.dt.float32r
ALU = mybir.AluOpType
ACT = mybir.ActivationFunctionType

P = 128
D_MODEL = 2048
KT = D_MODEL // P
SEQ = 256
DEC_B, DEC_T = 8, 4
NS = DEC_B * DEC_T
T = SEQ + NS
CH = 128
NC = SEQ // CH
CONV_W = 4
PRE = CONV_W - 1
EPS = 1e-6
DEPTH = 2
PLE_K = 256 // P

GH = 16
GV = 2 * GH
SG, SH = 8, 64
HPG = SH // SG
SX = HPG // 2
HD = 64

UP, UC, US = PRE, PRE + SEQ, PRE + SEQ + PRE * DEC_B
UW = US + NS
CW = PRE + PRE * DEC_B
PC_G = 4 * (PRE * DEC_B + CONV_W)
PC_S = 6 * (PRE * DEC_B + CONV_W + 1)

OFF = [0, 32, 56, 72]
LEN = [32, 24, 16, 8]
NPAIR = 80

T_GPRO = 0
T_GLOOP = T_GPRO + 6
T_GEND = T_GLOOP + 6 * (GH - 1)
T_O1 = T_GEND + 2
T_P1 = T_O1 + 32
T_E1 = T_P1 + 2
T_SPRO = T_E1 + 16
T_SLOOP = T_SPRO + 7
T_SEND = T_SLOOP + 10 * (SG - 1)
T_O2 = T_SEND + 4
T_P2 = T_O2 + 32
T_E2 = T_P2 + 2
N_TILES = T_E2 + 16
N_HALF = 2 * N_TILES
N_ROUND, N_REST = N_HALF // 4, N_HALF % 4

C_NORM, C_PLE, C_FINAL, C_GNORM = 0, 32, 64, 80
C_GDT, C_GA, C_SDT, C_SA = 81, 82, 83, 84
C_SND = 85
N_PRM = C_SND + 2 * SX * SG
G_DVE_LINKS, S_DVE_LINKS = 34, 27
ARENA = 15900
K_ID, K_ONE, K_INC, K_M1, K_LEV = 0, 1, 2, 3, 4
K_BM = 10
K_ROW = 16
N_CST = 11


def bc(ap, axis, n):
    a = ap.unsqueeze(axis)
    shape = list(a.shape)
    shape[axis] = n
    return a.to_broadcast(shape)


def half(ap, lv, odd):
    v = ap.rearrange("p j (i k s) -> p j i k s", k=2, s=2 << lv)
    return v[:, :, :, odd, :]


def packed(ap, lv):
    return ap.rearrange("p (j i s) -> p j i s", j=2, s=2 << lv)


class Order:

    def __init__(self, eng, sem):
        self.eng, self.sem, self.base, self.n, self.m, self.per = eng, sem, 0, 0, 0, 0

    def enter(self, m, per):
        assert self.n == 0 or self.per == 0
        self.base, self.n, self.m, self.per = self.base + self.n, 0, m, per

    def leave(self, times):
        assert self.n == self.per, (self.n, self.per)
        self.base, self.n, self.m, self.per = self.base + self.per * times, 0, 0, 0

    def link(self, ins):
        self.n += 1
        ins.then_inc(self.sem, 1)
        self.eng.wait_ge(self.sem, self.m * self.per + (self.base + self.n))


def build(nc, weights, x_in, p_in, prm_in, cst_in, gpack, spack, gstate, sstate,
          y_out, gconv_out, sconv_out, gst_p, gst_s, sst_p, sst_s,
          g_rows, s_rows, h_spill, G_DVE, G_ACT, S_DVE, S_ACT):
    with ExitStack() as ctx:
        def sb(name, shape, dt=F32):
            return ctx.enter_context(nc.sbuf_tensor(name, shape, dt))

        def sem(name):
            return ctx.enter_context(nc.semaphore(name))

        ring = sb("ring", [P, 4, 8, P])
        wh = sb("wh", [P, 4, 8, P], F32R)
        wl = sb("wl", [P, 4, 8, P], F32R)
        xh = sb("xh", [P, KT, T], F32R)
        xl = sb("xl", [P, KT, T], F32R)
        Y = sb("Y", [P, 2 * KT, T])
        h = sb("h", [P, KT, T])
        cst = sb("cst", [P, N_CST, P])
        prm = sb("prm", [P, N_PRM])
        small = sb("small", [P, 16])
        ccol = sb("ccol", [P, 6 * SH])
        arena = sb("arena", [P, ARENA])

        psj = [ctx.enter_context(nc.psum_tensor(f"psj{i}", [P, 512], F32)) for i in range(2)]
        psA, psB, psC, psD, psE, psF = (
            ctx.enter_context(nc.psum_tensor(f"ps{c}", [P, 512], F32)) for c in "ABCDEF")

        def carve(sizes):
            out, at = {}, 0
            for name, n in sizes:
                out[name] = arena[:, at:at + n]
                at += n
            assert at <= ARENA, at
            return out

        ident, ones = cst[:, K_ID, :], cst[:, K_ONE, :]
        bmask = cst[0:NS, K_BM, 0:DEC_B]
        eps_c = small[:, 0:1]

        ga = carve([("U", 4 * UW), ("CR", 4 * T), ("KN", 2 * T), ("R", 2 * 3 * T), ("SQ", 2 * T), ("RS", 2 * T),
                    ("SQO", 2 * T), ("RSO", 2 * T),
                    ("pc", PC_G), ("co", 4 * CW), ("cc", 16), ("PR", 2 * NPAIR), ("DEC", 2 * NPAIR),
                    ("CQ", 2 * NPAIR), ("CK", 2 * NPAIR), ("W", 64), ("WD", 64), ("TM", 64), ("BE", 64),
                    ("DT", 512), ("AT", 512), ("DE", 1024), ("PP", 512), ("QK", 512), ("VB", 512),
                    ("VN", 512), ("VND", 512), ("KTK", 256), ("S1", 256), ("S2", 256), ("QD", 256),
                    ("O", 2 * T), ("ZS", 2 * T), ("WT", 256)])
        gU = ga["U"].rearrange("p (i u) -> p i u", i=4)
        gCR = ga["CR"].rearrange("p (i t) -> p i t", i=4)
        gKN = ga["KN"].rearrange("p (i t) -> p i t", i=2)
        gR = ga["R"].rearrange("p (j k t) -> p j k t", j=2, k=3)
        gSQ = ga["SQ"].rearrange("p (i t) -> p i t", i=2)
        gSQO = ga["SQO"].rearrange("p (i t) -> p i t", i=2)
        gRS = ga["RS"].rearrange("p (i t) -> p i t", i=2)
        gRSO = ga["RSO"].rearrange("p (i t) -> p i t", i=2)
        gpc = ga["pc"].rearrange("p (h c) -> p h c", h=2)
        gpc_cache = [gpc[:, n, 0:48].rearrange("p (i c) -> p i c", i=2) for n in range(2)]
        gpc_tap = [gpc[:, n, 48:56].rearrange("p (i c) -> p i c", i=2) for n in range(2)]
        gco = ga["co"].rearrange("p (i c) -> p i c", i=4)
        gcc = ga["cc"].rearrange("p (k c j) -> p k c j", k=4, c=NC)
        gPR, gDEC, gCQ, gCK = (ga[n].rearrange("p (i c) -> p i c", i=2) for n in ("PR", "DEC", "CQ", "CK"))
        gW, gWD, gTM, gBE = (ga[n].rearrange("p (i c) -> p i c", i=2) for n in ("W", "WD", "TM", "BE"))
        gDT, gAT, gP, gQK, gVB, gVN, gVND = (
            ga[n].rearrange("p (u t) -> p u t", u=4) for n in ("DT", "AT", "PP", "QK", "VB", "VN", "VND"))
        gDE = ga["DE"].rearrange("p (c k j t) -> p c k j t", c=NC, k=2, j=2)
        gKT = ga["KTK"].rearrange("p (c t) -> p c t", c=NC)
        gS1 = ga["S1"].rearrange("p (j t) -> p j t", j=2)
        gS2 = ga["S2"].rearrange("p (j t) -> p j t", j=2)
        gQD = ga["QD"].rearrange("p (j t) -> p j t", j=2)
        gO = ga["O"].rearrange("p (j t) -> p j t", j=2)
        gZS = ga["ZS"].rearrange("p (j t) -> p j t", j=2)
        gWT = ga["WT"]
        hf = h[:, :, :].rearrange("p k t -> p (k t)")
        gS = hf[:, 0:2048].rearrange("p (b j e) -> p b j e", b=DEC_B, j=2)
        gKM = hf[0:NS, 2048:3072].rearrange("p (b d) -> p b d", b=DEC_B)
        HRG = arena[:, ARENA - 9 * T:ARENA].rearrange("p (k t) -> p k t", k=9)

        sa = carve([("U", 6 * UW), ("CV", 6 * T), ("R2", HPG * T), ("RP", SX * 224), ("pc", PC_S),
                    ("co", 6 * CW), ("cc", 6 * HPG), ("ND", 2 * SX), ("PR", NPAIR), ("DEC", SX * NPAIR), ("DT", 1024),
                    ("X", 1024), ("XD", 512), ("CB", 256), ("BT", 256), ("XS", 128), ("XE", 128), ("TM", 128),
                    ("XT", 512), ("YT", SX * T), ("ZS", SX * T), ("EG", 80), ("BM", 1024), ("RT", T)])
        sU = sa["U"].rearrange("p (i u) -> p i u", i=6)
        sCV = sa["CV"].rearrange("p (i t) -> p i t", i=6)
        sR2 = sa["R2"].rearrange("p (h t) -> p h t", h=HPG)
        sRP = sa["RP"].rearrange("p (i c) -> p i c", i=SX)
        spc = sa["pc"].rearrange("p (i c) -> p i c", i=6)
        spc_norm, spc_D = sa["ND"][:, 0:SX], sa["ND"][:, SX:2 * SX]
        sco = sa["co"].rearrange("p (i c) -> p i c", i=6)
        scc = sa["cc"].rearrange("p (k c j) -> p k c j", k=3, c=NC)
        sPR = sa["PR"]
        sDEC = sa["DEC"].rearrange("p (i c) -> p i c", i=SX)
        sDT = sa["DT"].rearrange("p (h t) -> p h t", h=HPG)
        sX = sa["X"].rearrange("p (c h d) -> p c h d", c=NC, h=HPG)
        sXD = sa["XD"].rearrange("p (h d) -> p h d", h=HPG)
        sCB = sa["CB"].rearrange("p (c t) -> p c t", c=NC)
        sBT = sa["BT"].rearrange("p (c t) -> p c t", c=NC)
        sXS, sXE, sTM = (sa[n].rearrange("p (i t) -> p i t", i=SX) for n in ("XS", "XE", "TM"))
        sXT = sa["XT"]
        sYT = sa["YT"].rearrange("p (i t) -> p i t", i=SX)
        sZS = sa["ZS"].rearrange("p (i t) -> p i t", i=SX)
        sEGc = sa["EG"][:, 0:8]
        sEGb = sa["EG"][:, 8:72].rearrange("p (h b) -> p h b", h=HPG)
        sS = hf[:, 0:4096].rearrange("p (b h d) -> p b h d", b=DEC_B, h=HPG)
        sS1 = hf[:, 4096:4608]
        sBMv = sa["BM"][0:NS, :].rearrange("p (b n) -> p b n", b=DEC_B)
        sTMr = sa["RT"]

        da = carve([("SQ", 2 * T), ("SGM", 2 * T), ("TM", 2 * T), ("RSTD", T), ("RSE", T), ("pT", 2 * T)])
        dSQ, dSG, dTM = (da[n].rearrange("p (i t) -> p i t", i=2) for n in ("SQ", "SGM", "TM"))
        dRS, dRE = da["RSTD"], da["RSE"]
        dp = da["pT"].rearrange("p (k t) -> p k t", k=PLE_K)
        eb = Y[:, 0:KT, :]

        w_in = [sem(f"w_in{i}") for i in range(4)]
        wh_ready = sem("wh_ready")
        wl_ready = sem("wl_ready")
        half_done = sem("half_done")
        took_act = sem("took_act")
        took_dve = sem("took_dve")
        xh_ready = sem("xh_ready")
        xl_ready = sem("xl_ready")
        dve_order, act_order = sem("dve_order"), sem("act_order")
        c_in = sem("c_in")
        sems = {}

        def S(name):
            if name not in sems:
                sems[name] = sem(name)
            return sems[name]

        X0 = {"g": 0, "oa1": 16, "ob1": 32, "p1": 48, "e1": 50, "s": 66, "oa2": 82, "ob2": 98, "p2": 114, "e2": 116}
        TA_G = 0
        TA_E1 = T_GEND + 2
        TA_S = TA_E1 + 16
        TA_E2 = TA_S + (T_SEND + 4 - T_SPRO)
        TD_O1, TD_P1, TD_O2, TD_P2 = 0, 32, 48, 80

        block = ctx.enter_context(nc.Block())

        @block.sync
        def _(sp):
            for n in range(4):
                sp.dma_start(h[:, 4 * n:4 * n + 4, :], x_in[:, 4 * n:4 * n + 4, :]).then_inc(S(f"x_in{n}"), 16)
                if n == 0:
                    sp.dma_start(cst[:, :, :], cst_in).then_inc(c_in, 16)
                    sp.dma_start(prm[:, :], prm_in).then_inc(S("prm_in"), 16)
            for s in range(4):
                sp.dma_start(ring[:, s], weights[s]).then_inc(w_in[s], 16)

            def refill(r, s):
                sp.wait_ge(wl_ready, r * 4 + (s - 3))
                sp.dma_start(ring[:, s], weights[r * 4 + s]).then_inc(w_in[s], 16)

            with sp.Fori(1, N_ROUND) as r:
                for s in range(4):
                    refill(r, s)
            for s in range(N_REST):
                refill(N_ROUND, s)

        @block.gpsimd
        def _(pool):
            def lower(r, s):
                pool.wait_ge(wh_ready, r * 4 + (s + 1))
                pool.tensor_tensor(wl[:, s], ring[:, s], wh[:, s].bitcast(F32), ALU.subtract) \
                    .then_inc(wl_ready, 1)

            with pool.Fori(0, N_ROUND) as r:
                for s in range(4):
                    lower(r, s)
            for s in range(N_REST):
                lower(N_ROUND, s)

        @block.tensor
        def _(pe):
            def project(m, per, t0, e, fresh=None):
                hc = 2 * t0 + e // 4
                if e % 4 == 0:
                    pe.wait_ge(wl_ready, m * (2 * per) + (hc + 1))
                for kt in (2 * e, 2 * e + 1):
                    if fresh is not None:
                        pe.wait_ge(xl_ready, fresh + kt + 1)
                    w_h, w_l = wh[:, hc % 4, kt % 8, :], wl[:, hc % 4, kt % 8, :]
                    out = psj[t0 % 2][:, 0:T]
                    pe.matmul(out, w_h, xh[:, kt, :], start=(kt == 0), stop=False)
                    pe.matmul(out, w_h, xl[:, kt, :], start=False, stop=False)
                    mm = pe.matmul(out, w_l, xh[:, kt, :], start=False, stop=(kt == KT - 1))
                if e % 4 == 3:
                    mm.then_inc(half_done, 1)

            def col_sum(out, rhs, start=True, stop=True):
                return pe.matmul(out, ones, rhs, start=start, stop=stop)

            pe.wait_ge(c_in, 16)
            pe.wait_ge(S("prm_in"), 16)

            def norm_sum(n):
                for kt in range(KT):
                    pe.wait_ge(S("hsq"), n + kt + 1)
                    mm = col_sum(psA[:, 0:T], dSQ[:, kt % 2, :], start=(kt == 0), stop=(kt == KT - 1))
                    mm.then_inc(S("hss"), 1)

            def gdn_norm(m):
                pe.wait_ge(S("g_sq"), m + 1)
                col_sum(psE[:, 0:T], gSQ[:, 0, :])
                col_sum(psF[:, 0:T], gSQ[:, 1, :]).then_inc(S("g_ss"), 1)

            def gdn_mix(m, e, more):
                if e == 0:
                    pe.wait_ge(S("g_kn"), m + 1)
                    for c in range(NC):
                        k_c, q_c = (gKN[:, n, c * CH:(c + 1) * CH] for n in (1, 0))
                        pe.transpose(psA[:, c * P:(c + 1) * P], k_c, ident)
                        pe.matmul(psC[:, c * CH:(c + 1) * CH], k_c, k_c, start=True, stop=True)
                        pe.matmul(psC[:, 256 + c * CH:256 + (c + 1) * CH], k_c, q_c, start=True, stop=True)
                    pe.transpose(psE[0:NS, 0:P], gKN[:, 1, SEQ:T], ident).then_inc(S("g_tok"), 1)
                if e == 3:
                    pe.wait_ge(S("g_pr"), m + 1)
                    col_sum(psD[:, 0:2 * NPAIR], ga["PR"])
                    pe.wait_ge(S("g_st_in"), m * 16 + 16)
                    for b in range(DEC_B):
                        for j in range(2):
                            at = 160 + 16 * b + 8 * j
                            mm = pe.matmul(psD[:, at:at + 8], gS[:, b, j, :], gKN[:, 0:2, SEQ + b:T:DEC_B],
                                           start=True, stop=True)
                    mm.then_inc(S("g_smp"), 1)
                if e == 5:
                    pe.wait_ge(S("g_e1"), m + 1)
                    for c in range(NC):
                        for j in range(2):
                            mm = pe.transpose(psB[:, (2 * c + j) * P:(2 * c + j + 1) * P], gDE[:, c, 1, j, :], ident)
                    mm.then_inc(S("g_dt"), 1)

                def inv_p(c, lv):
                    if lv == 0:
                        pe.wait_ge(S("g_d"), m + 1)
                        pe.wait_ge(S("g_km"), m + 1)
                    else:
                        pe.wait_ge(S(f"g_de{c}"), m * 6 + lv)
                    for j in range(2):
                        mm = pe.matmul((psC, psE)[c][:, j * 64:(j + 1) * 64], gAT[:, 2 * c + j, :],
                                       half(gDE[:, c, 0], lv, 0)[:, j], start=True, stop=True)
                    mm.then_inc(S(f"g_p{c}"), 1)

                def inv_q(c, lv):
                    pe.wait_ge(S(f"g_pm{c}"), m * 6 + lv + 1)
                    bank = (psA, psF)[c]
                    if lv < 5:
                        for j in range(2):
                            pe.matmul(bank[:, j * 64:(j + 1) * 64], gDE[:, c, 1, j, :],
                                      half(gP[:, 2 * c:2 * c + 2], lv, 0)[:, j], start=True, stop=True)
                    for j in range(2):
                        mm = pe.matmul(bank[:, (2 + j) * 64:(3 + j) * 64], gP[:, 2 * c + j, :],
                                       half(gDE[:, c, 1], lv, 1)[:, j], start=True, stop=True)
                    mm.then_inc(S(f"g_q{c}"), 1)

                for lv in range(6):
                    if e == 7 + 2 * lv:
                        if lv > 0:
                            inv_q(1, lv - 1)
                        inv_p(0, lv)
                    if e == 8 + 2 * lv:
                        inv_p(1, lv)
                        inv_q(0, lv)
                if e == 19:
                    inv_q(1, 5)
                    pe.wait_ge(S("g_cv"), m + 1)
                    for c in range(NC):
                        for j in range(2):
                            mm = pe.transpose(psB[:, (2 * c + j) * P:(2 * c + j + 1) * P],
                                              gCR[:, 2 + j, c * CH:(c + 1) * CH], ident)
                    mm.then_inc(S("g_tokv"), 1)

                def new_values(c):
                    for j in range(2):
                        mm = pe.matmul(psC[:, j * P:(j + 1) * P], gDE[:, c, 1, j, :], gVB[:, 2 * c + j, :],
                                       start=True, stop=True)
                    mm.then_inc(S("g_vn"), 1)

                if e == 21:
                    pe.wait_ge(S("g_de0"), m * 6 + 6)
                    pe.wait_ge(S("g_vb"), m + 1)
                    new_values(0)
                if e == 24:
                    pe.wait_ge(S("g_vnd"), m * 2 + 1)
                    pe.wait_ge(S("g_de1"), m * 6 + 6)
                    pe.matmul(psE[:, 0:2 * P], gKT[:, 0, :], ga["VND"][:, 0:2 * P], start=True, stop=True) \
                        .then_inc(S("g_s"), 1)
                    for j in range(2):
                        pe.matmul(psF[:, j * SEQ:j * SEQ + CH], gVN[:, j, :], gQK[:, j, :], start=True, stop=True)
                if e == 26:
                    pe.wait_ge(S("g_s1"), m + 1)
                    pe.wait_ge(S("g_wd"), m + 1)
                    pe.matmul(psD[:, 0:2 * P], gKN[:, 1, CH:2 * CH], ga["S1"], start=True, stop=True) \
                        .then_inc(S("g_ks"), 1)
                    for j in range(2):
                        mm = pe.transpose(psB[0:NS, j * P:(j + 1) * P], gWD[:, j, :], ident)
                    mm.then_inc(S("g_wt"), 1)
                if e == 28:
                    pe.wait_ge(S("g_rhs"), m + 1)
                    new_values(1)
                if e == 30:
                    pe.wait_ge(S("g_vnd"), m * 2 + 2)
                    pe.matmul(psE[:, 0:2 * P], gKT[:, 1, :], ga["VND"][:, 2 * P:4 * P], start=True, stop=True) \
                        .then_inc(S("g_s"), 1)
                    for j in range(2):
                        o = psF[:, j * SEQ + CH:(j + 1) * SEQ]
                        pe.matmul(o, gS1[:, j, :], gQD[:, j, :], start=True, stop=False)
                        mm = pe.matmul(o, gVN[:, 2 + j, :], gQK[:, 2 + j, :], start=False, stop=True)
                    mm.then_inc(S("g_o"), 1)
                for i in range(4):
                    if e == 31 + i:
                        if i == 0:
                            pe.wait_ge(S("g_wtc"), m + 1)
                        if i >= 2:
                            pe.wait_ge(S("g_su"), m * 4 + i - 1)
                        bank = (psA, psB)[i % 2]
                        for b in (2 * i, 2 * i + 1):
                            at = (b % 2) * 256
                            mm = pe.matmul(bank[:, at:at + 256], gKM[:, b, :], gWT[0:NS, :], start=True, stop=True)
                        mm.then_inc(S("g_sp"), 1)
                if e == 35:
                    pe.wait_ge(S("g_osq"), m + 1)
                    col_sum(psC[:, 0:T], gSQO[:, 0, :])
                    col_sum(psD[:, 0:T], gSQO[:, 1, :]).then_inc(S("g_os"), 1)
                if e == 38 and more:
                    pe.wait_ge(S("g_s2"), m + 1)
                    gdn_norm(m + 1)

            def bank_wait_act(m, per, t0, phase_t, took0):
                pe.wait_ge(took_act, m * per + (took0 + t0 - phase_t - 1))

            norm_sum(0)
            for k in range(6):
                if k >= 2:
                    bank_wait_act(0, 0, T_GPRO + k, T_GPRO, TA_G)
                for e in range(8):
                    project(0, 0, T_GPRO + k, e, fresh=X0["g"] if k == 0 else None)
                if k == 3:
                    gdn_norm(0)
            pe.wait_ge(S("g_hrows"), 1)
            for n in range(4):
                for c in range(NC):
                    src = HRG[0:GV, (7, 3, 4, 5)[n], c * CH:(c + 1) * CH]
                    at = (n * NC + c) * GV
                    mm = pe.transpose(psD[:, at:at + GV], src, ident[0:GV, 0:GV])
            mm.then_inc(S("g_ccol"), 1)
            with pe.Fori(0, GH - 1) as m:
                for e in range(48):
                    if e % 8 == 0:
                        bank_wait_act(m, 6, T_GLOOP + e // 8, T_GPRO, TA_G)
                    project(m, 6, T_GLOOP + e // 8, e % 8)
                    gdn_mix(m, e, True)
            for e in range(48):
                k = e // 8
                if e % 8 == 0:
                    if k < 4:
                        bank_wait_act(0, 0, T_GEND + k, T_GPRO, TA_G)
                    else:
                        pe.wait_ge(took_dve, TD_O1 + (k - 3))
                project(0, 0, T_GEND + k, e % 8, fresh=X0["oa1"] if k == 2 else None)
                if e < 16:
                    gdn_mix(GH - 1, e, False)
                elif e >= 20:
                    gdn_mix(GH - 1, e - 4, False)

            def dense(t0, x0, first_free, sem_took, took0, last=None):
                for k in range(2):
                    first_free(k)
                    for e in range(8):
                        project(0, 0, t0 + k, e, fresh=x0 if k == 0 else None)
                with pe.Fori(1, KT // 2) as i:
                    for k in range(2):
                        pe.wait_ge(sem_took, i * 2 + (took0 + k - 1))
                        for e in range(8):
                            project(i, 2, t0 + k, e)
                        if last is not None:
                            last(i, k)

            def out_proj(t0, xb, td, first):
                with pe.Fori(first // 2, KT // 2) as i:
                    for k in range(2):
                        pe.wait_ge(took_dve, i * 2 + (td + k - 1))
                        for e in range(8):
                            project(i, 2, t0 + k, e)
                dense(t0 + 16, xb, lambda k: pe.wait_ge(took_dve, td + 15 + k), took_dve, td + 16)

            def ple(tp, te, xp, xe, td, ta, hs, es, hq):
                for i in range(KT):
                    a, hc = i // 8, 2 * (tp + i // 8) + (i % 8) // 4
                    if i % 4 == 0:
                        pe.wait_ge(wl_ready, hc + 1)
                    pe.wait_ge(took_dve, td + i - 1)
                    out = psj[(tp + i) % 2][:, 0:T]
                    for kt in range(PLE_K):
                        if i == 0:
                            pe.wait_ge(xl_ready, xp + kt + 1)
                        at = (2 * i + kt) % 8
                        pe.matmul(out, wh[:, hc % 4, at, :], xh[:, kt, :], start=(kt == 0), stop=False)
                        pe.matmul(out, wh[:, hc % 4, at, :], xl[:, kt, :], start=False, stop=False)
                        mm = pe.matmul(out, wl[:, hc % 4, at, :], xh[:, kt, :], start=False, stop=(kt == PLE_K - 1))
                    if i % 4 != 3:
                        mm.then_inc(S("e_done"), 1)
                    else:
                        mm.then_inc(half_done, 1)
                    if i >= 1:
                        pe.wait_ge(S("esq"), es + i)
                        col_sum(psB[:, 0:T], dSQ[:, (i - 1) % 2, :], start=(i == 1), stop=False) \
                            .then_inc(S("ess"), 1)
                pe.wait_ge(S("esq"), es + KT)
                col_sum(psB[:, 0:T], dSQ[:, (KT - 1) % 2, :], start=False, stop=True).then_inc(S("ess"), 1)

                def add_sum(i, k):
                    pe.wait_ge(S("hsq"), i * 2 + (hq + k - 1))
                    col_sum(psA[:, 0:T], dSQ[:, k, :], start=False, stop=False).then_inc(S("hss"), 1)

                for k in range(2):
                    pe.wait_ge(took_dve, td + KT)
                    for e in range(8):
                        project(0, 0, te + k, e, fresh=xe if k == 0 else None)
                for k in range(2, 4):
                    pe.wait_ge(took_act, ta + k - 1)
                    for e in range(8):
                        project(0, 0, te + k, e)
                    pe.wait_ge(S("hsq"), hq + k - 1)
                    col_sum(psA[:, 0:T], dSQ[:, k % 2, :], start=(k == 2), stop=False).then_inc(S("hss"), 1)
                with pe.Fori(2, KT // 2) as i:
                    for k in range(2):
                        pe.wait_ge(took_act, i * 2 + (ta + k - 1))
                        for e in range(8):
                            project(i, 2, te + k, e)
                        add_sum(i, k)
                for k in range(2):
                    pe.wait_ge(S("hsq"), hq + 15 + k)
                    col_sum(psA[:, 0:T], dSQ[:, k, :], start=False, stop=(k == 1)).then_inc(S("hss"), 1)

            out_proj(T_O1, X0["ob1"], TD_O1, 4)
            ple(T_P1, T_E1, X0["p1"], X0["e1"], TD_P1, TA_E1, 16, 0, 16)

            def ssd_mix(m, e):
                if e == 21:
                    pe.wait_ge(S("s_cv"), m + 1)
                    pe.wait_ge(S("s_yd"), m + 1)
                    for c in range(NC):
                        pe.transpose(psA[:, c * P:(c + 1) * P], sCV[:, 0, c * CH:(c + 1) * CH], ident)
                        bank = (psB, psC)[c]
                        for i in range(SX):
                            pe.transpose(bank[:, i * P:(i + 1) * P], sCV[:, 2 + i, c * CH:(c + 1) * CH], ident)
                        pe.matmul(psD[:, c * CH:(c + 1) * CH], sCV[:, 0, c * CH:(c + 1) * CH],
                                  sCV[:, 1, c * CH:(c + 1) * CH], start=True, stop=True)
                    pe.transpose(psE[0:NS, 0:P], sCV[:, 0, SEQ:T], ident).then_inc(S("s_tok"), 1)
                if e == 24:
                    pe.wait_ge(S("s_pr"), m + 1)
                    col_sum(psF[:, 0:NPAIR], sPR)
                    pe.wait_ge(S("s_st_in"), m * 64 + 64)
                    for b in range(DEC_B):
                        for i in range(SX):
                            at = P + (i * DEC_B + b) * DEC_T
                            mm = pe.matmul(psF[:, at:at + DEC_T], sS[:, b, 2 * i:2 * i + 2, :],
                                           sCV[:, 1, SEQ + b:T:DEC_B], start=True, stop=True)
                    mm.then_inc(S("s_smp"), 1)
                if e == 27:
                    pe.wait_ge(S("s_xd"), m * 2 + 1)
                    pe.wait_ge(S("s_btc"), m + 1)
                    pe.matmul(psA[:, :], sBT[:, 0, :], sa["XD"], start=True, stop=True).then_inc(S("s_s"), 1)
                for c in range(NC):
                    if e == (31, 39)[c]:
                        pe.wait_ge(S("s_w"), m * 2 + c + 1)
                        for i in range(SX):
                            for j in range(2):
                                mm = pe.matmul((psB, psC)[c][HD * j:HD * j + HD, i * P:(i + 1) * P],
                                               sX[:, c, 2 * i + j, :], sDT[:, 2 * i + j, :], start=True, stop=True)
                        mm.then_inc(S("s_y"), 1)
                if e == 35:
                    pe.wait_ge(S("s_s1"), m + 1)
                    for i in range(SX):
                        mm = pe.matmul(psD[:, i * P:(i + 1) * P], sS1[:, i * P:(i + 1) * P],
                                       sCV[:, 1, CH:2 * CH], start=True, stop=True)
                    mm.then_inc(S("s_off"), 1)
                    pe.wait_ge(S("s_xd"), m * 2 + 2)
                    pe.matmul(psA[:, :], sBT[:, 1, :], sa["XD"], start=True, stop=True).then_inc(S("s_s"), 1)
                if e == 42:
                    pe.wait_ge(S("s_xe"), m + 1)
                    for i in range(SX):
                        mm = pe.transpose(psE[0:NS, i * P:(i + 1) * P], sXE[:, i, :], ident)
                    mm.then_inc(S("s_xt"), 1)
                for b in range(DEC_B):
                    if e == 46 + 2 * b:
                        if b == 0:
                            pe.wait_ge(S("s_xtc"), m + 1)
                            pe.wait_ge(S("s_yt"), m + 1)
                        if b >= 2:
                            pe.wait_ge(S("s_su"), m * 8 + b - 1)
                        pe.matmul((psA, psF)[b % 2][:, :], sBMv[:, b, :], sXT[0:NS, :], start=True, stop=True) \
                            .then_inc(S("s_sp"), 1)
                if e == 68:
                    pe.wait_ge(S("s_sq"), m + 1)
                    for i in range(SX):
                        mm = col_sum(psE[:, 0:T], sZS[:, i, :], start=(i == 0), stop=(i == SX - 1))
                    mm.then_inc(S("s_ss"), 1)

            for k in range(7):
                bank_wait_act(0, 0, max(T_SPRO + k, T_SPRO + 1), T_SPRO, TA_S)
                for e in range(8):
                    project(0, 0, T_SPRO + k, e, fresh=X0["s"] if k == 0 else None)
                if k == 4:
                    pe.wait_ge(S("s_hrows"), 1)
                    for n in range(3):
                        for c in range(NC):
                            src = HRG[0:SH, (4, 3, 5)[n], c * CH:(c + 1) * CH]
                            at = (n * NC + c) * SH
                            mm = pe.transpose(psA[:, at:at + SH], src, ident[0:SH, 0:SH])
                    mm.then_inc(S("s_ccol"), 1)
            with pe.Fori(0, SG - 1) as m:
                for e in range(80):
                    if e % 8 == 0:
                        bank_wait_act(m, 10, T_SLOOP + e // 8, T_SPRO, TA_S)
                    project(m, 10, T_SLOOP + e // 8, e % 8)
                    ssd_mix(m, e)
            for e in range(80):
                k = e // 8
                if e % 8 == 0:
                    if k < SX + 2:
                        bank_wait_act(0, 0, T_SEND + k, T_SPRO, TA_S)
                    else:
                        pe.wait_ge(took_dve, TD_O2 + (k - SX - 1))
                project(0, 0, T_SEND + k, e % 8, fresh=X0["oa2"] if k == SX else None)
                ssd_mix(SG - 1, e)

            out_proj(T_O2, X0["ob2"], TD_O2, 6)
            ple(T_P2, T_E2, X0["p2"], X0["e2"], TD_P2, TA_E2, 32, 16, 32)

        @block.scalar
        def _(act):
            ao = Order(act, act_order)

            def upper(m, per, hc):
                act.wait_ge(w_in[hc % 4], m * (4 * per) + 16 * (hc // 4 + 1))
                if hc >= 4:
                    act.wait_ge(half_done, m * per + (hc - 3))
                act.activation(wh[:, hc % 4], ring[:, hc % 4], ACT.Copy).then_inc(wh_ready, 1)

            def ahead(m, per, t):
                upper(m, 2 * per, 2 * t)
                upper(m, 2 * per, 2 * t + 1)

            def tile_wait(m, per, t):
                act.wait_ge(half_done, m * (2 * per) + 2 * t + 2)

            def split_x(src, n, t0):
                if t0:
                    act.wait_ge(half_done, 2 * t0)
                for kt in range(n):
                    act.activation(xh[:, kt, :], src(kt), ACT.Copy).then_inc(xh_ready, 1)

            def normed_x(base, t0, t_next):
                act.wait_ge(S("hss"), base + KT)
                act.activation(dRS, psA[:, 0:T], ACT.Sqrt, bias=eps_c, scale=1.0 / D_MODEL) \
                    .then_inc(S("n_root"), 1)
                if t0:
                    act.wait_ge(half_done, 2 * t0)
                for kt in range(KT):
                    if kt == KT // 2:
                        ahead(0, 0, t_next)
                    act.wait_ge(S("xn"), base + kt + 1)
                    act.activation(xh[:, kt, :], dTM[:, kt % 2, :], ACT.Copy).then_inc(xh_ready, 1)

            def softplus_rows(n, dtc, ac, tile_t, pre, took):
                tile_wait(0, 0, tile_t)
                act.activation(HRG[0:n, 0, :], psj[tile_t % 2][0:n, 0:T], ACT.Identity,
                               bias=prm[0:n, dtc:dtc + 1]).then_inc(took_act, 1)
                ahead(0, 0, tile_t + 2)
                act.wait_ge(took_act, took + 1)
                ao.link(act.activation(HRG[0:n, 1, :], HRG[0:n, 0, :], ACT.Abs))
                act.activation(small[0:n, 2:3], prm[0:n, ac:ac + 1], ACT.Exp)
                act.activation(HRG[0:n, 1, :], HRG[0:n, 1, :], ACT.Exp, scale=-1.0).then_inc(S(pre + "exp"), 1)

            def softplus_log(n, pre):
                act.wait_ge(S(pre + "w1"), 1)
                act.activation(HRG[0:n, 3, :], HRG[0:n, 2, :], ACT.Ln).then_inc(S(pre + "ln"), 1)

            def decay_rows(n, pre):
                act.wait_ge(S(pre + "cum"), 1)
                act.activation(HRG[0:n, 8, :], HRG[0:n, 6, :], ACT.Exp)
                act.activation(HRG[0:n, 5, 0:SEQ], HRG[0:n, 1, 0:SEQ], ACT.Exp).then_inc(S(pre + "eg"), 1)

            act.wait_ge(S("prm_in"), 16)
            act.wait_ge(S("konst"), 1)
            act.dma_start(gpc[:, 0, :], gpack[0, 0]).then_inc(S("g_pq_in"), 16)
            for kt in range(KT):
                if kt % 4 == 0:
                    act.wait_ge(S(f"x_in{kt // 4}"), 16)
                if kt >= 2:
                    act.wait_ge(S("hss"), kt - 1)
                act.activation(dSQ[:, kt % 2, :], h[:, kt, :], ACT.Square).then_inc(S("hsq"), 1)
            ahead(0, 0, 0)
            normed_x(0, 0, 1)
            act.dma_start(h_spill, h[:, :, :]).then_inc(S("spill"), 16)

            def take_u(i, U):
                return lambda bank: (act.activation(U[:, i, UP:UC], bank[:, 0:SEQ], ACT.Copy),
                                     act.activation(U[:, i, US:UW], bank[:, SEQ:T], ACT.Copy))[1]

            def g_load(m):
                act.dma_start(ga["R"], g_rows[m].partition_broadcast(P)).then_inc(S("g_r_in"), 16)
                act.dma_start(gpc[:, 1, :], gpack[m, 1]).then_inc(S("g_pv_in"), 16)
                act.dma_start(hf[:, 0:2048], gstate[m]).then_inc(S("g_st_in"), 16)

            def g_load_qk(m):
                act.dma_start(gpc[:, 0, :], gpack[m, 0]).then_inc(S("g_pq_in"), 16)

            def g_qk_silu(m):
                act.wait_ge(S("g_convq"), m + 1)
                act.dma_start(gconv_out[m, 0], gco[:, 0:2, :]).then_inc(S("g_cq_out"), 16)
                act.activation(gCR[:, 0:2, :], gCR[:, 0:2, :], ACT.Silu).then_inc(S("g_qk"), 1)
                act.wait_ge(S("g_qk"), m + 1)
                act.activation(gSQ[:, :, :], gCR[:, 0:2, :], ACT.Square).then_inc(S("g_sq"), 1)

            def g_qk_roots(m):
                act.wait_ge(S("g_ss"), m + 1)
                g_roots(gRS, psE, psF, 1.0).then_inc(S("g_rs"), 1)

            def g_roots(dst, bank0, bank1, scale):
                act.activation(dst[:, 1, :], bank1[:, 0:T], ACT.Sqrt, bias=eps_c, scale=scale)
                return act.activation(dst[:, 0, :], bank0[:, 0:T], ACT.Sqrt, bias=eps_c, scale=scale)

            def take(k, i):
                tile_wait(0, 0, k)
                take_u(i, gU)(psj[k % 2]).then_inc(took_act, 1)
                ahead(0, 0, k + 2)

            take(0, 0)
            take(1, 1)
            softplus_rows(GV, C_GDT, C_GA, 2, "g_", TA_G + 2)
            g_qk_silu(0)
            softplus_log(GV, "g_")
            tile_wait(0, 0, 3)
            act.activation(HRG[0:GV, 7, :], psj[1][0:GV, 0:T], ACT.Sigmoid).then_inc(took_act, 1)
            ahead(0, 0, 5)
            g_qk_roots(0)
            decay_rows(GV, "g_")
            act.wait_ge(S("g_hrows"), 1)
            act.dma_start(g_rows.rearrange("m (j c) -> (m j) c", j=2), HRG[0:GV, 6:9, :]) \
                .then_inc(S("g_rows_out"), 16)
            take(4, 2)
            act.wait_ge(S("g_rows_out"), 16)
            act.wait_ge(S("spill"), 16)
            g_load(0)
            take(5, 3)
            act.wait_ge(S("g_ccol"), 1)
            act.activation(ccol[:, 0:256], psD[:, 0:256], ACT.Copy).then_inc(S("g_ccolc"), 1)

            def gdn_body(m, full):
                per = 6 if full else 0
                zt = T_GLOOP + 2 if full else T_GEND

                def take_z(j):
                    tile_wait(m if full else 0, per, zt + j)
                    act.activation(gZS[:, j, :], psj[(zt + j) % 2][:, 0:T], ACT.Silu).then_inc(took_act, 1)

                if full:
                    act.wait_ge(S("g_cq_out"), m * 16 + 16)
                    g_load_qk(m + 1)
                act.wait_ge(S("g_dtx"), m + 1)
                act.activation(ga["DT"], ga["DT"], ACT.Exp)
                act.activation(ga["DEC"], ga["DEC"], ACT.Exp).then_inc(S("g_dte"), 1)
                act.wait_ge(S("g_tok"), m + 1)
                act.activation(ga["KTK"], psA[:, 0:2 * P], ACT.Copy)
                act.wait_ge(S("g_dt"), m + 1)
                act.activation(gDE[:, :, 0, :, :], psB[:, :].rearrange("p (c j t) -> p c j t", c=NC, j=2), ACT.Copy) \
                    .then_inc(S("g_d"), 1)
                if full:
                    tile_wait(m, per, T_GLOOP)
                    take_u(0, gU)(psj[T_GLOOP % 2]).then_inc(took_act, 1)
                    ahead(m, per, T_GLOOP + 2)
                else:
                    take_z(0)
                    ahead(0, 0, T_O1)
                if full:
                    tile_wait(m, per, T_GLOOP + 1)
                    take_u(1, gU)(psj[(T_GLOOP + 1) % 2]).then_inc(took_act, 1)
                    ahead(m, per, T_GLOOP + 3)
                else:
                    take_z(1)
                act.wait_ge(S("g_convv"), m + 1)
                act.dma_start(gconv_out[m, 1], gco[:, 2:4, :]).then_inc(S("g_cv_out"), 16)
                act.activation(gCR[:, 2:4, :], gCR[:, 2:4, :], ACT.Silu).then_inc(S("g_cv"), 1)
                if not full:
                    split_x(lambda kt: Y[:, kt, :], KT, T_O1)
                    ahead(0, 0, T_O1 + 1)
                act.wait_ge(S("g_tokv"), m + 1)
                for c in range(NC):
                    for j in range(2):
                        u = 2 * c + j
                        ins = act.activation(gVB[:, u, :], psB[:, u * P:(u + 1) * P], ACT.Copy,
                                             scale=gcc[:, 0, c, j:j + 1])
                ins.then_inc(S("g_vb"), 1)

                def values(c):
                    act.wait_ge(S("g_vn"), m * 2 + c + 1)
                    act.activation(gVN[:, 2 * c:2 * c + 2, :], psC[:, 0:2 * P].rearrange("p (j t) -> p j t", j=2),
                                   ACT.Copy)
                    for j in range(2):
                        ins = act.activation(gVND[:, 2 * c + j, :], psC[:, j * P:(j + 1) * P], ACT.Copy,
                                             scale=gcc[:, 3, c, j:j + 1])
                    ins.then_inc(S("g_vnd"), 1)

                values(0)
                if full:
                    take_z(0)
                    ahead(m, per, T_GLOOP + 4)
                else:
                    ahead(0, 0, T_O1 + 2)
                act.wait_ge(S("g_s"), m * 2 + 1)
                act.activation(ga["S1"], psE[:, 0:2 * P], ACT.Copy).then_inc(S("g_s1"), 1)
                act.wait_ge(S("g_wt"), m + 1)
                act.activation(gWT[0:NS, :], psB[0:NS, 0:2 * P], ACT.Copy).then_inc(S("g_wtc"), 1)
                values(1)
                if not full:
                    ahead(0, 0, T_O1 + 3)
                act.wait_ge(S("g_o"), m + 1)
                ao.link(act.activation(gO[:, :, 0:SEQ], psF[:, :].rearrange("p (j t) -> p j t", j=2), ACT.Copy))
                act.wait_ge(S("g_os_dve"), m + 1)
                act.activation(ga["SQO"], ga["O"], ACT.Square).then_inc(S("g_osq"), 1)
                if full:
                    take_z(1)
                    ahead(m, per, T_GLOOP + 5)
                    g_qk_silu(m + 1)
                act.wait_ge(S("g_os"), m + 1)
                g_roots(gRSO, psC, psD, 1.0 / P).then_inc(S("g_rs2"), 1)
                if not full:
                    ahead(0, 0, T_O1 + 4)
                act.wait_ge(S("g_s2"), m + 1)
                act.dma_start(gst_p[m], ga["S2"]).then_inc(S("g_sp_out"), 16)
                act.wait_ge(S("g_su"), m * 4 + 4)
                act.dma_start(gst_s[m], hf[:, 0:2048]).then_inc(S("g_st_out"), 16)
                if full:
                    g_qk_roots(m + 1)
                    tile_wait(m, per, T_GLOOP + 4)
                    take_u(2, gU)(psj[T_GLOOP % 2]).then_inc(took_act, 1)
                    ahead(m, per, T_GLOOP + 6)
                act.wait_ge(S("g_y"), m + 2)
                act.wait_ge(S("g_st_out"), m * 16 + 16)
                act.wait_ge(S("g_sp_out"), m * 16 + 16)
                act.wait_ge(S("g_cv_out"), m * 16 + 16)
                if full:
                    g_load(m + 1)
                    tile_wait(m, per, T_GLOOP + 5)
                    take_u(3, gU)(psj[(T_GLOOP + 5) % 2]).then_inc(took_act, 1)
                    ahead(m, per, T_GLOOP + 7)

            with act.Fori(0, GH - 1) as m:
                ao.enter(m, G_ACT)
                gdn_body(m, True)
            ao.leave(GH - 1)
            gdn_body(GH - 1, False)
            act.dma_start(h[:, :, :], h_spill).then_inc(S("h_back"), 16)

            def dense(t0, src):
                split_x(src, KT, t0)
                ahead(0, 0, t0 + 1)
                with act.Fori(0, KT // 2 - 1) as i:
                    for k in range(2):
                        ahead(i, 2, t0 + 2 + k)
                ahead(0, 0, t0 + KT)

            def ple(tp, te, es, hq, hbase, td, end):
                act.wait_ge(S("p_in"), 16 + es)
                split_x(lambda kt: dp[:, kt, :], PLE_K, tp)
                ahead(0, 0, tp + 1)
                for i in range(KT):
                    if i == 7:
                        ahead(0, 0, te)
                    act.wait_ge(took_dve, td + i + 1)
                    if i >= 2 or es:
                        act.wait_ge(S("ess"), es + i - 1)
                    act.activation(dSQ[:, i % 2, :], eb[:, i, :], ACT.Square).then_inc(S("esq"), 1)
                act.wait_ge(S("ess"), es + KT)
                act.activation(dRE, psB[:, 0:T], ACT.Sqrt, bias=eps_c, scale=1.0 / D_MODEL) \
                    .then_inc(S("e_root"), 1)

                def gate(i, k):
                    act.wait_ge(half_done, i * 4 + 2 * (te + k) + 2)
                    act.wait_ge(S("hnew"), i * 2 + (hq - 16 + k - 1)) if hq - 16 + k - 1 > 0 else None
                    act.activation(dSG[:, k % 2, :], psj[(te + k) % 2][:, 0:T], ACT.Sigmoid).then_inc(took_act, 1)

                def square(i, k):
                    act.wait_ge(S("hnew"), i * 2 + (hq - 16 + k + 1))
                    act.wait_ge(S("hss"), i * 2 + (hq + k - 1))
                    act.activation(dSQ[:, k % 2, :], h[:, (i * 2 + k), :], ACT.Square).then_inc(S("hsq"), 1)

                act.wait_ge(took_dve, td)
                split_x(lambda kt: h[:, kt, :], KT, te)
                ahead(0, 0, te + 1)
                gate(0, 0)
                ahead(0, 0, te + 2)
                gate(0, 1)
                square(0, 0)
                with act.Fori(0, KT // 2 - 2) as i:
                    for k in range(2):
                        ahead(i, 2, te + 3 + k)
                        gate(i, 2 + k)
                        square(i, 1 + k)
                ahead(0, 0, te + KT - 1)
                gate(0, KT - 2)
                square(0, KT - 3)
                if not end:
                    ahead(0, 0, te + KT)
                gate(0, KT - 1)
                square(0, KT - 2)
                square(0, KT - 1)

            def out_proj(t0, first):
                with act.Fori(0, (KT - first) // 2) as i:
                    for k in range(2):
                        ahead(i, 2, t0 + first + 1 + k)
                dense(t0 + KT, lambda kt: Y[:, KT + kt, :])

            act.wait_ge(S("g_y"), GH + 1)
            out_proj(T_O1, 4)
            act.dma_start(dp[:, :, :], p_in[0]).then_inc(S("p_in"), 16)
            ple(T_P1, T_E1, 0, 16, 16, TD_P1, False)

            normed_x(16, T_SPRO, T_SPRO + 1)
            act.dma_start(h_spill, h[:, :, :]).then_inc(S("spill"), 16)
            softplus_rows(SH, C_SDT, C_SA, T_SPRO, "s_", TA_S)

            def s_load_rows(m):
                act.dma_start(sa["R2"].rearrange("p (h t) -> p h t", h=HPG),
                              s_rows[m].rearrange("h c -> (h c)").partition_broadcast(P)
                              .rearrange("p (h c) -> p h c", h=HPG)[:, :, 0:T]).then_inc(S("s_r_in"), 16)
                for j in range(2):
                    act.dma_start(sRP[HD * j:HD * j + HD, :, :],
                                  s_rows[m].rearrange("h c -> (h c)").partition_broadcast(HD)
                                  .rearrange("p (i j c) -> p i j c", i=SX, j=2)[:, :, j, 256:480]) \
                        .then_inc(S("s_rp_in"), 16)

            def s_load_pack(m):
                act.dma_start(sa["pc"], spack[m]).then_inc(S("s_pc_in"), 16)

            def s_states_in(m, i):
                a = slice(1024 * i, 1024 * (i + 1))
                act.dma_start(hf[:, a], sstate[m, :, a]).then_inc(S("s_st_in"), 16)

            def s_states_out(m, i):
                a = slice(1024 * i, 1024 * (i + 1))
                act.wait_ge(S("s_su"), m * 8 + (2 * i + 2))
                act.dma_start(sst_s[m, :, a], hf[:, a]).then_inc(S(f"s_st_out{i}"), 16)

            def s_states_next(m, i, full):
                act.wait_ge(S(f"s_st_out{i}"), m * 16 + 16)
                if full:
                    s_states_in(m + 1, i)

            softplus_log(SH, "s_")
            s_load_pack(0)
            sr = s_rows.rearrange("g h c -> (g h) c")
            for k in range(1, 7):
                tile_wait(0, 0, T_SPRO + k)
                take_u(k - 1, sU)(psj[(T_SPRO + k) % 2]).then_inc(took_act, 1)
                ahead(0, 0, T_SPRO + k + 2)
                if k == 3:
                    decay_rows(SH, "s_")
                    act.wait_ge(S("s_hrows"), 1)
                    act.dma_start(sr[:, 0:T], HRG[0:SH, 6, :]).then_inc(S("s_rows_out"), 16)
                    act.dma_start(sr[:, T:T + 160], HRG[0:SH, 8, 128:T]).then_inc(S("s_rows_out"), 16)
                    act.dma_start(sr[:, T + 160:T + 192], HRG[0:SH, 4, SEQ:T]).then_inc(S("s_rows_out"), 16)
                if k == 4:
                    act.wait_ge(S("s_rows_out"), 48)
                    s_load_rows(0)
                    act.wait_ge(S("spill"), 32)
                    for i in range(4):
                        s_states_in(0, i)
                if k == 5:
                    act.wait_ge(S("s_ccol"), 1)
                    act.activation(ccol[:, 0:384], psA[:, 0:384], ACT.Copy).then_inc(S("s_ccolc"), 1)

            def ssd_body(m, full):
                per, t0 = (10, T_SLOOP) if full else (0, T_SEND)
                mt = m if full else 0
                z_of = {0: 0, 1: 1, 6: 2, 7: 3} if full else {0: 0, 1: 1, 2: 2, 3: 3}
                u_of = {2: 0, 3: 1, 4: 2, 5: 3, 8: 4, 9: 5} if full else {}

                def took(k):
                    tile_wait(mt, per, t0 + k)
                    bank = psj[(t0 + k) % 2]
                    if k in u_of:
                        take_u(u_of[k], sU)(bank).then_inc(took_act, 1)
                    if k in z_of:
                        act.activation(sZS[:, z_of[k], :], bank[:, 0:T], ACT.Silu).then_inc(took_act, 1)
                    if not full and k == SX - 1:
                        split_x(lambda kt: Y[:, kt, :], KT, T_O2)
                    ahead(mt, per, t0 + k + 2)

                took(0)
                took(1)
                act.wait_ge(S("s_conv"), m + 1)
                for i in range(6):
                    ins = act.activation(sCV[:, i, :], sCV[:, i, :], ACT.Silu, bias=spc[:, i, 28:29])
                ins.then_inc(S("s_cv"), 1)
                act.wait_ge(S("s_tok"), m + 1)
                act.activation(sa["BT"], psA[:, 0:2 * P], ACT.Copy).then_inc(S("s_btc"), 1)
                act.wait_ge(S("s_r_in"), m * 16 + 16)
                act.activation(sEGc, sR2[:, :, SEQ - 1], ACT.Exp)
                act.activation(sEGb, sR2[:, :, T - DEC_B:T], ACT.Exp)
                act.wait_ge(S("s_decx"), m + 1)
                act.activation(sa["DEC"], sa["DEC"], ACT.Exp).then_inc(S("s_dec"), 1)
                act.wait_ge(S("s_dtx"), m * 2 + 1)
                act.activation(sa["DT"], sa["DT"], ACT.Exp).then_inc(S("s_dt"), 1)
                if full:
                    act.wait_ge(S("s_cv"), m + 1)
                    s_load_pack(m + 1)
                took(2)
                act.wait_ge(S("s_s"), m * 2 + 1)
                act.activation(sS1, psA[:, :], ACT.Copy).then_inc(S("s_s1"), 1)
                took(3)
                act.wait_ge(S("s_dtx"), m * 2 + 2)
                act.activation(sa["DT"], sa["DT"], ACT.Exp).then_inc(S("s_dt"), 1)
                act.wait_ge(S("s_y"), m * 2 + 1)
                act.activation(sYT[:, :, 0:CH], psB[:, :].rearrange("p (i t) -> p i t", i=SX), ACT.Copy) \
                    .then_inc(S("s_y0"), 1)
                took(4)
                act.wait_ge(S("s_xt"), m + 1)
                act.wait_ge(S("s_bm"), m + 1)
                act.activation(sXT[0:NS, :], psE[0:NS, :], ACT.Copy).then_inc(S("s_xtc"), 1)
                act.wait_ge(S("s_s2"), m + 1)
                act.dma_start(sst_p[m], sS1).then_inc(S("s_sp_out"), 16)
                act.dma_start(sconv_out[m], sa["co"]).then_inc(S("s_co_out"), 16)
                if full:
                    s_load_rows(m + 1)
                took(5)
                s_states_out(m, 0)
                took(6)
                s_states_out(m, 1)
                s_states_next(m, 0, full)
                took(7)
                s_states_out(m, 2)
                s_states_out(m, 3)
                act.wait_ge(S("s_g"), m + 1)
                act.activation(sa["ZS"], sa["YT"], ACT.Square).then_inc(S("s_sq"), 1)
                s_states_next(m, 1, full)
                act.wait_ge(S("s_ss"), m + 1)
                act.activation(sTMr, psE[:, 0:T], ACT.Sqrt, bias=eps_c, scale=1.0 / (SX * P)).then_inc(S("s_root"), 1)
                took(8)
                s_states_next(m, 2, full)
                s_states_next(m, 3, full)
                act.wait_ge(S("s_sp_out"), m * 16 + 16)
                act.wait_ge(S("s_co_out"), m * 16 + 16)
                if full:
                    took(9)
                act.wait_ge(S("s_yd"), m + 2)

            with act.Fori(0, SG - 1) as m:
                ao.enter(m, S_ACT)
                ssd_body(m, True)
            ao.leave(SG - 1)
            ssd_body(SG - 1, False)
            act.dma_start(h[:, :, :], h_spill).then_inc(S("h_back"), 16)
            act.wait_ge(S("s_yd"), SG + 1)
            out_proj(T_O2, 6)
            act.dma_start(dp[:, :, :], p_in[1]).then_inc(S("p_in"), 16)
            ple(T_P2, T_E2, 16, 32, 32, TD_P2, True)

            act.wait_ge(S("hss"), 32 + KT)
            act.activation(dRS, psA[:, 0:T], ACT.Sqrt, bias=eps_c, scale=1.0 / D_MODEL).then_inc(S("n_root"), 1)
            for kt in range(0, KT, 4):
                act.wait_ge(S("fin"), kt + 4)
                act.dma_start(y_out[:, kt:kt + 4, :], h[:, kt:kt + 4, :]).then_inc(S("y_done"), 16)
            act.wait_ge(S("y_done"), 16 * (KT // 4))

        @block.vector
        def _(dve):
            do = Order(dve, dve_order)
            dve.memset(small[:, 0:1], EPS).then_inc(S("konst"), 1)

            def lower_x(src, n, x0):
                for kt in range(n):
                    dve.wait_ge(xh_ready, x0 + kt + 1)
                    dve.tensor_tensor(xl[:, kt, :], src(kt), xh[:, kt, :].bitcast(F32), ALU.subtract) \
                        .then_inc(xl_ready, 1)

            def norm_x(n, wcol, x0):
                dve.wait_ge(S("n_root"), n)
                do.link(dve.reciprocal(dRS, dRS))
                for kt in range(KT):
                    if kt >= 2:
                        dve.wait_ge(xl_ready, x0 + kt - 1)
                    dve.scalar_tensor_tensor(dTM[:, kt % 2, :], h[:, kt, :], prm[:, wcol + kt:wcol + kt + 1],
                                             dRS, ALU.mult, ALU.mult).then_inc(S("xn"), 1)
                    if kt >= 1:
                        k = kt - 1
                        dve.wait_ge(S("xn"), (n - 1) * KT + kt)
                        dve.wait_ge(xh_ready, x0 + k + 1)
                        dve.tensor_tensor(xl[:, k, :], dTM[:, k % 2, :], xh[:, k, :].bitcast(F32), ALU.subtract) \
                            .then_inc(xl_ready, 1)
                k = KT - 1
                dve.wait_ge(S("xn"), n * KT)
                dve.wait_ge(xh_ready, x0 + k + 1)
                dve.tensor_tensor(xl[:, k, :], dTM[:, k % 2, :], xh[:, k, :].bitcast(F32), ALU.subtract) \
                    .then_inc(xl_ready, 1)

            def gate_rows(n, pre):
                H = HRG[0:n]
                dve.wait_ge(S(pre + "exp"), 1)
                do.link(dve.tensor_scalar(H[:, 2, :], H[:, 1, :], 1.0, None, ALU.add))
                dve.tensor_scalar(H[:, 4, :], H[:, 2, :], -1.0, None, ALU.add).then_inc(S(pre + "w1"), 1)
                dve.wait_ge(S(pre + "w1"), 1)
                do.link(dve.tensor_scalar(H[:, 5, :], H[:, 4, :], 0.0, None, ALU.is_equal))
                do.link(dve.tensor_tensor(H[:, 4, :], H[:, 4, :], H[:, 5, :], ALU.add))
                do.link(dve.reciprocal(H[:, 4, :], H[:, 4, :]))
                dve.wait_ge(S(pre + "ln"), 1)
                do.link(dve.tensor_tensor(H[:, 3, :], H[:, 3, :], H[:, 5, :], ALU.add))
                do.link(dve.tensor_tensor(H[:, 3, :], H[:, 3, :], H[:, 1, :], ALU.mult))
                do.link(dve.tensor_tensor(H[:, 3, :], H[:, 3, :], H[:, 4, :], ALU.mult))
                do.link(dve.scalar_tensor_tensor(H[:, 4, :], H[:, 0, :], 0.0, H[:, 3, :], ALU.max, ALU.add))
                do.link(dve.tensor_scalar(H[:, 2, :], H[:, 4, :], small[0:n, 2:3], -1.0, ALU.mult, ALU.mult))
                for c in range(NC):
                    a = slice(c * CH, (c + 1) * CH)
                    dve.tensor_tensor_scan(H[:, 6, a], ones[0:n, :], H[:, 2, a], 0.0, ALU.mult, ALU.add)
                do.link(dve.tensor_copy(H[:, 6, SEQ:SEQ + 8], H[:, 2, SEQ:SEQ + 8]))
                for t in range(1, DEC_T):
                    a = SEQ + 8 * t
                    do.link(dve.tensor_tensor(H[:, 6, a:a + 8], H[:, 6, a - 8:a], H[:, 2, a:a + 8], ALU.add))
                for c in range(NC):
                    a = slice(c * CH, (c + 1) * CH)
                    dve.tensor_scalar(H[:, 1, a], H[:, 6, a], H[:, 6, (c + 1) * CH - 1:(c + 1) * CH], -1.0,
                                      ALU.subtract, ALU.mult)
                dve.tensor_scalar(H[:, 3, :], H[:, 6, :], -1.0, None, ALU.mult).then_inc(S(pre + "cum"), 1)

            for n in range(4):
                dve.wait_ge(S(f"x_in{n}"), 16)
            dve.wait_ge(S("prm_in"), 16)
            dve.wait_ge(c_in, 16)
            norm_x(1, C_NORM, X0["g"])
            dve.wait_ge(xl_ready, X0["g"] + KT)

            def conv_tap(U, CV, n, tap, cache, co, j):
                if j == 0:
                    do.link(dve.tensor_copy(U[:, :, UC:US], cache))
                    dve.tensor_copy(co[:, :, 0:PRE], U[:, :, UC - PRE:UC])
                    dve.tensor_copy(co[:, :, PRE:CW], U[:, :, UW - PRE * DEC_B:UW])
                for i in range(n):
                    for dst, a, w in (((0, SEQ), j, SEQ), ((SEQ, T), UC + DEC_B * j, NS)):
                        out, src = CV[:, i, dst[0]:dst[1]], U[:, i, a:a + w]
                        if j == 0:
                            ins = dve.tensor_scalar(out, src, tap(i, j), None, ALU.mult)
                        else:
                            ins = dve.scalar_tensor_tensor(out, src, tap(i, j), out, ALU.mult, ALU.add)
                return ins

            def conv(U, CV, n, tap, cache, co, ready):
                for j in range(CONV_W):
                    ins = conv_tap(U, CV, n, tap, cache, co, j)
                    if j < CONV_W - 1:
                        do.link(ins)
                ins.then_inc(ready, 1)

            def gdn_qk_conv(m, took):
                dve.wait_ge(S("g_pq_in"), m * 16 + 16)
                dve.wait_ge(took_act, took)
                conv(gU[:, 0:2, :], gCR[:, 0:2, :], 2, lambda i, j: gpc_tap[0][:, i, j:j + 1], gpc_cache[0],
                     gco[:, 0:2, :], S("g_convq"))

            def gdn_qk_norm(m):
                dve.wait_ge(S("g_rs"), m + 1)
                do.link(dve.reciprocal(gRS[:, 1, :], gRS[:, 1, :]))
                dve.tensor_tensor(gKN[:, 1, :], gCR[:, 1, :], gRS[:, 1, :], ALU.mult)
                do.link(dve.reciprocal(gRS[:, 0, :], gRS[:, 0, :]))
                dve.scalar_tensor_tensor(gKN[:, 0, :], gCR[:, 0, :], float(P) ** -0.5, gRS[:, 0, :],
                                         ALU.mult, ALU.mult).then_inc(S("g_kn"), 1)

            def take_out(t0, k):
                dve.wait_ge(half_done, 2 * (t0 + k) + 2)
                dve.tensor_copy(Y[:, k, :], psj[(t0 + k) % 2][:, 0:T]).then_inc(took_dve, 1)

            def gdn_sample(piece, m):
                v = gCR[:, 2:4, SEQ:T]
                _, B, EG = (gR[:, :, k, SEQ:T] for k in range(3))
                kq = psD[:, 160:288].rearrange("p (b j q t) -> p q j t b", b=DEC_B, j=2, q=2)
                if piece == 0:
                    dve.wait_ge(S("g_smp"), m + 1)
                    dve.tensor_tensor(gCQ[:, :, :], gDEC[:, :, :], bc(psD[:, 0:NPAIR], 1, 2), ALU.mult)
                    do.link(dve.tensor_tensor(gCK[:, :, :], gDEC[:, :, :], bc(psD[:, NPAIR:2 * NPAIR], 1, 2),
                                              ALU.mult))
                    for s in range(3):
                        a = slice(OFF[s], OFF[s] + LEN[s])
                        dve.tensor_tensor(gCK[:, :, a], gCK[:, :, a], B[:, :, 8 * s:NS], ALU.mult)
                    do.link(dve.tensor_tensor(gBE[:, :, :], B, EG, ALU.mult))
                if piece == 1:
                    e4 = lambda ap: ap.rearrange("p j (t b) -> p j t b", b=DEC_B)
                    dve.tensor_tensor(gW[:, :, :], B, v, ALU.mult)
                    do.link(dve.tensor_tensor(e4(gTM[:, :, :]), e4(gBE[:, :, :]), kq[:, 1], ALU.mult))
                    dve.tensor_tensor(gW[:, :, :], gW[:, :, :], gTM[:, :, :], ALU.subtract)
                    do.link(dve.tensor_tensor(e4(gO[:, :, SEQ:T]), e4(EG), kq[:, 0], ALU.mult))
                if piece in (2, 3, 4):
                    s = piece - 2
                    n = DEC_T - 1 - s
                    src = bc(gW[:, :, 8 * s:8 * s + 8], 2, n)
                    out = gTM[:, :, 0:8 * n].rearrange("p j (t b) -> p j t b", b=8)
                    ck = gCK[:, :, OFF[s] + 8:OFF[s] + LEN[s]].rearrange("p j (t b) -> p j t b", b=8)
                    do.link(dve.tensor_tensor(out, ck, src, ALU.mult))
                    do.link(dve.tensor_tensor(gW[:, :, 8 * s + 8:NS], gW[:, :, 8 * s + 8:NS], gTM[:, :, 0:8 * n],
                                              ALU.subtract))
                if piece == 5:
                    for s in range(DEC_T):
                        a = OFF[s] + LEN[s] - 8
                        ins = dve.tensor_tensor(gWD[:, :, 8 * s:8 * s + 8], gW[:, :, 8 * s:8 * s + 8],
                                                gDEC[:, :, a:a + 8], ALU.mult)
                    ins.then_inc(S("g_wd"), 1)
                if piece == 6:
                    for s in range(DEC_T):
                        n = DEC_T - s
                        out = gTM[:, :, 0:8 * n].rearrange("p j (t b) -> p j t b", b=8)
                        cq = gCQ[:, :, OFF[s]:OFF[s] + LEN[s]].rearrange("p j (t b) -> p j t b", b=8)
                        do.link(dve.tensor_tensor(out, cq, bc(gW[:, :, 8 * s:8 * s + 8], 2, n), ALU.mult))
                        o = gO[:, :, SEQ + 8 * s:T]
                        ins = dve.tensor_tensor(o, o, gTM[:, :, 0:8 * n], ALU.add)
                        if s < DEC_T - 1:
                            do.link(ins)
                    ins.then_inc(S("g_os_dve"), 1)

            def u4(ap):
                return ap.rearrange("p (c j) t -> p c j t", c=NC)

            def gdn_body(m, full):
                dve.wait_ge(S("g_r_in"), m * 16 + 16)
                do.link(dve.tensor_copy(
                    gcc.rearrange("p k c j -> p (k c) j"),
                    ccol[:, 0:8 * GV].rearrange("p (k h) -> p k h", h=GV)[:, :, bass.ds(m * 2, 2)]))
                for c in range(NC):
                    for j in range(2):
                        dve.tensor_scalar(gDT[:, 2 * c + j, :], gR[:, j, 0, c * CH:(c + 1) * CH],
                                          gcc[:, 1, c, j:j + 1], 0.0, ALU.add, ALU.min)
                G = gR[:, :, 0, SEQ:T].rearrange("p j (t b) -> p j t b", b=8)
                for s in range(DEC_T):
                    n = DEC_T - s
                    ins = dve.tensor_tensor(gDEC[:, :, OFF[s]:OFF[s] + LEN[s]].rearrange("p j (t b) -> p j t b", b=8),
                                            G[:, :, s:, :], bc(gR[:, :, 0, SEQ + 8 * s:SEQ + 8 * s + 8], 2, n),
                                            ALU.subtract)
                ins.then_inc(S("g_dtx"), 1)
                dve.wait_ge(S("g_kn"), m + 1)
                for s in range(DEC_T):
                    n = DEC_T - s
                    t4 = lambda ap: ap.rearrange("p i (t b) -> p i t b", b=8)
                    k_s = bc(bc(gKN[:, 1, SEQ + 8 * s:SEQ + 8 * s + 8], 1, n), 1, 2)
                    ins = dve.tensor_tensor(t4(gPR[:, :, OFF[s]:OFF[s] + LEN[s]]), t4(gKN[:, 0:2, SEQ + 8 * s:T]),
                                            k_s, ALU.mult)
                ins.then_inc(S("g_pr"), 1)
                dve.wait_ge(S("g_dte"), m + 1)
                do.link(dve.tensor_tensor(gDT[:, :, :], gDT[:, :, :], bc(cst[:, K_INC, :], 1, 4), ALU.mult))
                dve.wait_ge(S("g_tok"), m + 1)
                kk = bc(psC[:, 0:256].rearrange("p (c t) -> p c t", c=NC), 2, 2)
                qk = bc(psC[:, 256:512].rearrange("p (c t) -> p c t", c=NC), 2, 2)
                do.link(dve.tensor_tensor(u4(gAT[:, :, :]), u4(gDT[:, :, :]), kk, ALU.mult))
                beta = gR[:, :, 1, 0:SEQ].rearrange("p j (c t) -> p c j t", c=NC)
                do.link(dve.tensor_tensor(u4(gAT[:, :, :]), u4(gAT[:, :, :]), beta, ALU.mult))
                do.link(dve.tensor_tensor(gP[:, :, :], gAT[:, :, :], bc(cst[:, K_M1, :], 1, 4), ALU.mult))
                dve.tensor_tensor(gDE[:, :, 1, :, :], bc(bc(ident, 1, 2), 1, NC), u4(gP[:, :, :]), ALU.subtract) \
                    .then_inc(S("g_e1"), 1)
                dve.tensor_tensor(u4(gQK[:, :, :]), u4(gDT[:, :, :]), qk, ALU.mult)
                dve.tensor_tensor(gKM, bc(psE[0:NS, 0:P], 1, DEC_B), bc(bmask, 2, P), ALU.mult) \
                    .then_inc(S("g_km"), 1)
                dve.tensor_tensor(gQD[:, :, :], bc(gKN[:, 0, CH:2 * CH], 1, 2), gR[:, :, 2, CH:2 * CH], ALU.mult)

                def v_tap(j):
                    ins = conv_tap(gU[:, 2:4, :], gCR[:, 2:4, :], 2, lambda i, j: gpc_tap[1][:, i, j:j + 1],
                                   gpc_cache[1], gco[:, 2:4, :], j)
                    if j < CONV_W - 1:
                        do.link(ins)
                    else:
                        ins.then_inc(S("g_convv"), 1)

                def mask_p(c, lv):
                    dve.wait_ge(S(f"g_p{c}"), m * 6 + lv + 1)
                    dve.tensor_tensor(half(gP[:, 2 * c:2 * c + 2], lv, 0), packed((psC, psE)[c][:, 0:P], lv),
                                      half(bc(cst[:, K_LEV + lv, :], 1, 2), lv, 0), ALU.mult) \
                        .then_inc(S(f"g_pm{c}"), 1)

                def less_q(c, lv):
                    dve.wait_ge(S(f"g_q{c}"), m * 6 + lv + 1)
                    bank = (psA, psF)[c]
                    if lv < 5:
                        D = half(gDE[:, c, 0], lv, 0)
                        dve.tensor_tensor(D, D, packed(bank[:, 0:P], lv), ALU.subtract)
                    E = half(gDE[:, c, 1], lv, 1)
                    dve.scalar_tensor_tensor(E, packed(bank[:, P:2 * P], lv), cst[:, K_BM, K_ROW + lv:K_ROW + lv + 1],
                                             E, ALU.mult, ALU.add).then_inc(S(f"g_de{c}"), 1)

                dve.wait_ge(S("g_pv_in"), m * 16 + 16)
                dve.wait_ge(S("g_e1"), m + 1)
                for lv in range(6):
                    if lv > 0:
                        less_q(1, lv - 1)
                    mask_p(0, lv)
                    if lv < CONV_W:
                        v_tap(lv)
                    if lv == 4:
                        gdn_sample(0, m)
                        if not full:
                            lower_x(lambda kt: Y[:, kt, :], KT, X0["oa1"])
                    mask_p(1, lv)
                    less_q(0, lv)
                less_q(1, 5)
                dve.wait_ge(S("g_cv"), m + 1)
                for piece in range(1, 6):
                    gdn_sample(piece, m)
                if not full:
                    dve.wait_ge(xl_ready, X0["oa1"] + KT)
                    take_out(T_O1, 0)
                dve.wait_ge(S("g_ks"), m + 1)
                for j in range(2):
                    ins = dve.scalar_tensor_tensor(gVB[:, 2 + j, :], psD[:, j * P:(j + 1) * P], gcc[:, 2, 1, j:j + 1],
                                                   gVB[:, 2 + j, :], ALU.mult, ALU.add)
                ins.then_inc(S("g_rhs"), 1)
                gdn_sample(6, m)
                if full:
                    gdn_qk_conv(m + 1, m * 6 + 8)
                dve.wait_ge(S("g_s"), m * 2 + 2)
                for j in range(2):
                    ins = dve.scalar_tensor_tensor(gS2[:, j, :], gS1[:, j, :], gR[:, j, 2, SEQ - 1:SEQ],
                                                   psE[:, j * P:(j + 1) * P], ALU.mult, ALU.add)
                ins.then_inc(S("g_s2"), 1)
                if not full:
                    take_out(T_O1, 1)
                for i in range(4):
                    dve.wait_ge(S("g_sp"), m * 4 + i + 1)
                    for b in (2 * i, 2 * i + 1):
                        for j in range(2):
                            at = (b % 2) * 256 + j * P
                            ins = dve.scalar_tensor_tensor(gS[:, b, j, :], gS[:, b, j, :],
                                                           gR[:, j, 2, T - DEC_B + b:T - DEC_B + b + 1],
                                                           (psA, psB)[i % 2][:, at:at + P], ALU.mult, ALU.add)
                    ins.then_inc(S("g_su"), 1)
                if not full:
                    take_out(T_O1, 2)
                dve.wait_ge(S("g_rs2"), m + 1)
                do.link(dve.reciprocal(ga["RSO"], ga["RSO"]))
                do.link(dve.scalar_tensor_tensor(ga["O"], ga["O"], prm[:, C_GNORM:C_GNORM + 1], ga["RSO"],
                                                 ALU.mult, ALU.mult))
                dve.tensor_tensor(Y[:, bass.ds(m * 2, 2), :], gO[:, :, :], gZS[:, :, :], ALU.mult) \
                    .then_inc(S("g_y"), 1)
                if full:
                    gdn_qk_norm(m + 1)
                else:
                    take_out(T_O1, 3)

            do.link(dve.memset(gU[:, :, 0:PRE], 0.0))
            gdn_qk_conv(0, 2)
            gate_rows(GV, "g_")
            dve.wait_ge(S("g_eg"), 1)
            dve.wait_ge(took_act, 4)
            dve.scalar_tensor_tensor(HRG[0:GV, 4, :], HRG[0:GV, 7, :], -1.0, HRG[0:GV, 8, :],
                                     ALU.mult, ALU.mult).then_inc(S("g_hrows"), 1)
            dve.memset(small[:, 5:6], 0.0).then_inc(S("g_y"), 1)
            gdn_qk_norm(0)
            dve.wait_ge(S("g_ccolc"), 1)
            dve.wait_ge(took_act, 6)
            with dve.Fori(0, GH - 1) as m:
                do.enter(m, G_DVE)
                gdn_body(m, True)
                dve.wait_ge(took_act, m * 6 + 12)
            do.leave(GH - 1)
            gdn_body(GH - 1, False)

            def out_proj(t0, xb, td, back, first):
                with dve.Fori(first // 2, KT // 2) as i:
                    for k in range(2):
                        dve.wait_ge(half_done, i * 4 + 2 * (t0 + k) + 2)
                        dve.tensor_copy(Y[:, i * 2 + k, :], psj[(t0 + k) % 2][:, 0:T]).then_inc(took_dve, 1)
                lower_x(lambda kt: Y[:, KT + kt, :], KT, xb)
                dve.wait_ge(S("h_back"), back)
                dve.wait_ge(took_dve, td + KT)
                with dve.Fori(0, KT // 2) as i:
                    do.enter(i, 2)
                    for k in range(2):
                        t = t0 + KT + k
                        do.link(dve.tensor_tensor(h[:, i * 2 + k, :], h[:, i * 2 + k, :], Y[:, i * 2 + k, :], ALU.add))
                        dve.wait_ge(half_done, i * 4 + 2 * t + 2)
                        dve.tensor_tensor(h[:, i * 2 + k, :], h[:, i * 2 + k, :], psj[t % 2][:, 0:T], ALU.add) \
                            .then_inc(took_dve, 1)
                do.leave(KT // 2)

            def ple(tp, te, xp, xe, td, layer, hq):
                lower_x(lambda kt: dp[:, kt, :], PLE_K, xp)
                for i in range(KT):
                    if i % 4 == 3:
                        dve.wait_ge(half_done, 2 * tp + i // 4 + 1)
                    else:
                        dve.wait_ge(S("e_done"), layer * 12 + i - i // 4 + 1)
                    dve.tensor_copy(eb[:, i, :], psj[(tp + i) % 2][:, 0:T]).then_inc(took_dve, 1)
                lower_x(lambda kt: h[:, kt, :], KT, xe)
                dve.wait_ge(S("e_root"), layer + 1)
                do.link(dve.reciprocal(dRE, dRE))
                wc = C_PLE + layer * KT
                for i in range(KT):
                    ins = dve.scalar_tensor_tensor(eb[:, i, :], eb[:, i, :], prm[:, wc + i:wc + i + 1], dRE,
                                                   ALU.mult, ALU.mult)
                do.link(ins)
                with dve.Fori(0, KT // 2) as i:
                    do.enter(i, 2)
                    for k in range(2):
                        dve.wait_ge(took_act, i * 2 + ((TA_E1, TA_E2)[layer] + k + 1))
                        do.link(dve.tensor_tensor(dTM[:, k, :], eb[:, i * 2 + k, :], dSG[:, k, :], ALU.mult))
                        dve.tensor_tensor(h[:, i * 2 + k, :], h[:, i * 2 + k, :], dTM[:, k, :], ALU.add) \
                            .then_inc(S("hnew"), 1)
                do.leave(KT // 2)

            out_proj(T_O1, X0["ob1"], TD_O1, 16, 4)
            ple(T_P1, T_E1, X0["p1"], X0["e1"], TD_P1, 0, 16)

            norm_x(2, C_NORM + KT, X0["s"])
            dve.wait_ge(xl_ready, X0["s"] + KT)
            do.link(dve.memset(sU[:, :, 0:PRE], 0.0))
            gate_rows(SH, "s_")
            dve.wait_ge(S("s_eg"), 1)
            dve.memset(small[:, 4:5], 0.0).then_inc(S("s_hrows"), 1)
            dve.memset(small[:, 5:6], 0.0).then_inc(S("s_yd"), 1)

            def ssd_decays(m, c):
                for hh in range(HPG):
                    ins = dve.tensor_scalar(sDT[:, hh, :], sR2[:, hh, c * CH:(c + 1) * CH],
                                            scc[:, 1, c, hh:hh + 1], 0.0, ALU.add, ALU.min)
                ins.then_inc(S("s_dtx"), 1)

            def ssd_body(m, took0, last=False):
                dve.wait_ge(S("s_yd"), m + 1)
                dve.wait_ge(S("s_pc_in"), m * 16 + 16)
                dve.wait_ge(took_act, took0)
                dve.wait_ge(S("s_r_in"), m * 16 + 16)
                dve.wait_ge(S("s_rp_in"), m * 32 + 32)
                dve.tensor_copy(scc.rearrange("p k c j -> p (k c) j"),
                                ccol[:, 0:6 * SH].rearrange("p (k h) -> p k h", h=SH)[:, :, bass.ds(m * HPG, HPG)])
                dve.tensor_copy(sa["ND"], prm[:, C_SND:N_PRM][:, bass.ds(m * 2 * SX, 2 * SX)])
                conv(sU, sCV, 6, lambda i, j: spc[:, i, 24 + j:25 + j], spc[:, :, 0:24], sco, S("s_conv"))
                A = sRP[:, :, 0:NS].rearrange("p i (t b) -> p i t b", b=8)
                for s in range(DEC_T):
                    n = DEC_T - s
                    ins = dve.tensor_tensor(
                        sDEC[:, :, OFF[s]:OFF[s] + LEN[s]].rearrange("p i (t b) -> p i t b", b=8),
                        A[:, :, s:, :], bc(sRP[:, :, 8 * s:8 * s + 8], 2, n), ALU.subtract)
                ins.then_inc(S("s_decx"), 1)
                ssd_decays(m, 0)
                dve.wait_ge(S("s_cv"), m + 1)
                Bt = sCV[:, 0, SEQ:T]
                Ct = sCV[:, 1, SEQ:T].rearrange("p (t b) -> p t b", b=8)
                for s in range(DEC_T):
                    n = DEC_T - s
                    ins = dve.tensor_tensor(sPR[:, OFF[s]:OFF[s] + LEN[s]].rearrange("p (t b) -> p t b", b=8),
                                            Ct[:, s:, :], bc(Bt[:, 8 * s:8 * s + 8], 1, n), ALU.mult)
                ins.then_inc(S("s_pr"), 1)
                dve.wait_ge(S("s_tok"), m + 1)

                def decayed(c):
                    dve.tensor_tensor(sXD, sX[:, c], bc(scc[:, 2, c, :], 2, HD), ALU.mult).then_inc(S("s_xd"), 1)

                for c in range(NC):
                    ins = dve.tensor_tensor(sX[:, c], (psB, psC)[c][:, :].rearrange("p (h d) -> p h d", h=HPG),
                                            bc(scc[:, 0, c, :], 2, HD), ALU.mult)
                do.link(ins)
                decayed(0)
                dve.tensor_tensor(sCB[:, :, :], psD[:, 0:2 * P].rearrange("p (c t) -> p c t", c=NC),
                                  bc(cst[:, K_INC, :], 1, NC), ALU.mult)
                dve.tensor_tensor(sBMv, bc(psE[0:NS, 0:P], 1, DEC_B), bc(bmask, 2, P), ALU.mult) \
                    .then_inc(S("s_bm"), 1)
                dve.wait_ge(S("s_bm"), m + 1)
                dve.wait_ge(S("s_dt"), m * 2 + 1)
                dve.tensor_tensor(sDT[:, :, :], sDT[:, :, :], bc(sCB[:, 0, :], 1, HPG), ALU.mult).then_inc(S("s_w"), 1)
                dve.wait_ge(S("s_s"), m * 2 + 1)
                decayed(1)
                dve.tensor_tensor(sXS[:, :, :], sCV[:, 2:6, SEQ:T], sRP[:, :, 192:224], ALU.mult)
                dve.wait_ge(S("s_dec"), m + 1)
                dve.wait_ge(S("s_smp"), m + 1)
                ys = sYT[:, :, SEQ:T]
                y4 = lambda ap: ap.rearrange("p i (t b) -> p i t b", b=8)
                do.link(dve.tensor_tensor(y4(ys), y4(sRP[:, :, 160:192]),
                                          psF[:, P:2 * P].rearrange("p (i b t) -> p i t b", i=SX, b=8), ALU.mult))
                for s in range(DEC_T):
                    a = OFF[s] + LEN[s] - 8
                    ins = dve.tensor_tensor(sXE[:, :, 8 * s:8 * s + 8], sXS[:, :, 8 * s:8 * s + 8],
                                            sDEC[:, :, a:a + 8], ALU.mult)
                ins.then_inc(S("s_xe"), 1)
                dve.wait_ge(S("s_xe"), m + 1)
                do.link(dve.tensor_tensor(sDEC[:, :, :], sDEC[:, :, :], bc(psF[:, 0:NPAIR], 1, SX), ALU.mult))
                for s in range(DEC_T):
                    n = DEC_T - s
                    do.link(dve.tensor_tensor(y4(sTM[:, :, 0:8 * n]), y4(sDEC[:, :, OFF[s]:OFF[s] + LEN[s]]),
                                              bc(sXS[:, :, 8 * s:8 * s + 8], 2, n), ALU.mult))
                    do.link(dve.tensor_tensor(ys[:, :, 8 * s:NS], ys[:, :, 8 * s:NS], sTM[:, :, 0:8 * n], ALU.add))
                if last:
                    lower_x(lambda kt: Y[:, kt, :], KT, X0["oa2"])
                dve.wait_ge(S("s_y"), m * 2 + 1)
                ssd_decays(m, 1)
                dve.wait_ge(S("s_off"), m + 1)
                y1 = sYT[:, :, CH:SEQ]
                do.link(dve.tensor_tensor(y1, psD[:, :].rearrange("p (i t) -> p i t", i=SX), sRP[:, :, 32:160],
                                          ALU.mult))
                dve.wait_ge(S("s_dt"), m * 2 + 2)
                dve.tensor_tensor(sDT[:, :, :], sDT[:, :, :], bc(sCB[:, 1, :], 1, HPG), ALU.mult).then_inc(S("s_w"), 1)
                dve.wait_ge(S("s_s"), m * 2 + 2)
                s1 = sS1.rearrange("p (h d) -> p h d", h=HPG)
                do.link(dve.tensor_tensor(s1, s1, bc(sEGc, 2, HD), ALU.mult))
                dve.tensor_tensor(sS1, sS1, psA[:, :], ALU.add).then_inc(S("s_s2"), 1)
                dve.wait_ge(S("s_y"), m * 2 + 2)
                dve.wait_ge(S("s_y0"), m + 1)
                do.link(dve.tensor_tensor(y1, y1, psC[:, :].rearrange("p (i t) -> p i t", i=SX), ALU.add))
                for i in range(SX):
                    ins = dve.scalar_tensor_tensor(sYT[:, i, :], sCV[:, 2 + i, :], spc_D[:, i:i + 1], sYT[:, i, :],
                                                   ALU.mult, ALU.add)
                ins.then_inc(S("s_yt"), 1)
                dve.wait_ge(S("s_yt"), m + 1)
                if last:
                    dve.wait_ge(xl_ready, X0["oa2"] + KT)
                    take_out(T_O2, 0)
                for b in range(DEC_B):
                    do.link(dve.tensor_tensor(sS[:, b], sS[:, b], bc(sEGb[:, :, b], 2, HD), ALU.mult))
                    dve.wait_ge(S("s_sp"), m * 8 + b + 1)
                    dve.tensor_tensor(sS[:, b], sS[:, b],
                                      (psA, psF)[b % 2][:, :].rearrange("p (h d) -> p h d", h=HPG), ALU.add) \
                        .then_inc(S("s_su"), 1)
                    if last and b in (3, 7):
                        take_out(T_O2, b // 4 + 1)
                gate_y(m)
                if last:
                    take_out(T_O2, 3)
                dve.wait_ge(S("s_root"), m + 1)
                do.link(dve.reciprocal(sTMr, sTMr))
                for i in range(SX):
                    ins = dve.scalar_tensor_tensor(Y[:, m * SX + i, :], sYT[:, i, :], spc_norm[:, i:i + 1], sTMr,
                                                   ALU.mult, ALU.mult)
                ins.then_inc(S("s_yd"), 1)
                if last:
                    take_out(T_O2, 4)
                    take_out(T_O2, 5)

            def gate_y(m):
                dve.wait_ge(took_act, took_z[0])
                dve.tensor_tensor(sa["YT"], sa["YT"], sa["ZS"], ALU.mult).then_inc(S("s_g"), 1)

            took_z = [0]
            dve.wait_ge(S("s_ccolc"), 1)
            with dve.Fori(0, SG - 1) as m:
                do.enter(m, S_DVE)
                took_z[0] = m * 10 + (TA_S + 7 + 8)
                ssd_body(m, m * 10 + (TA_S + 7))
            do.leave(SG - 1)
            took_z[0] = TA_S + 7 + 10 * (SG - 1) + 4
            ssd_body(SG - 1, (SG - 1) * 10 + TA_S + 7, last=True)

            out_proj(T_O2, X0["ob2"], TD_O2, 32, 6)
            ple(T_P2, T_E2, X0["p2"], X0["e2"], TD_P2, 1, 32)

            dve.wait_ge(S("n_root"), 3)
            do.link(dve.reciprocal(dRS, dRS))
            for kt in range(KT):
                dve.scalar_tensor_tensor(h[:, kt, :], h[:, kt, :], prm[:, C_FINAL + kt:C_FINAL + kt + 1], dRS,
                                         ALU.mult, ALU.mult).then_inc(S("fin"), 1)


def _tiles(w, cols):
    k = w.shape[0] // D_MODEL
    out = []
    for part in range(k):
        blk = w[part * D_MODEL:(part + 1) * D_MODEL]
        for c in cols:
            out.append(blk[:, c:c + P].reshape(2, 8, P, P).transpose(0, 2, 1, 3))
    return out


def _narrow(w, c, n):
    import numpy as np
    a = np.concatenate([w[:, c:c + n], np.zeros((w.shape[0], P - n), w.dtype)], axis=1)
    return a.reshape(2, 8, P, P).transpose(0, 2, 1, 3)


def _tokens(prompt, sample):
    import numpy as np
    return np.concatenate([prompt, sample.transpose(1, 0, 2).reshape(NS, -1)], axis=0).T


def kernel(**inputs):
    import numpy as np
    import concourse.bacc as bacc
    from concourse.bass_utils import run_bass_kernel_spmd

    a = {k: np.asarray(v) for k, v in inputs.items()}
    gw, sw = a["gdn_w_in"][0], a["ssd_w_in"][0]
    QK, VW = GH * P, GV * P
    ZG, AG = 2 * QK + VW, 2 * QK + 2 * VW
    q = [P * n for n in range(GH)]
    k = [QK + P * n for n in range(GH)]
    v = [2 * QK + P * n for n in range(GV)]
    z = [ZG + P * n for n in range(GV)]
    DI = SH * HD
    zs = [P * n for n in range(SX * SG)]
    xs = [DI + P * n for n in range(SX * SG)]
    bs = [2 * DI + P * n for n in range(SG)]
    cs = [2 * DI + SG * P + P * n for n in range(SG)]
    stream = _tiles(gw, [q[0], k[0]]) + [_narrow(gw, AG, GV), _narrow(gw, AG + GV, GV)]
    stream += _tiles(gw, [v[0], v[1]])
    for m in range(GH - 1):
        stream += _tiles(gw, [q[m + 1], k[m + 1], z[2 * m], z[2 * m + 1], v[2 * m + 2], v[2 * m + 3]])
    stream += _tiles(gw, z[-2:])

    def dense(n, w_out):
        out = _tiles(w_out, range(0, D_MODEL, P))
        wp = a["ple_w_proj"][n].reshape(PLE_K, P, 2, 2, 4, P)
        out += list(wp.transpose(2, 3, 1, 4, 0, 5).reshape(2, 2, P, 8, P))
        return out + _tiles(a["ple_w_gate"][n], range(0, D_MODEL, P))

    stream += dense(0, a["gdn_w_out"][0])
    stream += [_narrow(sw, 2 * DI + 2 * SG * P, SH)]

    def bcx(g):
        return [bs[g], cs[g]] + xs[SX * g:SX * g + SX]

    stream += _tiles(sw, bcx(0))
    for m in range(SG - 1):
        n = bcx(m + 1)
        z = zs[SX * m:SX * m + SX]
        stream += _tiles(sw, z[:2] + n[:4] + z[2:] + n[4:])
    stream += _tiles(sw, zs[-SX:])
    stream += dense(1, a["ssd_w_out"][0])
    weights = np.stack(stream).reshape(N_HALF, P, 8, P)

    def kt_cols(w):
        return w.reshape(-1, P).T

    def act_layout(x):
        return x.reshape(-1, P, T).transpose(1, 0, 2)

    x_in = act_layout(_tokens(a["x_prompt"][0], a["x_sample"]))
    p_in = np.stack([act_layout(_tokens(a["p_prompt"][n, 0], a["p_sample"][n])) for n in range(DEPTH)])
    prm = np.zeros((P, N_PRM), np.float32)
    prm[:, C_NORM:C_NORM + 32] = kt_cols(a["norm_w"])
    prm[:, C_PLE:C_PLE + 32] = kt_cols(a["ple_norm_w"])
    prm[:, C_FINAL:C_FINAL + 16] = kt_cols(a["final_norm_w"])
    prm[:, C_GNORM] = a["gdn_norm_w"][0]
    prm[:GV, C_GDT], prm[:GV, C_GA] = a["gdn_dt_bias"][0], a["gdn_A_log"][0]
    prm[:SH, C_SDT], prm[:SH, C_SA] = a["ssd_dt_bias"][0], a["ssd_A_log"][0]

    i, j = np.arange(P)[:, None], np.arange(P)[None, :]
    cst = np.zeros((P, N_CST, P), np.float32)
    cst[:, K_ID], cst[:, K_ONE], cst[:, K_INC] = i == j, 1.0, j >= i
    cst[:, K_M1] = (i % 2 == 0) & (j == i + 1)
    for lv in range(6):
        s = 2 << lv
        cst[:, K_LEV + lv] = (i // (2 * s) == j // (2 * s)) & (i // s % 2 == 1) & (j // s % 2 == 0)
        cst[:, K_BM, K_ROW + lv] = -(i[:, 0] // s % 2 == 0).astype(np.float32)
    cst[:NS, K_BM, :DEC_B] = i[:NS] % DEC_B == j[:, :DEC_B]

    def chan(w, cols):
        return np.stack([w[:, c:c + P].T for c in cols], axis=1)

    gcache = a["cache_gdn_conv"][0].transpose(1, 0, 2).reshape(PRE * DEC_B, -1)
    scache = a["cache_ssd_conv"][0].transpose(1, 0, 2).reshape(PRE * DEC_B, -1)
    gpack, spack = [], []
    for m in range(GH):
        gpack.append(np.stack([np.concatenate([chan(gcache, cols).reshape(P, -1),
                                               chan(a["gdn_conv_w"][0], cols).reshape(P, -1)], axis=1)
                               for cols in ([q[m], k[m]], [v[2 * m], v[2 * m + 1]])]))
    D = np.repeat(a["ssd_D"][0], HD)[None]
    for g in range(SG):
        cols = [c - DI for c in bcx(g)]
        pack = np.concatenate([chan(scache, cols), chan(a["ssd_conv_w"][0], cols),
                               chan(a["ssd_conv_b"], cols)], axis=2).reshape(P, -1)
        spack.append(pack)
        mine = [P * (SX * g + n) for n in range(SX)]
        at = C_SND + 2 * SX * g
        prm[:, at:at + SX], prm[:, at + SX:at + 2 * SX] = chan(a["ssd_norm_w"], mine)[:, :, 0], chan(D, mine)[:, :, 0]
    gpack, spack = np.stack(gpack), np.stack(spack)
    gstate = a["state_gdn"][0].reshape(DEC_B, GH, 2, P, P).transpose(1, 3, 0, 2, 4).reshape(GH, P, -1)
    sstate = a["state_ssd"][0].reshape(DEC_B, SG, HPG, HD, P).transpose(1, 4, 0, 2, 3).reshape(SG, P, -1)

    nc = bacc.Bacc("TRN2", target_bir_lowering=False, num_devices=1)
    arrays, args = {}, {}
    for name, arr in (("weights", weights), ("x_in", x_in), ("p_in", p_in), ("prm_in", prm), ("cst_in", cst),
                      ("gpack", gpack), ("spack", spack), ("gstate", gstate), ("sstate", sstate)):
        arrays[name + "_d"] = np.ascontiguousarray(arr)
        args[name] = nc.dram_tensor(name + "_d", arr.shape, F32, kind="ExternalInput").ap()
    for name, shape in (("y_out", (P, KT, T)), ("gconv_out", (GH, 2, P, 2 * CW)), ("sconv_out", (SG, P, 6 * CW)),
                        ("gst_p", (GH, P, 2 * P)), ("gst_s", (GH, P, DEC_B * 2 * P)),
                        ("sst_p", (SG, P, HPG * HD)), ("sst_s", (SG, P, DEC_B * HPG * HD))):
        args[name] = nc.dram_tensor(name + "_d", shape, F32, kind="ExternalOutput").ap()
    for name, shape in (("g_rows", (GH, 2 * 3 * T)), ("s_rows", (SG, HPG, 480)), ("h_spill", (P, KT, T))):
        args[name] = nc.dram_tensor(name + "_d", shape, F32, kind="Internal").ap()
    build(nc, **args, G_DVE=G_DVE_LINKS, G_ACT=1, S_DVE=S_DVE_LINKS, S_ACT=0)
    r = run_bass_kernel_spmd(nc, [arrays], core_ids=[0]).results[0]

    y = r["y_out_d"].transpose(1, 0, 2).reshape(D_MODEL, T).T
    gconv = r["gconv_out_d"].reshape(GH, 2, P, 2, CW).transpose(0, 2, 1, 3, 4).reshape(GH, P, 4, CW)
    gch = np.concatenate([gconv[:, :, 0].transpose(2, 0, 1).reshape(CW, -1),
                          gconv[:, :, 1].transpose(2, 0, 1).reshape(CW, -1),
                          gconv[:, :, 2:4].transpose(3, 0, 2, 1).reshape(CW, -1)], axis=1)
    sconv = r["sconv_out_d"].reshape(SG, P, 6, CW)
    sch = np.concatenate([sconv[:, :, 2:6].transpose(3, 0, 2, 1).reshape(CW, -1),
                          sconv[:, :, 0].transpose(2, 0, 1).reshape(CW, -1),
                          sconv[:, :, 1].transpose(2, 0, 1).reshape(CW, -1)], axis=1)

    def caches(c):
        return c[None, None, :PRE], c[PRE:].reshape(PRE, DEC_B, -1).transpose(1, 0, 2)[None]

    cg_p, cg_s = caches(gch)
    cs_p, cs_s = caches(sch)
    sg_p = r["gst_p_d"].reshape(GH, P, 2, P).transpose(0, 2, 1, 3).reshape(1, 1, GV, P, P)
    sg_s = r["gst_s_d"].reshape(GH, P, DEC_B, 2, P).transpose(2, 0, 3, 1, 4).reshape(1, DEC_B, GV, P, P)
    ss_p = r["sst_p_d"].reshape(SG, P, HPG, HD).transpose(0, 2, 3, 1).reshape(1, 1, SH, HD, P)
    ss_s = r["sst_s_d"].reshape(SG, P, DEC_B, HPG, HD).transpose(2, 0, 3, 4, 1).reshape(1, DEC_B, SH, HD, P)
    y_s = y[SEQ:].reshape(DEC_T, DEC_B, D_MODEL).transpose(1, 0, 2)
    return tuple(np.ascontiguousarray(o) for o in
                 (y[:SEQ][None], y_s, sg_p, cg_p, ss_p, cs_p, sg_s, cg_s, ss_s, cs_s))
```
